# Optimizing a Trainium2 kernel written in Bass

```python
import math
import jax
import jax.numpy as jnp
from jax import lax
import numpy as np
import jax, jax.numpy as jnp

D_MODEL = 1024
BATCH = 1
SEQ = 1024
DEPTH = 1

CHUNK = 64
N_META = 16
N_PAD = CHUNK - N_META
CONV_K = 4
NORM_EPS = 1e-6

H_A = 6
DH_A = 128
D_A = H_A * DH_A
H_B = 8
DH_B = 64
D_B = H_B * DH_B
R_W = 64
R_A = 64
GN_EPS_B = 64e-5
H_C = 12
DH_C = 64
D_C = H_C * DH_C
G_C = 4
N_C = 128

D_MIX = D_A + D_B + D_C
P_A = 4 * D_A + 2 * H_A
P_B = 4 * D_B + R_W + R_A
P_C = 2 * D_C + 2 * G_C * N_C + H_C
D_PROJ = P_A + P_B + P_C


def _splits(sizes):
    return [int(s) for s in np.cumsum(sizes)[:-1]]

def rms_norm(x, w, eps=NORM_EPS):
    xf = x.astype(jnp.float32)
    y = xf * lax.rsqrt(jnp.mean(xf * xf, axis=-1, keepdims=True) + eps)
    return (y * w.astype(jnp.float32)).astype(x.dtype)

def l2_normalize(x, eps=1e-6):
    xf = x.astype(jnp.float32)
    return xf * lax.rsqrt(jnp.sum(xf * xf, axis=-1, keepdims=True) + eps)

def causal_dwconv(u, w):
    c = u.shape[-1]
    return lax.conv_general_dilated(
        u, w[:, None, :].astype(u.dtype), window_strides=(1,), padding=[(CONV_K - 1, 0)],
        dimension_numbers=("NWC", "WIO", "NWC"), feature_group_count=c)

def pad_front(u, n):
    return jnp.pad(u, [(0, 0), (n, 0)] + [(0, 0)] * (u.ndim - 2))

def token_shift(u):
    return jnp.pad(u, ((0, 0), (1, 0), (0, 0)))[:, :-1]

def gated_delta_rule(q, k, v, g, beta):
    bsz, t_len, n_h, dk = q.shape
    dv = v.shape[-1]
    n_c = t_len // CHUNK

    def to_chunks(u):
        u = u.astype(jnp.float32).reshape((bsz, n_c, CHUNK) + u.shape[2:])
        return jnp.moveaxis(u, 3, 1)

    q, k, v, g, beta = map(to_chunks, (q, k, v, g, beta))
    q = q * (dk ** -0.5)
    gc = jnp.cumsum(g, axis=-1)
    incl = jnp.tril(jnp.ones((CHUNK, CHUNK), dtype=bool))
    strict = jnp.tril(jnp.ones((CHUNK, CHUNK), dtype=bool), -1)
    seg = gc[..., :, None] - gc[..., None, :]
    dmask = jnp.where(incl, jnp.exp(jnp.where(incl, seg, 0.0)), 0.0)
    kb = k * beta[..., None]
    a_mat = jnp.where(strict, jnp.einsum("bhnid,bhnjd->bhnij", kb, k) * dmask, 0.0)
    rhs = jnp.concatenate([v * beta[..., None], kb * jnp.exp(gc)[..., None]], axis=-1)
    sol = lax.linalg.triangular_solve(a_mat + jnp.eye(CHUNK, dtype=jnp.float32), rhs,
                                      left_side=True, lower=True, unit_diagonal=True)
    u_c, w_c = sol[..., :dv], sol[..., dv:]
    attn = jnp.einsum("bhnid,bhnjd->bhnij", q, k) * dmask
    q_dec = q * jnp.exp(gc)[..., None]
    k_dec = k * jnp.exp(gc[..., -1:] - gc)[..., None]
    g_tot = jnp.exp(gc[..., -1])

    def step(state, inp):
        u_i, w_i, q_i, k_i, a_i, g_i = inp
        v_new = u_i - jnp.einsum("bhck,bhkv->bhcv", w_i, state)
        o_i = jnp.einsum("bhck,bhkv->bhcv", q_i, state) + jnp.einsum("bhij,bhjv->bhiv", a_i, v_new)
        state = state * g_i[..., None, None] + jnp.einsum("bhck,bhcv->bhkv", k_i, v_new)
        return state, o_i

    xs = tuple(jnp.moveaxis(u, 2, 0) for u in (u_c, w_c, q_dec, k_dec, attn, g_tot))
    s0 = jnp.zeros((bsz, n_h, dk, dv), jnp.float32)
    _, o = lax.scan(step, s0, xs)
    return jnp.transpose(o, (1, 0, 3, 2, 4)).reshape(bsz, t_len, n_h, dv)

def rwkv7_recurrence(r, w, k, v, a, b):
    bsz, _, n_h, dh = r.shape

    def step(state, inp):
        r_t, w_t, k_t, v_t, a_t, b_t = inp
        sa = jnp.einsum("bhvk,bhk->bhv", state, a_t)
        state = (state * w_t[:, :, None, :] + sa[..., None] * b_t[:, :, None, :]
                 + v_t[..., None] * k_t[:, :, None, :])
        return state, jnp.einsum("bhvk,bhk->bhv", state, r_t)

    xs = tuple(jnp.moveaxis(u.astype(jnp.float32), 1, 0) for u in (r, w, k, v, a, b))
    s0 = jnp.zeros((bsz, n_h, dh, dh), jnp.float32)
    _, y = lax.scan(step, s0, xs)
    return jnp.moveaxis(y, 0, 1)

def _segsum(a):
    t = a.shape[-1]
    cs = jnp.cumsum(a, axis=-1)
    mask = jnp.tril(jnp.ones((t, t), dtype=bool))
    return jnp.where(mask, cs[..., :, None] - cs[..., None, :], -jnp.inf)

def ssd_chunked(x, a, b_mat, c_mat):
    bsz, t_len, n_h, hp = x.shape
    n_c = t_len // CHUNK
    x, b_mat, c_mat = [u.reshape((bsz, n_c, CHUNK) + u.shape[2:]) for u in (x, b_mat, c_mat)]
    a = jnp.moveaxis(a.reshape(bsz, n_c, CHUNK, n_h), 3, 1)
    a_cs = jnp.cumsum(a, axis=-1)
    l_mat = jnp.exp(_segsum(a))
    y_diag = jnp.einsum("bclhn,bcshn,bhcls,bcshp->bclhp", c_mat, b_mat, l_mat, x)
    decay_states = jnp.exp(a_cs[..., -1:] - a_cs)
    states = jnp.einsum("bclhn,bhcl,bclhp->bchpn", b_mat, decay_states, x)
    states = jnp.concatenate([jnp.zeros_like(states[:, :1]), states], axis=1)
    decay_chunk = jnp.exp(_segsum(jnp.pad(a_cs[..., -1], ((0, 0), (0, 0), (1, 0)))))
    states = jnp.einsum("bhzc,bchpn->bzhpn", decay_chunk, states)[:, :-1]
    y_off = jnp.einsum("bclhn,bchpn,bhcl->bclhp", c_mat, states, jnp.exp(a_cs))
    return (y_diag + y_off).reshape(bsz, t_len, n_h, hp)

def gated_deltanet_group(p, conv_w, a_log, dt_bias, norm_w):
    out_dtype = p.dtype
    p = p.astype(jnp.float32)
    bsz, seq_len, _ = p.shape
    qkv, z, a_dt, b_raw = jnp.split(p, _splits([3 * D_A, D_A, H_A, H_A]), axis=-1)
    qkv = jax.nn.silu(causal_dwconv(qkv, conv_w.astype(jnp.float32)))
    q, k, v = [u.reshape(bsz, seq_len, H_A, DH_A) for u in jnp.split(qkv, 3, axis=-1)]
    g = -jnp.exp(a_log.astype(jnp.float32)) * jax.nn.softplus(a_dt + dt_bias.astype(jnp.float32))
    beta = jax.nn.sigmoid(b_raw)
    o = gated_delta_rule(*(pad_front(u, N_PAD) for u in (l2_normalize(q), l2_normalize(k), v, g, beta)))
    o = o[:, N_PAD:]
    o = rms_norm(o, norm_w) * jax.nn.silu(z.reshape(bsz, seq_len, H_A, DH_A))
    return o.reshape(bsz, seq_len, D_A).astype(out_dtype)

def rwkv7_group(p, mu, w0, w2, a0, a2, k_k, k_a, r_k, ln_w, ln_b):
    out_dtype = p.dtype
    p = p.astype(jnp.float32)
    bsz, seq_len, _ = p.shape
    p = p + (token_shift(p) - p) * mu.astype(jnp.float32)
    r, k, v, gate, w_lo, a_lo = jnp.split(p, _splits([D_B] * 4 + [R_W, R_A]), axis=-1)
    log_w = -jnp.exp(-jax.nn.softplus(-(w0 + jnp.tanh(w_lo) @ w2.astype(jnp.float32))) - 0.5)
    a = jax.nn.sigmoid(a0 + a_lo @ a2.astype(jnp.float32))
    heads = lambda u: u.reshape(bsz, seq_len, H_B, DH_B)
    kk = l2_normalize(heads(k * k_k))
    k = k * (1.0 + (a - 1.0) * k_a)
    r, k, v, a, log_w = map(heads, (r, k, v, a, log_w))
    y = rwkv7_recurrence(r, jnp.exp(log_w), k, v, -kk, kk * a)
    mean = jnp.mean(y, axis=-1, keepdims=True)
    var = jnp.mean(jnp.square(y - mean), axis=-1, keepdims=True)
    y = ((y - mean) * lax.rsqrt(var + GN_EPS_B)).reshape(bsz, seq_len, D_B) * ln_w + ln_b
    y = y + (jnp.sum(r * k * r_k, axis=-1, keepdims=True) * v).reshape(bsz, seq_len, D_B)
    return (y * jax.nn.silu(gate)).astype(out_dtype)

def mamba2_group(p, conv_w, conv_b, dt_bias, a_log, d_skip, norm_w):
    out_dtype = p.dtype
    p = p.astype(jnp.float32)
    bsz, seq_len, _ = p.shape
    z, xbc, dt = jnp.split(p, _splits([D_C, D_C + 2 * G_C * N_C, H_C]), axis=-1)
    xbc = jax.nn.silu(causal_dwconv(xbc, conv_w.astype(jnp.float32)) + conv_b)
    xs, b_mat, c_mat = jnp.split(xbc, _splits([D_C, G_C * N_C, G_C * N_C]), axis=-1)
    xs = xs.reshape(bsz, seq_len, H_C, DH_C)
    to_heads = lambda u: jnp.repeat(u.reshape(bsz, seq_len, G_C, N_C), H_C // G_C, axis=2)
    dt = jax.nn.softplus(dt + dt_bias.astype(jnp.float32))
    a = -jnp.exp(a_log.astype(jnp.float32))
    y = ssd_chunked(*(pad_front(u, N_PAD) for u in (xs * dt[..., None], a * dt, to_heads(b_mat), to_heads(c_mat))))
    y = (y[:, N_PAD:] + d_skip[:, None] * xs).reshape(bsz, seq_len, D_C)
    y = y * jax.nn.silu(z)
    yg = y.reshape(bsz, seq_len, G_C, D_C // G_C)
    yg = yg * lax.rsqrt(jnp.mean(yg * yg, axis=-1, keepdims=True) + NORM_EPS)
    return (yg.reshape(bsz, seq_len, D_C) * norm_w).astype(out_dtype)

def first_inputs(seed: int = 0) -> dict:
    key = jax.random.key(seed)
    ks = jax.random.split(key, 26)
    f32 = jnp.float32

    def nrm(k, shape, scale):
        return scale * jax.random.normal(k, shape, f32)

    def gain(k, shape):
        return 1.0 + 0.05 * jax.random.normal(k, shape, f32)

    def a_log_init(k, shape):
        return jnp.log(jax.random.uniform(k, shape, f32, minval=1.0, maxval=16.0))

    def dt_bias_init(k, shape):
        dt = jnp.exp(jax.random.uniform(k, shape, f32, minval=math.log(1e-3), maxval=math.log(1e-1)))
        return dt + jnp.log(-jnp.expm1(-dt))

    conv_c = D_C + 2 * G_C * N_C
    return {
        "x": nrm(ks[0], (BATCH, SEQ, D_MODEL), 1.0),
        "meta_tokens": nrm(ks[1], (N_META, D_MODEL), 1.0),
        "norm_pre": gain(ks[2], (DEPTH, D_MODEL)),
        "norm_post": gain(ks[3], (DEPTH, D_MODEL)),
        "w_in": nrm(ks[4], (DEPTH, D_MODEL, D_PROJ), D_MODEL ** -0.5),
        "w_out": nrm(ks[5], (DEPTH, D_MIX, D_MODEL), D_MIX ** -0.5),
        "dn_conv": nrm(ks[6], (DEPTH, CONV_K, 3 * D_A), CONV_K ** -0.5),
        "dn_A_log": a_log_init(ks[7], (DEPTH, H_A)),
        "dn_dt_bias": dt_bias_init(ks[8], (DEPTH, H_A)),
        "dn_norm": gain(ks[9], (DEPTH, DH_A)),
        "rw_mu": jax.random.uniform(ks[10], (DEPTH, P_B), f32),
        "rw_w0": jax.random.uniform(ks[11], (DEPTH, D_B), f32, minval=-2.0, maxval=2.0),
        "rw_w2": nrm(ks[12], (DEPTH, R_W, D_B), 0.5 * R_W ** -0.5),
        "rw_a0": nrm(ks[13], (DEPTH, D_B), 0.1),
        "rw_a2": nrm(ks[14], (DEPTH, R_A, D_B), 0.5 * R_A ** -0.5),
        "rw_k_k": 0.85 + 0.05 * jax.random.normal(ks[15], (DEPTH, D_B), f32),
        "rw_k_a": gain(ks[16], (DEPTH, D_B)),
        "rw_r_k": nrm(ks[17], (DEPTH, H_B, DH_B), 0.1),
        "rw_ln_w": gain(ks[18], (DEPTH, D_B)),
        "rw_ln_b": nrm(ks[19], (DEPTH, D_B), 0.01),
        "mb_conv": nrm(ks[20], (DEPTH, CONV_K, conv_c), CONV_K ** -0.5),
        "mb_conv_b": nrm(ks[21], (DEPTH, conv_c), 0.01),
        "mb_dt_bias": dt_bias_init(ks[22], (DEPTH, H_C)),
        "mb_A_log": a_log_init(ks[23], (DEPTH, H_C)),
        "mb_D": gain(ks[24], (DEPTH, H_C)),
        "mb_norm": gain(ks[25], (DEPTH, D_C)),
    }

def first_block(x, meta_tokens, norm_pre, norm_post, w_in, w_out,
              dn_conv, dn_A_log, dn_dt_bias, dn_norm,
              rw_mu, rw_w0, rw_w2, rw_a0, rw_a2, rw_k_k, rw_k_a, rw_r_k, rw_ln_w, rw_ln_b,
              mb_conv, mb_conv_b, mb_dt_bias, mb_A_log, mb_D, mb_norm):
    bsz = x.shape[0]
    meta = jnp.broadcast_to(meta_tokens.astype(x.dtype)[None], (bsz, N_META, D_MODEL))
    h = jnp.concatenate([meta, x], axis=1)
    for l in range(DEPTH):
        hn = rms_norm(h, norm_pre[l])
        proj = jnp.einsum("bld,dp->blp", hn, w_in[l])
        p_a, p_b, p_c = jnp.split(proj, _splits([P_A, P_B, P_C]), axis=-1)
        mixed = jnp.concatenate([
            gated_deltanet_group(p_a, dn_conv[l], dn_A_log[l], dn_dt_bias[l], dn_norm[l]),
            rwkv7_group(p_b, rw_mu[l], rw_w0[l], rw_w2[l], rw_a0[l], rw_a2[l],
                        rw_k_k[l], rw_k_a[l], rw_r_k[l], rw_ln_w[l], rw_ln_b[l]),
            mamba2_group(p_c, mb_conv[l], mb_conv_b[l], mb_dt_bias[l], mb_A_log[l], mb_D[l], mb_norm[l]),
        ], axis=-1)
        out = jnp.einsum("blm,md->bld", mixed, w_out[l])
        h = h + rms_norm(out, norm_post[l])
    return h[:, N_META:]


_first_inputs = first_inputs


def first_inputs(seed=0):
    import zlib

    import numpy as np

    out = dict(_first_inputs(seed))
    spreads = {}
    factors = {'dn_norm': 13.126,
     'rw_w2': 4.348,
     'rw_a0': 5.138,
     'rw_k_k': 200.0,
     'rw_k_a': 4.301,
     'rw_ln_w': 24.163,
     'rw_ln_b': 64.0,
     'mb_conv_b': 19.556,
     'mb_D': 155.015,
     'mb_dt_bias': 22.312,
     'mb_A_log': 30.952,
     'mb_norm': 4.669}
    for name, (base, spread) in spreads.items():
        noise = np.random.default_rng([zlib.crc32(name.encode()), seed]).standard_normal(out[name].shape)
        drawn = base * np.exp(spread * noise) if base else spread * noise
        out[name] = jnp.asarray(drawn.astype(out[name].dtype))
    for name, factor in factors.items():
        out[name] = (out[name] * factor).astype(out[name].dtype)
    return out


_narrow_inputs = first_inputs


def first_inputs(seed=0):

    out = dict(_narrow_inputs(seed))
    wider = {'rw_k_k': 10.06, 'rw_r_k': 5.32, 'rw_ln_b': 5.05, 'mb_D': 11.62, 'mb_norm': 5.01}
    for name, times in wider.items():
        mean = out[name].mean()
        out[name] = (mean + times * (out[name] - mean)).astype(out[name].dtype)
    return out


HEAD_DIM = 64
W_CONV = D_MODEL // 2
W_ATTN = D_MODEL - W_CONV
N_CONV_GROUPS = W_CONV // HEAD_DIM
N_ATTN_HEADS = W_ATTN // HEAD_DIM
CONV_K_2 = 3
D_FF = 4 * D_MODEL
PLE_DIM = 256
Q_BLOCK = 128
EPS = 1e-6
IN_COLS = 3 * W_CONV + 3 * W_ATTN


def rmsnorm(x, g):
    xf = x.astype(jnp.float32)
    y = xf * lax.rsqrt(jnp.mean(xf * xf, axis=-1, keepdims=True) + EPS)
    return (y * g.astype(jnp.float32)).astype(x.dtype)

def head_rmsnorm(y, g):
    b, s, w = y.shape
    yf = y.astype(jnp.float32).reshape(b, s, w // HEAD_DIM, HEAD_DIM)
    yf = yf * lax.rsqrt(jnp.mean(yf * yf, axis=-1, keepdims=True) + EPS)
    return (yf.reshape(b, s, w) * g.astype(jnp.float32)).astype(y.dtype)

def short_gated_conv(b_gate, c_gate, u, w_conv):
    v = c_gate * u
    y = lax.conv_general_dilated(
        v, w_conv[:, None, :].astype(v.dtype),
        window_strides=(1,), padding=[(CONV_K_2 - 1, 0)],
        dimension_numbers=('NWC', 'WIO', 'NWC'),
        feature_group_count=v.shape[-1])
    return b_gate * y

def stick_breaking_attention(q, k, v):
    b, h, s, dh = q.shape
    n_blk = s // Q_BLOCK
    scale = dh ** -0.5
    qb = q.reshape(b, h, n_blk, Q_BLOCK, dh).transpose(2, 0, 1, 3, 4)
    kf = k.astype(jnp.float32)
    vf = v.astype(jnp.float32)
    key_pos = jnp.arange(s)

    def one_block(args):
        qi, blk = args
        z = jnp.einsum('bhqd,bhkd->bhqk', qi.astype(jnp.float32), kf) * scale
        q_pos = blk * Q_BLOCK + jnp.arange(Q_BLOCK)
        mask = key_pos[None, :] < q_pos[:, None]
        log_keep = jnp.where(mask, jax.nn.log_sigmoid(-z), 0.0)
        suffix = lax.cumsum(log_keep, axis=3, reverse=True) - log_keep
        a = jnp.where(mask, jnp.exp(jax.nn.log_sigmoid(z) + suffix), 0.0)
        return jnp.einsum('bhqk,bhkd->bhqd', a, vf)

    out = lax.map(one_block, (qb, jnp.arange(n_blk)))
    return out.transpose(1, 2, 0, 3, 4).reshape(b, h, s, dh).astype(q.dtype)

def second_inputs(seed: int = 0) -> dict:
    key = jax.random.key(seed)
    ks = jax.random.split(key, 20)
    f32 = jnp.float32

    def nrm(k, shape, fan_in):
        return jax.random.normal(k, shape, f32) * (fan_in ** -0.5)

    def gain(k, shape):
        return 1.0 + 0.02 * jax.random.normal(k, shape, f32)

    return {
        "x": jax.random.normal(ks[0], (BATCH, SEQ, D_MODEL), f32),
        "p": jax.random.normal(ks[1], (DEPTH, BATCH, SEQ, PLE_DIM), f32),
        "g_mix": gain(ks[2], (DEPTH, D_MODEL)),
        "w_in": nrm(ks[3], (DEPTH, D_MODEL, IN_COLS), D_MODEL),
        "conv_w": nrm(ks[4], (DEPTH, CONV_K_2, W_CONV), CONV_K_2),
        "g_conv_out": gain(ks[5], (DEPTH, W_CONV)),
        "g_attn_out": gain(ks[6], (DEPTH, W_ATTN)),
        "w_out": nrm(ks[7], (DEPTH, W_CONV + W_ATTN, D_MODEL), W_CONV + W_ATTN),
        "g_mlp": gain(ks[8], (DEPTH, D_MODEL)),
        "w_up": nrm(ks[9], (DEPTH, D_MODEL, D_FF), D_MODEL),
        "w_down": nrm(ks[10], (DEPTH, D_FF, D_MODEL), D_FF),
        "g_ple": gain(ks[11], (DEPTH, D_MODEL)),
        "w_ple_gate": nrm(ks[12], (DEPTH, D_MODEL, D_MODEL), D_MODEL),
        "w_ple_proj": nrm(ks[13], (DEPTH, PLE_DIM, D_MODEL), PLE_DIM),
        "g_final": gain(ks[14], (D_MODEL,)),
    }

def second_block(x, p, g_mix, w_in, conv_w, g_conv_out, g_attn_out, w_out, g_mlp, w_up, w_down,
              g_ple, w_ple_gate, w_ple_proj, g_final):
    b, s, _ = x.shape
    splits = [W_CONV, 2 * W_CONV, 3 * W_CONV, 3 * W_CONV + W_ATTN, 3 * W_CONV + 2 * W_ATTN]
    h = x
    for i in range(DEPTH):
        a = rmsnorm(h, g_mix[i])
        proj = a @ w_in[i]
        cb, cc, cu, q, k, v = jnp.split(proj, splits, axis=-1)
        conv_out = head_rmsnorm(short_gated_conv(cb, cc, cu, conv_w[i]), g_conv_out[i])
        to_heads = lambda t: t.reshape(b, s, N_ATTN_HEADS, HEAD_DIM).transpose(0, 2, 1, 3)
        attn = stick_breaking_attention(to_heads(q), to_heads(k), to_heads(v))
        attn = head_rmsnorm(attn.transpose(0, 2, 1, 3).reshape(b, s, W_ATTN), g_attn_out[i])
        h = h + jnp.concatenate([conv_out, attn], axis=-1) @ w_out[i]
        m = rmsnorm(h, g_mlp[i])
        h = h + jnp.square(jax.nn.relu(m @ w_up[i])) @ w_down[i]
        gate = jax.nn.sigmoid(rmsnorm(h, g_ple[i]) @ w_ple_gate[i])
        h = h + gate * (p[i] @ w_ple_proj[i])
    return rmsnorm(h, g_final)


_first_inputs_2 = second_inputs


def second_inputs(seed=0):
    import zlib

    import numpy as np

    out = dict(_first_inputs_2(seed))
    spreads = {}
    factors = {'g_conv_out': 5.269, 'g_attn_out': 5.317, 'g_mlp': 4.081, 'g_ple': 8.0, 'g_final': 2.88}
    for name, (base, spread) in spreads.items():
        noise = np.random.default_rng([zlib.crc32(name.encode()), seed]).standard_normal(out[name].shape)
        drawn = base * np.exp(spread * noise) if base else spread * noise
        out[name] = __import__('jax').numpy.asarray(drawn.astype(out[name].dtype))
    for name, factor in factors.items():
        out[name] = (out[name] * factor).astype(out[name].dtype)
    return out


_narrow_inputs_2 = second_inputs


def second_inputs(seed=0):

    out = dict(_narrow_inputs_2(seed))
    wider = {'g_conv_out': 3.87, 'g_attn_out': 3.86, 'g_ple': 12.0, 'g_final': 3.25}
    for name, times in wider.items():
        mean = out[name].mean()
        out[name] = (mean + times * (out[name] - mean)).astype(out[name].dtype)
    return out


GLA_HEADS = 4
GLA_DK = 64
GLA_DV = 128
GLA_RANK = 16
GLA_TAU = 16.0
GLA_CHUNK = 64
SGU_GROUPS = 4
SGU_DC = 128
SGU_CHUNK = 128
D_FF_3 = 4 * D_MODEL

GLA_QK = GLA_HEADS * GLA_DK
GLA_V = GLA_HEADS * GLA_DV
SGU_W = SGU_GROUPS * SGU_DC
D_MIX_3 = GLA_V + SGU_W
IN_SIZES = (GLA_QK, GLA_QK, GLA_V, GLA_V, GLA_RANK, GLA_RANK, SGU_W, SGU_W)
D_IN = GLA_QK * 2 + GLA_V * 2 + GLA_RANK * 2 + SGU_W * 2
SPLIT_POINTS = (GLA_QK, 2 * GLA_QK, 2 * GLA_QK + GLA_V, 2 * GLA_QK + 2 * GLA_V,
                2 * GLA_QK + 2 * GLA_V + GLA_RANK, 2 * GLA_QK + 2 * GLA_V + 2 * GLA_RANK,
                2 * GLA_QK + 2 * GLA_V + 2 * GLA_RANK + SGU_W)


def rmsnorm_3(x, g):
    xf = x.astype(jnp.float32)
    y = xf * lax.rsqrt(jnp.mean(xf * xf, axis=-1, keepdims=True) + EPS)
    return (y * g.astype(jnp.float32)).astype(x.dtype)

def gla_one_direction(q, k, v, log_a, strict):
    B, S, H, K = q.shape
    V = v.shape[-1]
    C = GLA_CHUNK
    N = S // C
    q = q.reshape(B, N, C, H, K)
    k = k.reshape(B, N, C, H, K)
    v = v.reshape(B, N, C, H, V)
    b = jnp.cumsum(log_a.reshape(B, N, C, H, K), axis=2)
    b_mid = b[:, :, C // 2:C // 2 + 1]
    q_in = q * jnp.exp(b - b_mid)
    k_in = k * jnp.exp(b_mid - b)
    scores = jnp.einsum('bnchk,bnjhk->bnhcj', q_in, k_in)
    idx = jnp.arange(C)
    mask = (idx[:, None] > idx[None, :]) if strict else (idx[:, None] >= idx[None, :])
    scores = jnp.where(mask, scores, 0.0)
    o_intra = jnp.einsum('bnhcj,bnjhv->bnchv', scores, v)
    b_last = b[:, :, -1]
    kv = jnp.einsum('bnchk,bnchv->bnhkv', k * jnp.exp(b_last[:, :, None] - b), v)

    def step(state, inp):
        dec, kv_n = inp
        return dec[..., None] * state + kv_n, state

    init = jnp.zeros((B, H, K, V), q.dtype)
    _, s_in = lax.scan(step, init, (jnp.moveaxis(jnp.exp(b_last), 1, 0), jnp.moveaxis(kv, 1, 0)))
    s_in = jnp.moveaxis(s_in, 0, 1)
    o_inter = jnp.einsum('bnchk,bnhkv->bnchv', q * jnp.exp(b), s_in)
    return (o_intra + o_inter).reshape(B, S, H, V)

def gla_mixer(q, k, v, g, a_f, a_b, w_a2_f, b_a_f, w_a2_b, b_a_b, norm_g):
    B, S, _ = q.shape
    f32 = jnp.float32
    q = q.astype(f32).reshape(B, S, GLA_HEADS, GLA_DK) * (GLA_DK ** -0.5)
    k = k.astype(f32).reshape(B, S, GLA_HEADS, GLA_DK)
    v = v.astype(f32).reshape(B, S, GLA_HEADS, GLA_DV)
    log_a_f = (jax.nn.log_sigmoid(a_f.astype(f32) @ w_a2_f.astype(f32) + b_a_f.astype(f32)) / GLA_TAU
               ).reshape(B, S, GLA_HEADS, GLA_DK)
    log_a_b = (jax.nn.log_sigmoid(a_b.astype(f32) @ w_a2_b.astype(f32) + b_a_b.astype(f32)) / GLA_TAU
               ).reshape(B, S, GLA_HEADS, GLA_DK)
    o_f = gla_one_direction(q, k, v, log_a_f, False)
    flip = lambda t: jnp.flip(t, axis=1)
    o_b = flip(gla_one_direction(flip(q), flip(k), flip(v), flip(log_a_b), True))
    o = o_f + o_b
    o = o * lax.rsqrt(jnp.mean(o * o, axis=-1, keepdims=True) + EPS) * norm_g.astype(f32)
    return o.reshape(B, S, GLA_V) * jax.nn.silu(g.astype(f32))

def sgu_mixer(u, v, norm_g, w_s, b_s):
    B, S, _ = u.shape
    f32 = jnp.float32
    N = S // SGU_CHUNK
    v = v.astype(f32).reshape(B, N, SGU_CHUNK, SGU_GROUPS, SGU_DC)
    v = v * lax.rsqrt(jnp.mean(v * v, axis=-1, keepdims=True) + EPS) * norm_g.astype(f32)
    mixed = jnp.einsum('gpq,bnqgc->bnpgc', w_s.astype(f32), v) + b_s.astype(f32).T[:, :, None]
    return u.astype(f32) * mixed.reshape(B, S, SGU_W)

def third_inputs(seed: int = 0) -> dict:
    key = jax.random.key(seed)
    ks = jax.random.split(key, 20)
    nrm = lambda k, shape, s: jax.random.normal(k, shape, jnp.float32) * s
    L = DEPTH
    return {
        "x": nrm(ks[0], (BATCH, SEQ, D_MODEL), 1.0),
        "norm_mix_g": 1.0 + nrm(ks[1], (L, D_MODEL), 0.02),
        "w_in": nrm(ks[2], (L, D_MODEL, D_IN), D_MODEL ** -0.5),
        "w_a2_fwd": nrm(ks[3], (L, GLA_RANK, GLA_QK), GLA_RANK ** -0.5),
        "b_a_fwd": 1.5 + nrm(ks[4], (L, GLA_QK), 1.0),
        "w_a2_bwd": nrm(ks[5], (L, GLA_RANK, GLA_QK), GLA_RANK ** -0.5),
        "b_a_bwd": 1.5 + nrm(ks[6], (L, GLA_QK), 1.0),
        "gla_norm_g": 1.0 + nrm(ks[7], (L, GLA_HEADS, GLA_DV), 0.02),
        "sgu_norm_g": 1.0 + nrm(ks[8], (L, SGU_GROUPS, SGU_DC), 0.02),
        "w_s": nrm(ks[9], (L, SGU_GROUPS, SGU_CHUNK, SGU_CHUNK), SGU_CHUNK ** -0.5),
        "b_s": 1.0 + nrm(ks[10], (L, SGU_GROUPS, SGU_CHUNK), 0.1),
        "w_out": nrm(ks[11], (L, D_MIX_3, D_MODEL), D_MIX_3 ** -0.5),
        "norm_mlp_g": 1.0 + nrm(ks[12], (L, D_MODEL), 0.02),
        "w_mlp1": nrm(ks[13], (L, D_MODEL, D_FF_3), D_MODEL ** -0.5),
        "w_mlp2": nrm(ks[14], (L, D_FF_3, D_MODEL), D_FF_3 ** -0.5),
        "final_norm_g": 1.0 + nrm(ks[15], (D_MODEL,), 0.02),
    }

def third_block(x, norm_mix_g, w_in, w_a2_fwd, b_a_fwd, w_a2_bwd, b_a_bwd, gla_norm_g,
              sgu_norm_g, w_s, b_s, w_out, norm_mlp_g, w_mlp1, w_mlp2, final_norm_g):
    for l in range(DEPTH):
        h = rmsnorm_3(x, norm_mix_g[l])
        z = h @ w_in[l]
        q, k, v, g, a_f, a_b, su, sv = jnp.split(z, SPLIT_POINTS, axis=-1)
        o_gla = gla_mixer(q, k, v, g, a_f, a_b, w_a2_fwd[l], b_a_fwd[l],
                          w_a2_bwd[l], b_a_bwd[l], gla_norm_g[l]).astype(x.dtype)
        o_sgu = sgu_mixer(jax.nn.gelu(su, approximate=False), jax.nn.gelu(sv, approximate=False),
                          sgu_norm_g[l], w_s[l], b_s[l]).astype(x.dtype)
        x = x + jnp.concatenate([o_gla, o_sgu], axis=-1) @ w_out[l]
        h = rmsnorm_3(x, norm_mlp_g[l])
        x = x + jnp.square(jax.nn.relu(h @ w_mlp1[l])) @ w_mlp2[l]
    return rmsnorm_3(x, final_norm_g)


_first_inputs_3 = third_inputs


def third_inputs(seed=0):
    import zlib

    import numpy as np

    out = dict(_first_inputs_3(seed))
    spreads = {}
    factors = {}
    for name, (base, spread) in spreads.items():
        noise = np.random.default_rng([zlib.crc32(name.encode()), seed]).standard_normal(out[name].shape)
        drawn = base * np.exp(spread * noise) if base else spread * noise
        out[name] = __import__('jax').numpy.asarray(drawn.astype(out[name].dtype))
    for name, factor in factors.items():
        out[name] = (out[name] * factor).astype(out[name].dtype)
    return out


_narrow_inputs_3 = third_inputs


def third_inputs(seed=0):

    out = dict(_narrow_inputs_3(seed))
    wider = {'gla_norm_g': 8.98, 'sgu_norm_g': 8.66, 'norm_mlp_g': 4.05, 'final_norm_g': 3.2}
    for name, times in wider.items():
        mean = out[name].mean()
        out[name] = (mean + times * (out[name] - mean)).astype(out[name].dtype)
    return out


def setup_inputs(seed=0):
    out = dict(first_inputs(seed))
    for name, value in second_inputs(seed + 1).items():
        if name != "x":
            out[name + "_2"] = value
    for name, value in third_inputs(seed + 2).items():
        if name != "x":
            out[name + "_3"] = value
    return out


def reference(
    x, meta_tokens, norm_pre, norm_post, w_in, w_out, dn_conv, dn_A_log, dn_dt_bias, dn_norm,
    rw_mu, rw_w0, rw_w2, rw_a0, rw_a2, rw_k_k, rw_k_a, rw_r_k, rw_ln_w, rw_ln_b, mb_conv,
    mb_conv_b, mb_dt_bias, mb_A_log, mb_D, mb_norm, p_2, g_mix_2, w_in_2, conv_w_2,
    g_conv_out_2, g_attn_out_2, w_out_2, g_mlp_2, w_up_2, w_down_2, g_ple_2, w_ple_gate_2,
    w_ple_proj_2, g_final_2, norm_mix_g_3, w_in_3, w_a2_fwd_3, b_a_fwd_3, w_a2_bwd_3, b_a_bwd_3,
    gla_norm_g_3, sgu_norm_g_3, w_s_3, b_s_3, w_out_3, norm_mlp_g_3, w_mlp1_3, w_mlp2_3,
    final_norm_g_3,
):
    x = first_block(
        x, meta_tokens, norm_pre, norm_post, w_in, w_out, dn_conv, dn_A_log, dn_dt_bias,
        dn_norm, rw_mu, rw_w0, rw_w2, rw_a0, rw_a2, rw_k_k, rw_k_a, rw_r_k, rw_ln_w, rw_ln_b,
        mb_conv, mb_conv_b, mb_dt_bias, mb_A_log, mb_D, mb_norm,
    )
    x = second_block(
        x, p_2, g_mix_2, w_in_2, conv_w_2, g_conv_out_2, g_attn_out_2, w_out_2, g_mlp_2, w_up_2,
        w_down_2, g_ple_2, w_ple_gate_2, w_ple_proj_2, g_final_2,
    )
    return third_block(
        x, norm_mix_g_3, w_in_3, w_a2_fwd_3, b_a_fwd_3, w_a2_bwd_3, b_a_bwd_3, gla_norm_g_3,
        sgu_norm_g_3, w_s_3, b_s_3, w_out_3, norm_mlp_g_3, w_mlp1_3, w_mlp2_3, final_norm_g_3,
    )


_drawn_inputs = setup_inputs


def setup_inputs(seed=0):
    import zlib

    import numpy as np

    out = dict(_drawn_inputs(seed))
    spreads = {}
    factors = {'g_ple_2': 33.361, 'norm_mix_g_3': 6.49, 'b_s_3': 3.785, 'norm_mlp_g_3': 6.58}
    for name, (base, spread) in spreads.items():
        noise = np.random.default_rng([zlib.crc32(name.encode()), seed]).standard_normal(out[name].shape)
        drawn = base * np.exp(spread * noise) if base else spread * noise
        out[name] = jnp.asarray(drawn.astype(out[name].dtype))
    for name, factor in factors.items():
        out[name] = (out[name] * factor).astype(out[name].dtype)
    return out
```

```python
import math
from contextlib import ExitStack

import numpy as np

import concourse.bass as bass
from concourse import mybir

F32 = mybir.dt.float32
ACT = mybir.ActivationFunctionType
ALU = mybir.AluOpType

P = 128
D = 1024
KD = D // P
SEQ = 1024
META = 16
FRONT = P - META
T1 = FRONT + META + SEQ
NT1 = T1 // P
NT = SEQ // P
W1 = 352
C1 = 3
S1 = T1 - C1 * W1
LIVE = C1 * W1
W2 = 512
C2 = SEQ // W2
NORM_EPS = 1e-6

H_A, DH_A = 6, 128
D_A = H_A * DH_A
H_B, DH_B = 8, 64
D_B = H_B * DH_B
H_C, DH_C, G_C, N_C = 12, 64, 4, 128
D_C = H_C * DH_C
P_A = 4 * D_A + 2 * H_A
P_B = 4 * D_B + 128
P_C = 2 * D_C + 2 * G_C * N_C + H_C
GN_EPS = 64e-5

LEVELS = 7


def constant_matrices():
    r = np.arange(P)[:, None]
    c = np.arange(P)[None, :]
    m = {
        "ident": r == c,
        "ones": np.ones((P, P)),
        "zeros": np.zeros((P, P)),
        "upto": r <= c,
        "before": r < c,
        "after": r > c,
        "from": r >= c,
        "neg_before": -1.0 * (r < c),
        "neg_from": -1.0 * (r >= c),
        "neg_ones": -np.ones((P, P)),
        "upto_mid": 1.0 * (r <= c) - (r <= P // 2 - 1),
        "before_mid": 1.0 * (r < c) - (r <= P // 2 - 1),
        "head_mean": (r // 64 == c // 64) / 64.0,
        "head_ones": r // 64 == c // 64,
        "upto_mid64": 1.0 * (r <= c) - (r <= 32),
        "from_mid64": 1.0 * (r >= c) - (r >= 31),
        "mid64": np.where(c == 0, r <= 32, (c == 1) & (r >= 31)),
        "real": r >= FRONT,
        "mean": np.full((P, P), 1.0 / P),
        "mid": (r <= P // 2 - 1) & (c == 0),
    }
    for l in range(LEVELS):
        b = 2 ** l
        pair = (r // (2 * b) == c // (2 * b)) & (r // b % 2 == 1) & (c // b % 2 == 0)
        m[f"join{l}"] = pair | (r == c)
    m["join0T"] = m["join0"].T
    g = lambda tile, i: (tile * P + i) // 192
    for a in range(3):
        for b in range(3):
            if abs(a - b) < 2:
                m[f"group{a}{b}"] = (g(a, r) == g(b, c)) / 192.0
    return {k: np.broadcast_to(v, (P, P)).astype(np.float32) for k, v in m.items()}


NAMES = list(constant_matrices())


class Part:

    def __init__(self, nc, name, dram):
        self.nc, self.name, self.dram, self.stack = nc, name, dram, ExitStack()
        self.sems = []

    def __enter__(self):
        return self

    def __exit__(self, *a):
        self.stack.close()
        if self.sems:
            self.nc.clear_and_free_semaphores(self.sems)
            self.nc.all_engine_barrier()

    def sb(self, name, shape, dt=F32):
        return self.stack.enter_context(self.nc.sbuf_tensor(f"{self.name}_{name}", list(shape), dt))

    def ps(self, name, shape):
        return self.stack.enter_context(self.nc.psum_tensor(f"{self.name}_{name}", list(shape), F32))

    def sem(self, name):
        s = self.nc.alloc_semaphore(f"{self.name}_{name}")
        self.sems.append(s)
        return s

    def load_matrices(self, eng, where, names, sem):
        for i, n in enumerate(names):
            j = NAMES.index(n)
            eng.dma_start(where[:, i, :], self.dram["matrices"][j * P:(j + 1) * P, :]).then_inc(sem, 16)
        return 16 * len(names)


def spread(ap, n):
    return ap.unsqueeze(2).to_broadcast([ap.shape[0], ap.shape[1], n])


def project(nc, dram, name, src, src0, weights, col0, k_tiles, n_tiles, chunks, width, dst, dst0,
            dst_tile0, mode, extra=None):
    live = chunks * width
    halo = {"conv": 3, "shift": 1}.get(mode, 0)
    with Part(nc, name, dram) as part:
        w = [part.sb(f"w{s}", [P, k_tiles, P]) for s in range(2)]
        acc = [part.ps(f"acc{s}", [P, chunks, 512]) for s in range(2)]
        w_ready = [part.sem(f"w_ready{s}") for s in range(2)]
        params_ready = part.sem("params_ready")
        product_done = part.sem("product_done")
        acc_free = part.sem("acc_free")
        raw_ready = part.sem("raw_ready")
        vector_done = part.sem("vector_done")
        tile_done = part.sem("tile_done")
        step = part.sem("step")
        n_params, params = 0, {}
        if halo:
            raw = [part.sb(f"raw{s}", [P, halo + live]) for s in range(2)]
        if mode in ("conv", "shift"):
            tmp = [part.sb(f"tmp{s}", [P, live]) for s in range(2)]
        if mode in ("silu_gain", "gate_add"):
            tmp = [part.sb(f"tmp{s}", [P, chunks, width]) for s in range(2)]
        if mode == "conv":
            params["taps"] = part.sb("taps", [P, 4, n_tiles])
            if extra.get("bias") is not None:
                params["bias"] = part.sb("bias", [P, n_tiles])
        if mode == "shift":
            params["mu"] = part.sb("mu", [P, n_tiles])
            params["keep"] = part.sb("keep", [P, n_tiles])
        if mode == "silu_gain":
            params["gain"] = part.sb("gain", [P, n_tiles])
        block = part.stack.enter_context(nc.Block())
        w_view = weights.rearrange("(k p) c -> p k c", p=P)

        def each_tile(eng, body):
            if n_tiles >= 2:
                with eng.Fori(0, n_tiles // 2) as i:
                    for s in range(2):
                        body(i * 2 + s, s, i)
            if n_tiles % 2:
                body(n_tiles - 1, 0, n_tiles // 2)

        @block.sync
        def _(sp):
            if mode == "conv":
                for j in range(4):
                    sp.dma_start(params["taps"][:, j, :], extra["taps"][:, j, :]).then_inc(params_ready, 16)
                if "bias" in params:
                    sp.dma_start(params["bias"][:, :], extra["bias"]).then_inc(params_ready, 16)
            if mode == "shift":
                sp.dma_start(params["mu"][:, :], extra["mu"]).then_inc(params_ready, 16)
            if mode == "silu_gain":
                sp.dma_start(params["gain"][:, :], extra["gain"]).then_inc(params_ready, 16)

            def load(f, s, i):
                sp.wait_ge(product_done, f + 1)
                sp.dma_start(w[s][:, :, :], w_view[:, :, bass.ds(f * P + col0, P)]).then_inc(w_ready[s], 16)
            each_tile(sp, load)

        n_params = {"conv": 5 if "bias" in params else 4, "shift": 1, "silu_gain": 1}.get(mode, 0) * 16

        @block.tensor
        def _(pe):
            pe.sem_inc(product_done, 2)

            def multiply(f, s, i):
                pe.wait_ge(w_ready[s], i * 16 + 16)
                pe.wait_ge(acc_free, f + 1)
                for c in range(chunks):
                    for k in range(k_tiles):
                        mm = nc.tensor.matmul(acc[s][:, c, :width], w[s][:, k, :],
                                              src[:, k, src0 + c * width:src0 + (c + 1) * width],
                                              start=(k == 0), stop=(k == k_tiles - 1))
                mm.then_inc(product_done, 1)
            each_tile(pe, multiply)

        def out(f):
            return dst[:, f + dst_tile0, dst0:dst0 + live]

        def out3(f):
            return out(f).rearrange("p (c n) -> p c n", c=chunks)

        def a3(s):
            return acc[s][:, :, :width]

        @block.scalar
        def _(act):
            if mode in ("conv", "shift"):
                act.sem_inc(acc_free, 2)

                def finish(f, s, i):
                    act.wait_ge(product_done, f + 3)
                    act.wait_ge(vector_done, f + 1)
                    nc.scalar.activation(raw[s][:, halo:].rearrange("p (c n) -> p c n", c=chunks), a3(s),
                                         ACT.Copy).then_inc(acc_free, 1)
                    if mode == "conv":
                        act.wait_ge(vector_done, f + 3)
                        bias = params["bias"][:, bass.ds(f, 1)] if "bias" in params else 0.0
                        nc.scalar.activation(out(f), tmp[s][:, :], ACT.Silu, bias=bias).then_inc(tile_done, 1)
                if mode == "conv":
                    act.sem_inc(tile_done, 2)
                    act.wait_ge(params_ready, n_params)
                each_tile(act, finish)
            elif mode in ("silu_gain", "relu2"):
                if mode == "silu_gain":
                    act.sem_inc(acc_free, 2)

                def finish(f, s, i):
                    act.wait_ge(product_done, f + 3)
                    if mode == "silu_gain":
                        act.wait_ge(vector_done, f + 1)
                    a = nc.scalar.activation(tmp[s][:, :, :] if mode == "silu_gain" else out3(f), a3(s),
                                             ACT.Silu if mode == "silu_gain" else ACT.Relu)
                    a.then_inc(acc_free if mode == "silu_gain" else raw_ready, 1)
                each_tile(act, finish)
            elif mode in ("copy", "gelu", "sigmoid", "silu"):
                act.sem_inc(acc_free, 2)
                func = {"copy": ACT.Copy, "gelu": ACT.Gelu, "sigmoid": ACT.Sigmoid, "silu": ACT.Silu}[mode]

                def finish(f, s, i):
                    act.wait_ge(product_done, f + 3)
                    nc.scalar.activation(out3(f), a3(s), func).then_inc(acc_free, 1)
                each_tile(act, finish)

        @block.vector
        def _(dve):
            if n_params:
                dve.wait_ge(params_ready, n_params)
            if mode == "conv":
                for s in range(2):
                    nc.vector.memset(raw[s][:, 0:halo], 0.0)
                dve.sem_inc(vector_done, 2)

                def finish(f, s, i):
                    dve.wait_ge(acc_free, f + 3)
                    dve.wait_ge(tile_done, f + 1)
                    tap = lambda j: params["taps"][:, j, bass.ds(f, 1)]
                    nc.vector.tensor_scalar(tmp[s][:, :], raw[s][:, 3:3 + live], tap(3), None, ALU.mult).then_inc(step, 1)
                    for n, j in enumerate((2, 1, 0)):
                        dve.wait_ge(step, f * 3 + n + 1)
                        nc.vector.scalar_tensor_tensor(tmp[s][:, :], raw[s][:, j:j + live], tap(j), tmp[s][:, :],
                                                       ALU.mult, ALU.add).then_inc(step if j else vector_done, 1)
                each_tile(dve, finish)
            if mode == "shift":
                for s in range(2):
                    nc.vector.memset(raw[s][:, 0:halo], 0.0)
                nc.vector.tensor_scalar(params["keep"][:, :], params["mu"][:, :], -1.0, 1.0, ALU.mult, ALU.add).then_inc(step, 1)
                dve.wait_ge(step, 1)
                dve.sem_inc(vector_done, 2)

                def finish(f, s, i):
                    dve.wait_ge(acc_free, f + 3)
                    nc.vector.tensor_scalar(tmp[s][:, :], raw[s][:, 0:live], params["mu"][:, bass.ds(f, 1)], None,
                                            ALU.mult).then_inc(step, 1)
                    dve.wait_ge(step, f + 2)
                    nc.vector.scalar_tensor_tensor(out(f), raw[s][:, 1:1 + live], params["keep"][:, bass.ds(f, 1)],
                                                   tmp[s][:, :], ALU.mult, ALU.add).then_inc(vector_done, 1)
                each_tile(dve, finish)
            if mode == "silu_gain":
                dve.sem_inc(vector_done, 2)

                def finish(f, s, i):
                    dve.wait_ge(acc_free, f + 3)
                    nc.vector.tensor_scalar(out3(f), tmp[s][:, :, :], params["gain"][:, bass.ds(f, 1)], None,
                                            ALU.mult).then_inc(vector_done, 1)
                each_tile(dve, finish)
            if mode == "relu2":
                dve.sem_inc(vector_done, 2)
                dve.sem_inc(acc_free, 2)

                def finish(f, s, i):
                    dve.wait_ge(raw_ready, f + 1)
                    nc.vector.tensor_tensor(out3(f), out3(f), a3(s), ALU.mult).then_inc(vector_done, 1)
                    dve.wait_ge(vector_done, f + 3)
                    dve.sem_inc(acc_free, 1)
                each_tile(dve, finish)
            if mode == "add":
                dve.sem_inc(acc_free, 2)

                def finish(f, s, i):
                    dve.wait_ge(product_done, f + 3)
                    nc.vector.tensor_tensor(out3(f), out3(f), a3(s), ALU.add).then_inc(acc_free, 1)
                each_tile(dve, finish)
            if mode == "gate_add":
                dve.sem_inc(acc_free, 2)
                gate = extra["gate"]

                def finish(f, s, i):
                    dve.wait_ge(product_done, f + 3)
                    nc.vector.tensor_tensor(tmp[s][:, :, :], gate[:, f, :].rearrange("p (c n) -> p c n", c=chunks),
                                            a3(s), ALU.mult).then_inc(acc_free, 1)
                    dve.wait_ge(acc_free, f + 3)
                    nc.vector.tensor_tensor(out3(f), out3(f), tmp[s][:, :, :], ALU.add).then_inc(step, 1)
                    dve.wait_ge(step, f + 1)
                each_tile(dve, finish)


def normalise(nc, dram, name, src, src0, gain, chunks, width, dst, add=False, scratch=None):
    with Part(nc, name, dram) as part:
        mats = part.sb("mats", [P, 1, P])
        gains = part.sb("gains", [P, KD])
        square = part.sb("square", [P, 2, KD, width]) if scratch is None else scratch
        scale = part.sb("scale", [P, 2, width])
        total = part.ps("total", [P, 2, 512])
        grown = part.sb("grown", [P, KD, width]) if add else None
        loaded, squared, summed, logged, scaled, out_done, step = (part.sem(n) for n in (
            "loaded", "squared", "summed", "logged", "scaled", "out_done", "step"))
        block = part.stack.enter_context(nc.Block())

        @block.sync
        def _(sp):
            part.load_matrices(sp, mats, ["ones"], loaded)
            sp.dma_start(gains[:, :], gain).then_inc(loaded, 16)

        cols = lambda c: slice(src0 + c * width, src0 + (c + 1) * width)

        @block.scalar
        def _(act):
            def square_of(c):
                if c >= 2:
                    act.wait_ge(summed, c - 1)
                nc.scalar.activation(square[:, c % 2], src[:, :, cols(c)], ACT.Square).then_inc(squared, 1)

            square_of(0)
            for c in range(chunks):
                if c + 1 < chunks:
                    square_of(c + 1)
                act.wait_ge(summed, c + 1)
                if c >= 2:
                    act.wait_ge(out_done, KD * (c - 1))
                nc.scalar.activation(scale[:, c % 2], total[:, c % 2, :width], ACT.Ln, scale=1.0 / D, bias=NORM_EPS).then_inc(logged, 1)
                act.wait_ge(logged, c + 1)
                nc.scalar.activation(scale[:, c % 2], scale[:, c % 2], ACT.Exp, scale=-0.5).then_inc(scaled, 1)

        @block.tensor
        def _(pe):
            pe.wait_ge(loaded, 32)
            for c in range(chunks):
                pe.wait_ge(squared, c + 1)
                if c >= 2:
                    pe.wait_ge(logged, c - 1)
                for k in range(KD):
                    mm = nc.tensor.matmul(total[:, c % 2, :width], mats[:, 0, :], square[:, c % 2, k, :],
                                          start=(k == 0), stop=(k == KD - 1))
                mm.then_inc(summed, 1)

        @block.vector
        def _(dve):
            dve.wait_ge(loaded, 32)
            for c in range(chunks):
                dve.wait_ge(scaled, c + 1)
                for k in range(KD):
                    if add:
                        if c >= 1:
                            dve.wait_ge(out_done, KD * (c - 1) + k + 1)
                        nc.vector.scalar_tensor_tensor(grown[:, k, :], src[:, k, cols(c)], gains[:, k:k + 1],
                                                       scale[:, c % 2], ALU.mult, ALU.mult).then_inc(step, 1)
                        dve.wait_ge(step, KD * c + k + 1)
                        nc.vector.tensor_tensor(dst[:, k, cols(c)], dst[:, k, cols(c)], grown[:, k, :], ALU.add).then_inc(out_done, 1)
                        continue
                    nc.vector.scalar_tensor_tensor(dst[:, k, cols(c)], src[:, k, cols(c)], gains[:, k:k + 1],
                                                   scale[:, c % 2], ALU.mult, ALU.mult).then_inc(out_done, 1)


def entry(nc, dram, frame, rows):
    with Part(nc, "entry", dram) as part:
        ident = part.sb("ident", [P, 1, P])
        cross = part.ps("cross", [P, 4, KD, P])
        loaded, cleared, turned, moved = (part.sem(n) for n in ("loaded", "cleared", "turned", "moved"))
        block = part.stack.enter_context(nc.Block())

        @block.sync
        def _(sp):
            part.load_matrices(sp, ident, ["ident"], loaded)
            sp.wait_ge(cleared, 1)
            sp.dma_start(rows[FRONT:P, 0, :], dram["meta_tokens"][:, :]).then_inc(loaded, 16)
            sp.dma_start(rows[:, 1:, :], dram["x"][0].rearrange("(t p) d -> p t d", p=P)).then_inc(loaded, 16)

        @block.gpsimd
        def _(pool):
            nc.gpsimd.memset(rows[:, 0, :], 0.0).then_inc(cleared, 1)

        @block.tensor
        def _(pe):
            pe.wait_ge(loaded, 48)
            for t in range(NT1):
                if t >= 4:
                    pe.wait_ge(moved, t - 3)
                for k in range(KD):
                    mm = nc.tensor.transpose(cross[:, t % 4, k, :], rows[:, t, k * P:(k + 1) * P], ident[:, 0, :])
                mm.then_inc(turned, 1)

        @block.vector
        def _(dve):
            for t in range(NT1):
                dve.wait_ge(turned, t + 1)
                nc.vector.tensor_copy(frame[:, :, t * P:(t + 1) * P], cross[:, t % 4]).then_inc(moved, 1)


def leave(nc, dram, hidden, out):
    with Part(nc, "leave", dram) as part:
        ident = part.sb("ident", [P, 1, P])
        rows = part.sb("rows", [P, 2, D])
        cross = part.ps("cross", [P, 4, KD, P])
        loaded, turned, moved = (part.sem(n) for n in ("loaded", "turned", "moved"))
        stored = [part.sem(f"stored{s}") for s in range(2)]
        block = part.stack.enter_context(nc.Block())

        @block.sync
        def _(sp):
            part.load_matrices(sp, ident, ["ident"], loaded)
            for t in range(NT):
                sp.wait_ge(moved, t + 1)
                sp.dma_start(out[t * P:(t + 1) * P, :], rows[:, t % 2, :]).then_inc(stored[t % 2], 16)
            for s in range(2):
                sp.wait_ge(stored[s], 16 * (NT // 2))

        @block.tensor
        def _(pe):
            pe.wait_ge(loaded, 16)
            for t in range(NT):
                if t >= 4:
                    pe.wait_ge(moved, t - 3)
                for k in range(KD):
                    mm = nc.tensor.transpose(cross[:, t % 4, k, :], hidden[:, k, t * P:(t + 1) * P], ident[:, 0, :])
                mm.then_inc(turned, 1)

        @block.vector
        def _(dve):
            for t in range(NT):
                dve.wait_ge(turned, t + 1)
                if t >= 2:
                    dve.wait_ge(stored[t % 2], 16 * (t // 2))
                nc.vector.tensor_copy(rows[:, t % 2, :], cross[:, t % 4].rearrange("p k n -> p (k n)")).then_inc(moved, 1)


def over_heads(m, n):
    return m.unsqueeze(1).to_broadcast([m.shape[0], n, m.shape[1]])


def gates(nc, dram, hn, decay, beta, dt):
    HS = H_A + H_C
    with Part(nc, "gates", dram) as part:
        w = part.sb("w", [P, KD, 24])
        real = part.sb("real", [P, 1, P])
        rows = part.sb("rows", [P, 2, HS])
        v, u, w1, d1, eq, lg = (part.sb(n, [P, NT1, HS]) for n in ("v", "u", "w1", "d1", "eq", "lg"))
        e = part.sb("e", [P, NT1, H_A])
        ea = part.sb("ea", [P, HS])
        acc = part.ps("acc", [P, 2, 512])
        raw = acc[:, 0, :NT1 * 24].rearrange("p (t c) -> p t c", c=24)
        loaded, product, biased, absolute, small, plus1, logged, grown, betas, step = (part.sem(n) for n in (
            "loaded", "product", "biased", "absolute", "small", "plus1", "logged", "grown", "betas", "step"))
        block = part.stack.enter_context(nc.Block())
        w_in = dram["w_in"].rearrange("(k p) c -> p k c", p=P)

        @block.sync
        def _(sp):
            with nc.allow_non_contiguous_dma(reason="24 columns of gates"):
                sp.dma_start(w[:, :, 0:6], w_in[:, :, 4 * D_A:4 * D_A + 6]).then_inc(loaded, 16)
                sp.dma_start(w[:, :, 6:18], w_in[:, :, P_A + P_B + P_C - H_C:P_A + P_B + P_C]).then_inc(loaded, 16)
                sp.dma_start(w[:, :, 18:24], w_in[:, :, 4 * D_A + 6:4 * D_A + 12]).then_inc(loaded, 16)
            sp.dma_start(rows[:, 0, :], dram["gate_bias"].to_broadcast([P, HS])).then_inc(loaded, 16)
            sp.dma_start(rows[:, 1, :], dram["gate_log"].to_broadcast([P, HS])).then_inc(loaded, 16)
            part.load_matrices(sp, real, ["real"], loaded)

        @block.tensor
        def _(pe):
            pe.wait_ge(loaded, 96)
            for t in range(NT1):
                for k in range(KD):
                    mm = nc.tensor.matmul(raw[:, t, :], hn[:, k, t * P:(t + 1) * P], w[:, k, :],
                                          start=(k == 0), stop=(k == KD - 1))
            mm.then_inc(product, 1)

        @block.scalar
        def _(act):
            act.wait_ge(loaded, 96)
            nc.scalar.activation(ea[:, :], rows[:, 1, :], ACT.Exp).then_inc(grown, 1)
            act.wait_ge(biased, 1)
            nc.scalar.activation(e[:, :, :], raw[:, :, 18:24], ACT.Exp, scale=-1.0).then_inc(betas, 1)
            nc.scalar.activation(u[:, :, :], v[:, :, :], ACT.Abs).then_inc(absolute, 1)
            act.wait_ge(absolute, 1)
            nc.scalar.activation(u[:, :, :], u[:, :, :], ACT.Exp, scale=-1.0).then_inc(small, 1)
            act.wait_ge(plus1, 1)
            nc.scalar.activation(lg[:, :, :], w1[:, :, :], ACT.Ln).then_inc(logged, 1)

        @block.vector
        def _(dve):
            n = [0]

            def then(i):
                n[0] += 1
                i.then_inc(step, 1)
                dve.wait_ge(step, n[0])
            V = nc.vector
            over = lambda r: over_heads(r, NT1)
            dve.wait_ge(product, 1)
            dve.wait_ge(loaded, 96)
            V.tensor_tensor(v[:, :, :], raw[:, :, 0:HS], over(rows[:, 0, :]), ALU.add).then_inc(biased, 1)
            dve.wait_ge(betas, 1)
            then(V.tensor_scalar(e[:, :, :], e[:, :, :], 1.0, None, ALU.add))
            V.reciprocal(beta[:, :, :], e[:, :, :])
            dve.wait_ge(small, 1)
            V.tensor_scalar(w1[:, :, :], u[:, :, :], 1.0, None, ALU.add).then_inc(plus1, 1)
            dve.wait_ge(plus1, 1)
            then(V.tensor_scalar(d1[:, :, :], w1[:, :, :], -1.0, None, ALU.add))
            then(V.tensor_scalar(eq[:, :, :], d1[:, :, :], 0.0, None, ALU.is_equal))
            then(V.tensor_tensor(d1[:, :, :], d1[:, :, :], eq[:, :, :], ALU.add))
            then(V.reciprocal(d1[:, :, :], d1[:, :, :]))
            dve.wait_ge(logged, 1)
            then(V.tensor_tensor(d1[:, :, :], d1[:, :, :], lg[:, :, :], ALU.mult))
            then(V.tensor_tensor(d1[:, :, :], d1[:, :, :], eq[:, :, :], ALU.add))
            then(V.tensor_tensor(u[:, :, :], u[:, :, :], d1[:, :, :], ALU.mult))
            then(V.scalar_tensor_tensor(v[:, :, :], v[:, :, :], 0.0, u[:, :, :], ALU.max, ALU.add))
            dve.wait_ge(grown, 1)
            V.scalar_tensor_tensor(decay[:, :, :], v[:, :, :], -1.0, over(ea[:, :]), ALU.mult, ALU.mult)
            then(V.tensor_copy(dt[:, :, :], v[:, :, H_A:]))
            V.tensor_scalar(dt[:, 0, :], dt[:, 0, :], real[:, 0, 0:1], None, ALU.mult)


def unit(nc, dram, name, buf, first, n_tiles, matrix, scale, eps=1e-6, times=None, src0=S1, chunks=C1, width=W1):
    live = chunks * width
    with Part(nc, name, dram) as part:
        mats = part.sb("mats", [P, 1, P])
        square = part.sb("square", [P, 2, live])
        root = part.sb("root", [P, 2, chunks, width])
        total = part.ps("total", [P, 2, 4, 512])
        gains = None if isinstance(scale, float) else part.sb("gains", [P, n_tiles])
        loaded, squared, summed, logged, scaled, out_done, step = (part.sem(n) for n in (
            "loaded", "squared", "summed", "logged", "scaled", "out_done", "step"))
        block = part.stack.enter_context(nc.Block())
        tile = lambda f: buf[:, f + first, src0:src0 + live]
        sums = lambda s: total[:, s, :chunks, :width]

        @block.sync
        def _(sp):
            part.load_matrices(sp, mats, [matrix], loaded)
            if gains is not None:
                sp.dma_start(gains[:, :], scale).then_inc(loaded, 16)

        @block.scalar
        def _(act):
            with act.Fori(0, n_tiles // 2) as i:
                for s in range(2):
                    nc.scalar.activation(square[:, s], tile(i * 2 + s), ACT.Square).then_inc(squared, 1)
                for s in range(2):
                    act.wait_ge(summed, i * 2 + s + 1)
                    act.wait_ge(out_done, i * 2 + s + 1)
                    nc.scalar.activation(root[:, s], sums(s), ACT.Ln, bias=eps).then_inc(logged, 1)
                    act.wait_ge(logged, i * 2 + s + 1)
                    nc.scalar.activation(root[:, s], root[:, s], ACT.Exp, scale=-0.5).then_inc(scaled, 1)

        @block.tensor
        def _(pe):
            pe.wait_ge(loaded, 16 if gains is None else 32)
            with pe.Fori(0, n_tiles // 2) as i:
                for s in range(2):
                    pe.wait_ge(squared, i * 2 + s + 1)
                    for c in range(chunks):
                        mm = nc.tensor.matmul(total[:, s, c, :width], mats[:, 0, :], square[:, s, c * width:(c + 1) * width],
                                              start=True, stop=True)
                    mm.then_inc(summed, 1)

        @block.vector
        def _(dve):
            dve.wait_ge(loaded, 16 if gains is None else 32)
            dve.sem_inc(out_done, 2)
            with dve.Fori(0, n_tiles // 2) as i:
                for s in range(2):
                    f = i * 2 + s
                    dve.wait_ge(scaled, f + 1)
                    r = root[:, s].rearrange("p c n -> p (c n)")
                    if times is not None:
                        nc.vector.tensor_tensor(r, r, times[:, f, :], ALU.mult).then_inc(step, 1)
                        dve.wait_ge(step, f + 1)
                    nc.vector.scalar_tensor_tensor(tile(f), tile(f), scale if gains is None else gains[:, bass.ds(f, 1)],
                                                   r, ALU.mult, ALU.mult).then_inc(out_done, 1)


class Inverse:

    LAST = LEVELS - 1

    def __init__(self, nc, part, heads, flip, x, x_t, part_x, mats, regions, flip_ready):
        self.nc, self.heads = nc, heads
        self.flip, self.x, self.x_t, self.part_x, self.mats = flip, x, x_t, part_x, mats
        self.r_part, self.r_x, self.r_xt = regions
        self.flip_ready = flip_ready
        self.start_t, self.product, self.masked, self.joined, self.x_ready, self.xt_ready = (
            part.sem("inv_" + n) for n in ("start_t", "product", "masked", "joined", "x_ready", "xt_ready"))

    def tensor(self, pe, t, start_free):
        nc, H, L = self.nc, self.heads, self.LAST
        pe.wait_ge(self.start_t, t + 1)
        for h in range(H):
            mm = nc.tensor.transpose(self.r_x[:, h, :], self.x_t[:, h, :], self.mats("ident"))
        mm.then_inc(self.joined, 1)
        for l in range(1, LEVELS):
            pe.wait_ge(self.x_ready, t * L + l)
            for h in range(H):
                mm = nc.tensor.matmul(self.r_part[:, h, :], self.flip[:, h, :], self.x[:, h, :], start=True, stop=True)
            mm.then_inc(self.product, 1)
            pe.wait_ge(self.masked, t * L + l)
            if l > 1:
                pe.wait_ge(self.xt_ready, t * L + l - 1)
            for h in range(H):
                if l < L:
                    nc.tensor.matmul(self.r_x[:, h, :], self.x_t[:, h, :], self.part_x[:, h, :], start=True, stop=True)
                mm = nc.tensor.matmul(self.r_xt[:, h, :], self.part_x[:, h, :], self.x_t[:, h, :], start=True, stop=True)
            mm.then_inc(self.joined, 1)

    def scalar(self, act, t):
        for l in range(1, LEVELS):
            act.wait_ge(self.joined, t * LEVELS + l)
            self.nc.scalar.activation(self.x[:, :, :], self.r_x[:, :, :], ACT.Copy).then_inc(self.x_ready, 1)

    def vector(self, dve, t):
        V, H, L = self.nc.vector, self.heads, self.LAST
        V.tensor_tensor(self.x_t[:, :, :], self.flip[:, :, :], over_heads(self.mats("join0T"), H), ALU.mult).then_inc(self.start_t, 1)
        for l in range(1, LEVELS):
            dve.wait_ge(self.product, t * L + l)
            V.tensor_tensor(self.part_x[:, :, :], self.r_part[:, :, :], over_heads(self.mats(f"join{l}"), H), ALU.mult).then_inc(self.masked, 1)
            dve.wait_ge(self.joined, t * LEVELS + l + 1)
            V.tensor_copy(self.x_t[:, :, :], self.r_xt[:, :, :]).then_inc(self.xt_ready, 1)


def delta_rule(nc, dram, act_a, decay, beta):
    H = H_A
    with Part(nc, "delta", dram) as part:
        names = ["ident", "ones", "upto", "after", "neg_before", "join0T"] + [f"join{l}" for l in range(1, LEVELS)]
        mt = part.sb("mats", [P, len(names), P])
        mat = lambda n: mt[:, names.index(n), :]
        over = lambda n: over_heads(mat(n), H)
        head = lambda n: part.sb(n, [P, H, P])
        stage = part.sb("stage", [P, 3 * H, P])
        q, k, v = (stage[:, i * H:(i + 1) * H, :] for i in range(3))
        state = head("state")
        gm, dec, eg, pt, dn, flip, x, xt, px, kt, vt = (head(n) for n in (
            "gm", "dec", "eg", "pt", "dn", "flip", "x", "xt", "px", "kt", "vt"))
        gs = part.sb("gs", [P, 3, H])
        vn, qd, o, sq, rs = gm, eg, head("o"), flip, dec
        R = [part.ps(f"r{i}", [P, 8, P]) for i in range(4)]
        r = lambda i: R[i][:, :H, :]
        small = R[0][:, 6, 0:3 * H].rearrange("p (a h) -> p a h", a=3)
        S = {n: part.sem(n) for n in (
            "loaded", "staged", "stage_used", "turn", "decays_spread", "segments", "exps", "keys", "kq_read",
            "flip_ready", "turned", "kt_done", "vt_done", "ks", "rhs", "fresh", "fresh_read", "queries",
            "outputs", "squares", "norms", "logs", "roots", "gated", "stored", "state_done", "d", "grow")}
        inv = Inverse(nc, part, H, flip, x, xt, px, mat, (r(1), r(2), r(3)), S["flip_ready"])
        block = part.stack.enter_context(nc.Block())
        mix = dram["mix"]

        @block.sync
        def _(sp):
            part.load_matrices(sp, mt, names, S["loaded"])
            with sp.Fori(0, NT1) as t:
                sp.wait_ge(S["stage_used"], t + 1)
                sp.dma_start(stage[:, :, :], act_a[:, 0:3 * H, bass.ts(t, P)]).then_inc(S["staged"], 16)
                sp.wait_ge(S["gated"], t + 1)
                sp.dma_start(mix.rearrange("(f p) t -> p f t", p=P)[:, 0:H, bass.ts(t, P)], o[:, :, :]).then_inc(S["stored"], 16)
            sp.wait_ge(S["stored"], 16 * NT1 + 16)

        @block.tensor
        def _(pe):
            M = nc.tensor.matmul
            pe.wait_ge(S["loaded"], 16 * len(names))
            with pe.Fori(0, NT1) as t:
                pe.wait_ge(S["decays_spread"], t + 1)
                for i, m in ((0, "after"), (1, "ones")):
                    M(R[i][:, 0:4, :], mat(m), gm[:, 0:4, :], start=True, stop=True)
                    M(R[i][:, 4:6, :], mat(m), gm[:, 4:6, :], start=True, stop=True)
                for i, m in enumerate(("upto", "ones", "after")):
                    mm = M(small[:, i, :], mat(m), decay[:, bass.ds(t, 1), 0:H].rearrange("p a h -> p (a h)"), start=True, stop=True)
                mm.then_inc(S["segments"], 1)
                pe.wait_ge(S["staged"], t * 16 + 16)
                for h in range(H):
                    M(R[2][:, h, :], k[:, h, :], k[:, h, :], start=True, stop=True)
                    mm = M(R[3][:, h, :], k[:, h, :], q[:, h, :], start=True, stop=True)
                mm.then_inc(S["keys"], 1)
                pe.wait_ge(S["exps"], t * 3 + 3)
                for h in range(H):
                    nc.tensor.transpose(R[0][:, h, :], k[:, h, :], mat("ident"))
                    mm = nc.tensor.transpose(R[1][:, h, :], v[:, h, :], mat("ident"))
                mm.then_inc(S["turned"], 1)
                pe.wait_ge(S["kt_done"], t + 1)
                pe.wait_ge(S["vt_done"], t + 1)
                pe.wait_ge(S["flip_ready"], t + 1)
                inv.tensor(pe, t, None)
                for h in range(H):
                    mm = M(R[0][:, h, :], k[:, h, :], state[:, h, :], start=True, stop=True)
                mm.then_inc(S["ks"], 1)
                pe.wait_ge(S["rhs"], t + 1)
                pe.wait_ge(inv.xt_ready, t * 6 + 6)
                for h in range(H):
                    mm = M(R[1][:, h, :], xt[:, h, :], px[:, h, :], start=True, stop=True)
                mm.then_inc(S["fresh"], 1)
                pe.wait_ge(S["fresh_read"], t + 1)
                for h in range(H):
                    M(R[0][:, h, :], vn[:, h, :], pt[:, h, :], start=True, stop=False)
                    mm = M(R[0][:, h, :], state[:, h, :], qd[:, h, :], start=False, stop=True)
                mm.then_inc(S["outputs"], 1)
                for h in range(H):
                    mm = M(R[2][:, h, :], kt[:, h, :], vn[:, h, :], start=True, stop=True)
                mm.then_inc(S["grow"], 1)
                pe.wait_ge(S["squares"], t + 1)
                M(R[3][:, 0:4, :], mat("ones"), sq[:, 0:4, :], start=True, stop=True)
                M(R[3][:, 4:6, :], mat("ones"), sq[:, 4:6, :], start=True, stop=True).then_inc(S["norms"], 1)

        @block.scalar
        def _(act):
            A = nc.scalar.activation
            with act.Fori(0, NT1) as t:
                act.wait_ge(S["segments"], t + 1)
                A(dec[:, :, :], r(0), ACT.Exp).then_inc(S["exps"], 1)
                A(gs[:, :, :], small, ACT.Exp).then_inc(S["exps"], 1)
                A(eg[:, :, :], r(1), ACT.Exp).then_inc(S["exps"], 1)
                act.wait_ge(S["turned"], t + 1)
                A(vt[:, :, :], r(1), ACT.Copy).then_inc(S["vt_done"], 1)
                inv.scalar(act, t)
                act.wait_ge(S["outputs"], t + 1)
                act.wait_ge(S["stored"], t * 16 + 16)
                A(sq[:, :, :], r(0), ACT.Square).then_inc(S["squares"], 1)
                A(o[:, :, :], r(0), ACT.Copy)
                act.wait_ge(S["norms"], t + 1)
                A(rs[:, :, :], r(3), ACT.Ln, scale=1.0 / DH_A, bias=NORM_EPS).then_inc(S["logs"], 1)
                act.wait_ge(S["logs"], t + 1)
                A(rs[:, :, :], rs[:, :, :], ACT.Exp, scale=-0.5).then_inc(S["roots"], 1)

        @block.vector
        def _(dve):
            V, T = nc.vector, nc.vector.tensor_tensor
            K = 10
            V.memset(state[:, :, :], 0.0).then_inc(S["turn"], 1)
            dve.sem_inc(S["stage_used"], 1)
            dve.sem_inc(S["stored"], 16)
            dve.wait_ge(S["loaded"], 16 * len(names))
            with dve.Fori(0, NT1) as t:
                n = [0]

                def then(i):
                    n[0] += 1
                    i.then_inc(S["d"], 1)
                    dve.wait_ge(S["d"], t * K + n[0])
                per_head = lambda a: spread(a, P)
                beta_h = per_head(beta[:, bass.ds(t, 1), :].rearrange("p a h -> p (a h)"))
                decay_h = per_head(decay[:, bass.ds(t, 1), 0:H].rearrange("p a h -> p (a h)"))
                dve.wait_ge(S["turn"], t + 1)
                T(gm[:, :, :], over("upto"), decay_h, ALU.mult).then_inc(S["decays_spread"], 1)
                dve.wait_ge(S["exps"], t * 3 + 3)
                T(dn[:, :, :], dec[:, :, :], over("neg_before"), ALU.mult)
                then(T(dec[:, :, :], dec[:, :, :], over("upto"), ALU.mult))
                then(T(dn[:, :, :], dn[:, :, :], beta_h, ALU.mult))
                dve.wait_ge(S["keys"], t + 1)
                T(pt[:, :, :], r(3), dec[:, :, :], ALU.mult)
                then(T(flip[:, :, :], r(2), dn[:, :, :], ALU.mult))
                then(T(flip[:, :, :], flip[:, :, :], over("ident"), ALU.add))
                dve.wait_ge(S["turned"], t + 1)
                T(kt[:, :, :], r(0), per_head(gs[:, 2, :]), ALU.mult).then_inc(S["kt_done"], 1)
                then(T(qd[:, :, :], q[:, :, :], eg[:, :, :], ALU.mult))
                dve.sem_inc(S["flip_ready"], 1)
                inv.vector(dve, t)
                dve.wait_ge(S["ks"], t + 1)
                then(T(px[:, :, :], r(0), per_head(gs[:, 0, :]), ALU.mult))
                T(px[:, :, :], vt[:, :, :], px[:, :, :], ALU.subtract).then_inc(S["rhs"], 1)
                dve.wait_ge(S["fresh"], t + 1)
                T(vn[:, :, :], r(1), beta_h, ALU.mult).then_inc(S["fresh_read"], 1)
                dve.wait_ge(S["grow"], t + 1)
                then(T(state[:, :, :], state[:, :, :], per_head(gs[:, 1, :]), ALU.mult))
                then(T(state[:, :, :], state[:, :, :], r(2), ALU.add))
                dve.wait_ge(S["roots"], t + 1)
                then(T(o[:, :, :], o[:, :, :], rs[:, :, :], ALU.mult))
                then(T(o[:, :, :], o[:, :, :], act_a[:, 3 * H:4 * H, bass.ts(t, P)], ALU.mult))
                dve.sem_inc(S["gated"], 1)
                dve.sem_inc(S["stage_used"], 1)
                dve.sem_inc(S["turn"], 1)
                assert n[0] == K


def rwkv_prepare(nc, dram, b, rate, unit_k):
    F = 4
    with Part(nc, "rwprep", dram) as part:
        a2 = part.sb("a2", [P, D_B])
        w2 = part.sb("w2", [64, D_B])
        w0 = part.sb("w0", [1, D_B])
        mt = part.sb("mats", [P, 1, P])
        par = part.sb("par", [P, 4, F])
        mixk = part.sb("mixk", [P, 2, LIVE])
        lw = part.sb("lw", [P, 2, D_B])
        acc = [part.ps(f"acc{s}", [P, C1, 512]) for s in range(2)]
        dec = part.ps("dec", [P, 2, 512])
        loaded, squashed, product, rate_done, dec_done, dec_read, scaled, stored, mixed, used, step = (part.sem(n) for n in (
            "loaded", "squashed", "product", "rate_done", "dec_done", "dec_read", "scaled", "stored", "mixed", "used", "step"))
        stored = [stored, mixed]
        block = part.stack.enter_context(nc.Block())

        @block.sync
        def _(sp):
            sp.dma_start(a2[64:128, :], dram["rw_a2"][:, :]).then_inc(loaded, 16)
            sp.dma_start(w2[:, :], dram["rw_w2"][:, :]).then_inc(loaded, 16)
            sp.dma_start(w0[:, :], dram["rw_w0"][:, :]).then_inc(loaded, 16)
            for i, n in enumerate(("rw_a0", "rw_k_k", "rw_k_a")):
                sp.dma_start(par[:, i, :], dram[n]).then_inc(loaded, 16)
            part.load_matrices(sp, mt, ["ones"], loaded)
            for t in range(NT1):
                sp.wait_ge(scaled, t + 1)
                sp.dma_start(dram["log_w"][t * P:(t + 1) * P, :], lw[:, t % 2, :]).then_inc(stored[t % 2], 16)
            sp.wait_ge(stored[0], 16 * ((NT1 + 1) // 2))
            sp.wait_ge(stored[1], 16 * (NT1 // 2))

        @block.scalar
        def _(act):
            A = nc.scalar.activation
            act.wait_ge(loaded, 112)
            A(b[0:64, 16, :], b[0:64, 16, :], ACT.Tanh).then_inc(squashed, 1)
            for f in range(F):
                act.wait_ge(product, f + 1)
                A(rate[:, f, S1:].rearrange("p (c n) -> p c n", c=C1), acc[f % 2][:, :, :W1], ACT.Sigmoid,
                  bias=par[:, 0, f:f + 1]).then_inc(rate_done, 1)
            for t in range(NT1):
                act.wait_ge(dec_done, t + 1)
                if t >= 2:
                    act.wait_ge(stored[t % 2], 16 * (t // 2))
                A(lw[:, t % 2, :], dec[:, t % 2, :], ACT.Sigmoid).then_inc(dec_read, 1)
                act.wait_ge(dec_read, t + 1)
                A(lw[:, t % 2, :], lw[:, t % 2, :], ACT.Copy, scale=-math.exp(-0.5)).then_inc(scaled, 1)
            A(b[:, 12:16, :], b[:, 12:16, :], ACT.Silu)

        @block.tensor
        def _(pe):
            M = nc.tensor.matmul
            pe.wait_ge(loaded, 112)
            for f in range(F):
                if f >= 2:
                    pe.wait_ge(rate_done, f - 1)
                for c in range(C1):
                    mm = M(acc[f % 2][:, c, :W1], a2[64:128, f * P:(f + 1) * P],
                           b[64:128, 16, S1 + c * W1:S1 + (c + 1) * W1], start=True, stop=True)
                mm.then_inc(product, 1)
            pe.wait_ge(squashed, 1)
            for t in range(NT1):
                if t >= 2:
                    pe.wait_ge(dec_read, t - 1)
                M(dec[:, t % 2, :], b[0:64, 16, t * P:(t + 1) * P], w2[:, :], start=True, stop=False)
                M(dec[:, t % 2, :], mt[0:1, 0, :], w0[:, :], start=False, stop=True).then_inc(dec_done, 1)

        @block.vector
        def _(dve):
            V = nc.vector
            dve.wait_ge(loaded, 112)
            V.tensor_scalar(par[:, 3, :], par[:, 2, :], -1.0, 1.0, ALU.mult, ALU.add).then_inc(step, 1)
            dve.wait_ge(step, 1)
            for f in range(F):
                dve.wait_ge(rate_done, f + 1)
                V.tensor_scalar(unit_k[:, f, S1:], b[:, 4 + f, S1:], par[:, 1, f:f + 1], None, ALU.mult)
                V.tensor_scalar(mixk[:, f % 2, :], rate[:, f, S1:], par[:, 2, f:f + 1], par[:, 3, f:f + 1],
                                ALU.mult, ALU.add).then_inc(step, 1)
                dve.wait_ge(step, 2 * f + 2)
                V.tensor_tensor(b[:, 4 + f, S1:], b[:, 4 + f, S1:], mixk[:, f % 2, :], ALU.mult).then_inc(step, 1)
                dve.wait_ge(step, 2 * f + 3)


def rwkv(nc, dram, b, rate, unit_k):
    H, F = H_B, 4
    BIG = 1e38
    with Part(nc, "rwkv", dram) as part:
        names = ["ident", "upto_mid", "before_mid", "mid", "upto", "before", "head_mean", "head_ones", "join0T"] + \
                [f"join{l}" for l in range(1, LEVELS)]
        mt = part.sb("mats", [P, len(names), P])
        mat = lambda n: mt[:, names.index(n), :]
        over = lambda n: over_heads(mat(n), H)
        par = part.sb("par", [P, 3, F])
        lw, vst, bt, kt, e1, e2, e3, y, sq, rk = (part.sb(n, [P, F, P]) for n in (
            "lw", "vst", "bt", "kt", "e1", "e2", "e3", "y", "sq", "rk"))
        rz, az = (part.sb(n, [P, F, 2, P]) for n in ("rz", "az"))
        flip, x, xt, px, ak, pb, pk = (part.sb(n, [P, H, P]) for n in ("flip", "x", "xt", "px", "ak", "pb", "pk"))
        tok = part.sb("tok", [P, 3, F, P])
        em = part.sb("em", [P, F])
        state, hm = (part.sb(n, [P, F, 64]) for n in ("state", "hm"))
        rhs, u = e2, e3
        heads = lambda a: a.rearrange("p f (e c) -> p (f e) c", e=2)
        R = [part.ps(f"r{i}", [P, 8, P]) for i in range(4)]
        S = {n: part.sem(n) for n in (
            "loaded", "staged", "stage_used", "turn", "decays", "exps", "scaled_in", "scores", "scores_read",
            "turned", "tokens", "flip_ready", "hm_done", "rhs_done", "rhs_read", "u_done", "u_read", "outputs",
            "grown", "y_read", "mean", "centred", "squared", "var", "logs", "roots", "rk_ready", "bonus",
            "gated", "stored", "d")}
        inv = Inverse(nc, part, H, flip, x, xt, px, mat, (R[1], R[2], R[3]), None)
        block = part.stack.enter_context(nc.Block())
        n_loads = 16 * (len(names) + 3)

        @block.sync
        def _(sp):
            part.load_matrices(sp, mt, names, S["loaded"])
            for i, n in enumerate(("rw_r_k", "rw_ln_w", "rw_ln_b")):
                sp.dma_start(par[:, i, :], dram[n]).then_inc(S["loaded"], 16)
            with sp.Fori(0, NT1) as t:
                sp.wait_ge(S["stage_used"], t + 1)
                sp.dma_start(lw[:, :, :].rearrange("p f c -> p (f c)"), dram["log_w"][bass.ts(t, P), :]).then_inc(S["staged"], 16)
                sp.dma_start(vst[:, :, :], b[:, 8:12, bass.ts(t, P)]).then_inc(S["staged"], 16)
                sp.wait_ge(S["gated"], t + 1)
                sp.dma_start(dram["mix"].rearrange("(f p) t -> p f t", p=P)[:, 6:10, bass.ts(t, P)], y[:, :, :]).then_inc(S["stored"], 16)
            sp.wait_ge(S["stored"], 16 * NT1 + 16)

        @block.tensor
        def _(pe):
            M = nc.tensor.matmul
            pe.wait_ge(S["loaded"], n_loads)
            with pe.Fori(0, NT1) as t:
                pe.wait_ge(S["staged"], t * 32 + 32)
                pe.wait_ge(S["turn"], t + 1)
                for f in range(F):
                    M(R[0][:, f, :], lw[:, f, :], mat("upto_mid"), start=True, stop=True)
                    M(R[0][:, 4 + f, :], lw[:, f, :], mat("before_mid"), start=True, stop=True)
                    mm = M(R[1][:, 0, f:f + 1], lw[:, f, :], mat("mid")[:, 0:1], start=True, stop=True)
                mm.then_inc(S["decays"], 1)
                pe.wait_ge(S["scaled_in"], t + 1)
                for f in range(F):
                    for i, (l, r) in enumerate(((bt, az), (kt, az), (bt, rz), (kt, rz))):
                        mm = M(R[i][:, 2 * f:2 * f + 2, :], l[:, f, :], r[:, f, :, :], start=True, stop=True)
                mm.then_inc(S["scores"], 1)
                pe.wait_ge(S["scores_read"], t + 1)
                for f in range(F):
                    nc.tensor.transpose(R[0][:, f, :], vst[:, f, :], mat("ident"))
                    nc.tensor.transpose(R[0][:, 4 + f, :], bt[:, f, :], mat("ident"))
                    mm = nc.tensor.transpose(R[1][:, f, :], kt[:, f, :], mat("ident"))
                mm.then_inc(S["turned"], 1)
                pe.wait_ge(S["tokens"], t * 2 + 2)
                inv.tensor(pe, t, None)
                pe.wait_ge(S["hm_done"], t + 1)
                pe.wait_ge(inv.xt_ready, t * 6 + 6)
                out = heads(R[0][:, 0:4, :])
                for h in range(H):
                    M(out[:, h, :], az[:, h // 2, h % 2, :], hm[:, h // 2, :], start=True, stop=False)
                    mm = M(out[:, h, :], ak[:, h, :], heads(tok[:, 0])[:, h, :], start=False, stop=True)
                mm.then_inc(S["rhs_done"], 1)
                pe.wait_ge(S["rhs_read"], t + 1)
                out = heads(R[1][:, 0:4, :])
                for h in range(H):
                    mm = M(out[:, h, :], xt[:, h, :], heads(rhs[:, :, :])[:, h, :], start=True, stop=True)
                mm.then_inc(S["u_done"], 1)
                pe.wait_ge(S["u_read"], t + 1)
                for h in range(H):
                    o = R[2][(h % 2) * 64:(h % 2) * 64 + 64, h // 2, :]
                    M(o, heads(u[:, :, :])[:, h, :], pb[:, h, :], start=True, stop=False)
                    M(o, heads(tok[:, 0])[:, h, :], pk[:, h, :], start=False, stop=False)
                    mm = M(o, hm[:, h // 2, :], rz[:, h // 2, h % 2, :], start=False, stop=True)
                mm.then_inc(S["outputs"], 1)
                for f in range(F):
                    M(R[3][:, f, :], tok[:, 1, f, :], u[:, f, :], start=True, stop=False)
                    mm = M(R[3][:, f, :], tok[:, 2, f, :], tok[:, 0, f, :], start=False, stop=True)
                mm.then_inc(S["grown"], 1)
                pe.wait_ge(S["y_read"], t + 1)
                M(R[0][:, 0:4, :], mat("head_mean"), y[:, :, :], start=True, stop=True).then_inc(S["mean"], 1)
                pe.wait_ge(S["squared"], t + 1)
                M(R[1][:, 0:4, :], mat("head_mean"), sq[:, :, :], start=True, stop=True).then_inc(S["var"], 1)
                pe.wait_ge(S["rk_ready"], t + 1)
                M(R[0][:, 4:8, :], mat("head_ones"), rk[:, :, :], start=True, stop=True).then_inc(S["bonus"], 1)

        @block.scalar
        def _(act):
            A = nc.scalar.activation
            with act.Fori(0, NT1) as t:
                act.wait_ge(S["decays"], t + 1)
                A(e1[:, :, :], R[0][:, 0:4, :], ACT.Exp).then_inc(S["exps"], 1)
                A(e3[:, :, :], R[0][:, 0:4, :], ACT.Exp, scale=-1.0).then_inc(S["exps"], 1)
                A(e2[:, :, :], R[0][:, 4:8, :], ACT.Exp).then_inc(S["exps"], 1)
                A(em[:, :], R[1][:, 0, 0:4], ACT.Exp).then_inc(S["exps"], 1)
                act.wait_ge(S["turned"], t + 1)
                A(tok[:, 0:2].rearrange("p a f c -> p (a f) c"), R[0][:, :, :], ACT.Copy).then_inc(S["tokens"], 1)
                A(tok[:, 2], R[1][:, 0:4, :], ACT.Copy).then_inc(S["tokens"], 1)
                inv.scalar(act, t)
                act.wait_ge(S["rhs_done"], t + 1)
                A(rhs[:, :, :], R[0][:, 0:4, :], ACT.Copy).then_inc(S["rhs_read"], 1)
                act.wait_ge(S["u_done"], t + 1)
                A(u[:, :, :], R[1][:, 0:4, :], ACT.Copy).then_inc(S["u_read"], 1)
                act.wait_ge(S["outputs"], t + 1)
                act.wait_ge(S["stored"], t * 16 + 16)
                A(y[:, :, :], R[2][:, 0:4, :], ACT.Copy).then_inc(S["y_read"], 1)
                act.wait_ge(S["centred"], t + 1)
                A(sq[:, :, :], y[:, :, :], ACT.Square).then_inc(S["squared"], 1)
                act.wait_ge(S["var"], t + 1)
                A(sq[:, :, :], R[1][:, 0:4, :], ACT.Ln, bias=GN_EPS).then_inc(S["logs"], 1)
                act.wait_ge(S["logs"], t + 1)
                A(sq[:, :, :], sq[:, :, :], ACT.Exp, scale=-0.5).then_inc(S["roots"], 1)

        @block.vector
        def _(dve):
            V, T, STT = nc.vector, nc.vector.tensor_tensor, nc.vector.scalar_tensor_tensor
            K = 13
            V.memset(rz[:, :, :, :], 0.0)
            V.memset(az[:, :, :, :], 0.0)
            V.memset(state[:, :, :], 0.0).then_inc(S["turn"], 1)
            dve.wait_ge(S["turn"], 1)
            dve.sem_inc(S["stage_used"], 1)
            dve.sem_inc(S["stored"], 16)
            dve.wait_ge(S["loaded"], n_loads)
            with dve.Fori(0, NT1) as t:
                n = [0]

                def then(i):
                    n[0] += 1
                    i.then_inc(S["d"], 1)
                    dve.wait_ge(S["d"], t * K + n[0])
                at = bass.ts(t, P)
                r, k2, v, gate = (b[:, 4 * i:4 * i + 4, at] for i in range(4))
                dve.wait_ge(S["exps"], t * 4 + 4)
                T(hm[:, :, :], state[:, :, :], spread(em[:, :], 64), ALU.mult).then_inc(S["hm_done"], 1)
                for e in range(2):
                    half = slice(64 * e, 64 * e + 64)
                    T(rz[half, :, e, :], b[half, 0:4, at], e1[half, :, :], ALU.mult)
                    STT(az[half, :, e, :], unit_k[half, :, at], -1.0, e2[half, :, :], ALU.mult, ALU.mult)
                T(bt[:, :, :], unit_k[:, :, at], e3[:, :, :], ALU.mult).then_inc(S["d"], 1)
                n[0] += 1
                T(kt[:, :, :], k2, e3[:, :, :], ALU.mult)
                dve.wait_ge(S["d"], t * K + n[0])
                then(T(bt[:, :, :], bt[:, :, :], rate[:, :, at], ALU.mult))
                dve.sem_inc(S["scaled_in"], 1)
                dve.wait_ge(S["scores"], t + 1)
                then(STT(flip[:, :, :], R[0][:, :, :], BIG, over("before"), ALU.min, ALU.mult))
                T(flip[:, :, :], flip[:, :, :], over("ident"), ALU.add)
                STT(ak[:, :, :], R[1][:, :, :], BIG, over("before"), ALU.min, ALU.mult)
                STT(pb[:, :, :], R[2][:, :, :], BIG, over("upto"), ALU.min, ALU.mult)
                then(STT(pk[:, :, :], R[3][:, :, :], BIG, over("upto"), ALU.min, ALU.mult))
                dve.sem_inc(S["scores_read"], 1)
                inv.vector(dve, t)
                dve.wait_ge(S["grown"], t + 1)
                for e in range(2):
                    half = slice(64 * e, 64 * e + 64)
                    i = T(state[half, :, :], hm[half, :, :], R[3][half, 0:4, half], ALU.add)
                then(i)
                then(T(state[:, :, :], state[:, :, :], e1[:, :, P - 1:P].to_broadcast([P, F, 64]), ALU.mult))
                then(T(rk[:, :, :], r, k2, ALU.mult))
                T(rk[:, :, :], rk[:, :, :], spread(par[:, 0, :], P), ALU.mult).then_inc(S["rk_ready"], 1)
                dve.wait_ge(S["mean"], t + 1)
                T(y[:, :, :], y[:, :, :], R[0][:, 0:4, :], ALU.subtract).then_inc(S["centred"], 1)
                dve.wait_ge(S["bonus"], t + 1)
                then(T(rk[:, :, :], v, R[0][:, 4:8, :], ALU.mult))
                dve.wait_ge(S["roots"], t + 1)
                then(T(y[:, :, :], y[:, :, :], sq[:, :, :], ALU.mult))
                then(T(y[:, :, :], y[:, :, :], spread(par[:, 1, :], P), ALU.mult))
                then(T(y[:, :, :], y[:, :, :], spread(par[:, 2, :], P), ALU.add))
                then(T(y[:, :, :], y[:, :, :], rk[:, :, :], ALU.add))
                then(T(y[:, :, :], y[:, :, :], gate, ALU.mult))
                dve.sem_inc(S["gated"], 1)
                dve.sem_inc(S["stage_used"], 1)
                dve.sem_inc(S["turn"], 1)
                assert n[0] == K, n[0]


def clear(nc, dram, name, *where):
    with Part(nc, name, dram) as part:
        block = part.stack.enter_context(nc.Block())

        @block.gpsimd
        def _(pool):
            for w in where:
                nc.gpsimd.memset(w, 0.0)


def copy_out(nc, dram, name, to, what):
    with Part(nc, name, dram) as part:
        moved = part.sem("moved")
        block = part.stack.enter_context(nc.Block())

        @block.sync
        def _(sp):
            sp.dma_start(to, what).then_inc(moved, 16)
            sp.wait_ge(moved, 16)


def mamba(nc, dram, c_in, decay, dt):
    H, G, F = H_C, G_C, D_C // P
    with Part(nc, "mamba", dram) as part:
        groups = [f"group{a}{b}" for a in range(3) for b in range(3) if abs(a - b) < 2]
        names = ["ident", "ones", "upto", "after"] + groups
        mt = part.sb("mats", [P, len(names), P])
        mat = lambda n: mt[:, names.index(n), :]
        par = part.sb("par", [P, 2, F])
        stage = part.sb("stage", [P, 14, P])
        xs, bs, cs = stage[:, 0:6, :], stage[:, 6:10, :], stage[:, 10:14, :]
        gm, dec, pt = (part.sb(n, [P, H, P]) for n in ("gm", "dec", "pt"))
        cd = gm
        y, sq, skip, rs = (part.sb(n, [P, F, P]) for n in ("y", "sq", "skip", "rs"))
        xdt, xdd, state = (part.sb(n, [P, H, DH_C]) for n in ("xdt", "xdd", "state"))
        btok = part.sb("btok", [P, G, P])
        gs = part.sb("gs", [P, 2, H])
        bank = [part.ps(f"bank{i}", [P, n, 512]) for i, n in ((0, 3), (3, 2), (5, 2), (7, 1))]
        flat = lambda a: a.rearrange("p b (s c) -> p (b s) c", c=P)
        seg, ys, cb = flat(bank[0]), flat(bank[1]), flat(bank[3])
        small = bank[2][:, 1, 0:2 * H].rearrange("p (a h) -> p a h", a=2)
        grow = bank[2][:, :, :].rearrange("p b (s c) -> p (b s) c", c=256)[:, :, 0:192]
        S = {n: part.sem(n) for n in (
            "loaded", "staged", "stage_used", "turn", "decays_spread", "segments", "exps", "cb_done",
            "dec_read", "turned", "bt_done", "x_done", "ready", "outputs", "grown", "squared", "sums",
            "logs", "roots", "gated", "stored", "d")}
        block = part.stack.enter_context(nc.Block())
        n_loads = 16 * (len(names) + 2)

        @block.sync
        def _(sp):
            part.load_matrices(sp, mt, names, S["loaded"])
            sp.dma_start(par[:, 0, :], dram["mb_D"]).then_inc(S["loaded"], 16)
            sp.dma_start(par[:, 1, :], dram["mb_norm"]).then_inc(S["loaded"], 16)
            with sp.Fori(0, NT1) as t:
                sp.wait_ge(S["stage_used"], t + 1)
                sp.dma_start(stage[:, :, :], c_in[:, 6:20, bass.ts(t, P)]).then_inc(S["staged"], 16)
                sp.wait_ge(S["gated"], t * 2 + 2)
                sp.dma_start(dram["mix"].rearrange("(f p) t -> p f t", p=P)[:, 10:16, bass.ts(t, P)], y[:, :, :]).then_inc(S["stored"], 16)
            sp.wait_ge(S["stored"], 16 * NT1 + 16)

        @block.tensor
        def _(pe):
            M = nc.tensor.matmul
            pe.wait_ge(S["loaded"], n_loads)
            with pe.Fori(0, NT1) as t:
                pe.wait_ge(S["decays_spread"], t + 1)
                for b in range(3):
                    M(seg[:, 4 * b:4 * b + 4, :], mat("after"), gm[:, 4 * b:4 * b + 4, :], start=True, stop=True)
                for b in range(2):
                    M(ys[:, 4 * b:4 * b + 4, :], mat("ones"), gm[:, 4 * b:4 * b + 4, :], start=True, stop=True)
                M(flat(bank[2])[:, 0:4, :], mat("ones"), gm[:, 8:12, :], start=True, stop=True)
                for i, m in enumerate(("ones", "after")):
                    mm = M(small[:, i, :], mat(m), decay[:, bass.ds(t, 1), H_A:].rearrange("p a h -> p (a h)"), start=True, stop=True)
                mm.then_inc(S["segments"], 1)
                pe.wait_ge(S["staged"], t * 16 + 16)
                for g in range(G):
                    mm = M(cb[:, g, :], bs[:, g, :], cs[:, g, :], start=True, stop=True)
                mm.then_inc(S["cb_done"], 1)
                pe.wait_ge(S["exps"], t * 4 + 4)
                for f in range(F):
                    nc.tensor.transpose(seg[:, f, :], xs[:, f, :], mat("ident"))
                for g in range(G):
                    mm = nc.tensor.transpose(seg[:, 8 + g, :], bs[:, g, :], mat("ident"))
                mm.then_inc(S["turned"], 1)
                pe.wait_ge(S["bt_done"], t + 1)
                pe.wait_ge(S["ready"], t + 1)
                for h in range(H):
                    o = ys[(h % 2) * 64:(h % 2) * 64 + 64, h // 2, :]
                    M(o, xdt[:, h, :], pt[:, h, :], start=True, stop=False)
                    mm = M(o, state[:, h, :], cd[:, h, :], start=False, stop=True)
                mm.then_inc(S["outputs"], 1)
                for g in range(G):
                    mm = M(grow[:, g, :], btok[:, g, :], xdd[:, 3 * g:3 * g + 3, :], start=True, stop=True)
                mm.then_inc(S["grown"], 1)
                pe.wait_ge(S["squared"], t + 1)
                for m in range(3):
                    near = [f for f in range(3) if abs(f - m) < 2]
                    for f in near:
                        mm = M(bank[0][:, m, 0:256], mat(f"group{f}{m}"),
                               sq[:, :, :].rearrange("p (a f) c -> p a f c", a=2)[:, :, f, :],
                               start=(f == near[0]), stop=(f == near[-1]))
                mm.then_inc(S["sums"], 1)

        @block.scalar
        def _(act):
            A = nc.scalar.activation
            with act.Fori(0, NT1) as t:
                act.wait_ge(S["segments"], t + 1)
                act.wait_ge(S["turn"], t + 1)
                A(dec[:, :, :], seg, ACT.Exp).then_inc(S["exps"], 1)
                A(cd[:, 0:8, :], ys, ACT.Exp).then_inc(S["exps"], 1)
                A(cd[:, 8:12, :], flat(bank[2])[:, 0:4, :], ACT.Exp).then_inc(S["exps"], 1)
                A(gs[:, :, :], small, ACT.Exp).then_inc(S["exps"], 1)
                act.wait_ge(S["turned"], t + 1)
                A(btok[:, :, :], seg[:, 8:12, :], ACT.Copy).then_inc(S["bt_done"], 1)
                act.wait_ge(S["gated"], t * 2 + 1)
                A(sq[:, :, :], y[:, :, :], ACT.Square).then_inc(S["squared"], 1)
                act.wait_ge(S["sums"], t + 1)
                rs3 = rs[:, :, :].rearrange("p (m a) c -> p m (a c)", m=3)
                A(rs3, bank[0][:, :, 0:256], ACT.Ln, bias=NORM_EPS).then_inc(S["logs"], 1)
                act.wait_ge(S["logs"], t + 1)
                A(rs3, rs3, ACT.Exp, scale=-0.5).then_inc(S["roots"], 1)

        @block.vector
        def _(dve):
            V, T = nc.vector, nc.vector.tensor_tensor
            K = 9
            V.memset(state[:, :, :], 0.0).then_inc(S["turn"], 1)
            dve.sem_inc(S["stage_used"], 1)
            dve.sem_inc(S["stored"], 16)
            dve.wait_ge(S["loaded"], n_loads)
            with dve.Fori(0, NT1) as t:
                n = [0]

                def then(i):
                    n[0] += 1
                    i.then_inc(S["d"], 1)
                    dve.wait_ge(S["d"], t * K + n[0])
                row = lambda a: a.rearrange("p a h -> p (a h)")
                dve.wait_ge(S["turn"], t + 1)
                T(gm[:, :, :], over_heads(mat("upto"), H), spread(row(decay[:, bass.ds(t, 1), H_A:]), P), ALU.mult).then_inc(S["decays_spread"], 1)
                dve.wait_ge(S["staged"], t * 16 + 16)
                T(skip[:, :, :], xs, spread(par[:, 0, :], P), ALU.mult)
                dve.wait_ge(S["exps"], t * 4 + 4)
                then(T(dec[:, :, :], dec[:, :, :], over_heads(mat("upto"), H), ALU.mult))
                grouped = lambda a: a.rearrange("p (g e) c -> p g e c", g=G)
                by_group = lambda a: a.unsqueeze(2).to_broadcast([P, G, H // G, P])
                T(grouped(cd[:, :, :]), grouped(cd[:, :, :]), by_group(cs), ALU.mult)
                dve.wait_ge(S["cb_done"], t + 1)
                T(grouped(pt[:, :, :]), by_group(cb), grouped(dec[:, :, :]), ALU.mult)
                dve.wait_ge(S["turned"], t + 1)
                then(T(xdt[:, :, :], seg[:, 0:6, :].rearrange("p f (e c) -> p (f e) c", e=2), spread(row(dt[:, bass.ds(t, 1), :]), DH_C), ALU.mult))
                then(T(xdd[:, :, :], xdt[:, :, :], spread(gs[:, 1, :], DH_C), ALU.mult))
                dve.sem_inc(S["ready"], 1)
                dve.wait_ge(S["outputs"], t + 1)
                dve.wait_ge(S["stored"], t * 16 + 16)
                then(T(y[:, :, :], ys[:, 0:6, :], skip[:, :, :], ALU.add))
                then(T(y[:, :, :], y[:, :, :], c_in[:, 0:6, bass.ts(t, P)], ALU.mult))
                dve.sem_inc(S["gated"], 1)
                dve.wait_ge(S["grown"], t + 1)
                then(T(state[:, :, :], state[:, :, :], spread(gs[:, 0, :], DH_C), ALU.mult))
                then(T(state[:, :, :].rearrange("p (g e) c -> p g (e c)", g=G), state[:, :, :].rearrange("p (g e) c -> p g (e c)", g=G), grow, ALU.add))
                dve.wait_ge(S["roots"], t + 1)
                turned = y[:, :, :].rearrange("p (a m) c -> p m a c", a=2)
                then(T(turned, turned, rs[:, :, :].rearrange("p (m a) c -> p m a c", m=3), ALU.mult))
                then(T(y[:, :, :], y[:, :, :], spread(par[:, 1, :], P), ALU.mult))
                dve.sem_inc(S["gated"], 1)
                dve.sem_inc(S["stage_used"], 1)
                dve.sem_inc(S["turn"], 1)
                assert n[0] == K, n[0]


W_CONV = 512
HEADS2 = 8
DFF = 4096
EPS = 1e-6


def by_tokens(nc, dram, name, src, weights, col0, n, dst, func):
    with Part(nc, name, dram) as part:
        w = part.sb("w", [P, KD, n])
        acc = part.ps("acc", [P, 4, 512])
        loaded, product, read = (part.sem(x) for x in ("loaded", "product", "read"))
        block = part.stack.enter_context(nc.Block())

        @block.sync
        def _(sp):
            sp.dma_start(w[:, :, :], weights.rearrange("(k p) c -> p k c", p=P)[:, :, col0:col0 + n]).then_inc(loaded, 16)

        @block.tensor
        def _(pe):
            pe.wait_ge(loaded, 16)
            for t in range(NT):
                if t >= 4:
                    pe.wait_ge(read, t - 3)
                for k in range(KD):
                    mm = nc.tensor.matmul(acc[:, t % 4, :n], src[:, k, t * P:(t + 1) * P], w[:, k, :],
                                          start=(k == 0), stop=(k == KD - 1))
                mm.then_inc(product, 1)

        @block.scalar
        def _(act):
            for t in range(NT):
                act.wait_ge(product, t + 1)
                nc.scalar.activation(dst[:, t, :], acc[:, t % 4, :n], func).then_inc(read, 1)


def gated_conv(nc, dram, proj, dst):
    F, N = 4, SEQ
    with Part(nc, "gconv", dram) as part:
        taps = part.sb("taps", [P, 3, F])
        v = part.sb("v", [P, 2, 2 + N])
        loaded, step = part.sem("loaded"), part.sem("step")
        block = part.stack.enter_context(nc.Block())

        @block.sync
        def _(sp):
            sp.dma_start(taps[:, :, :], dram["conv_w_2"]).then_inc(loaded, 16)

        @block.vector
        def _(dve):
            V, n = nc.vector, [0]

            def then(i):
                n[0] += 1
                i.then_inc(step, 1)
                dve.wait_ge(step, n[0])
            dve.wait_ge(loaded, 16)
            then(V.memset(v[:, :, 0:2], 0.0))
            for f in range(F):
                s, out = f % 2, dst[:, f, :]
                then(V.tensor_tensor(v[:, s, 2:], proj[:, 4 + f, :], proj[:, 8 + f, :], ALU.mult))
                then(V.tensor_scalar(out, v[:, s, 2:], taps[:, 2, f:f + 1], None, ALU.mult))
                then(V.scalar_tensor_tensor(out, v[:, s, 1:1 + N], taps[:, 1, f:f + 1], out, ALU.mult, ALU.add))
                then(V.scalar_tensor_tensor(out, v[:, s, 0:N], taps[:, 0, f:f + 1], out, ALU.mult, ALU.add))
                then(V.tensor_tensor(out, out, proj[:, f, :], ALU.mult))


def stick_breaking(nc, dram, qk, v, dst):
    PAIRS, QC = HEADS2 // 2, SEQ // 512
    units = [(qc, kt, e) for qc in range(QC) for kt in range(4 * qc + 3, -1, -1) for e in range(2)]
    U, SL = len(units), 4

    def span(u):
        qc, kt, _ = units[u]
        return max(kt * P - qc * 512, 0), kt >= 4 * qc
    first = lambda u: units[u][1] == 4 * units[u][0] + 3
    last = lambda u: units[u][1] == 0
    runs = lambda u: sum(not last(w) for w in range(u + 1))
    RU = runs(U - 1)
    with Part(nc, "stick", dram) as part:
        names = ["neg_from", "neg_ones", "before", "zeros"]
        mt = part.sb("mats", [P, len(names), P])
        mat = lambda n: mt[:, names.index(n), :]
        k = part.sb("k", [P, SEQ])
        vs = part.sb("vs", [P, NT, P])
        qz = part.sb("qz", [P, 2, SEQ])
        ex, soft, att = (part.sb(n, [P, SL, 512]) for n in ("ex", "soft", "att"))
        run = part.sb("run", [P, 2, 512])
        score = part.ps("score", [P, SL, 512])
        out = part.ps("out", [P, 4, 512])
        S = {n: part.sem(n) for n in (
            "loaded", "staged", "stage_used", "zeroed", "q_ready", "z_done", "absd", "expd", "logd", "soft_done",
            "summed", "weighed", "masked", "run_done", "applied", "out_read", "d")}
        block = part.stack.enter_context(nc.Block())
        n_diag = sum(span(u)[1] for u in range(U))

        @block.sync
        def _(sp):
            part.load_matrices(sp, mt, names, S["loaded"])
            with sp.Fori(0, PAIRS) as i:
                sp.wait_ge(S["stage_used"], i + 1)
                sp.dma_start(k[:, :], qk[:, bass.ds(i + 4, 1), :].rearrange("p a n -> p (a n)")).then_inc(S["staged"], 16)
                sp.dma_start(vs[:, :, :], v[:, :, bass.ts(i, P)]).then_inc(S["staged"], 16)

        @block.tensor
        def _(pe):
            M = nc.tensor.matmul
            pe.wait_ge(S["loaded"], 16 * len(names))
            with pe.Fori(0, PAIRS) as i:
                def scores(u):
                    qc, kt, e = units[u]
                    o, _ = span(u)
                    if u >= SL:
                        pe.wait_ge(S["weighed"], i * U + u - SL + 1)
                    M(score[:, u % SL, o:], k[:, kt * P:(kt + 1) * P], qz[:, e, qc * 512 + o:(qc + 1) * 512],
                      start=True, stop=True).then_inc(S["z_done"], 1)
                pe.wait_ge(S["staged"], i * 32 + 32)
                pe.wait_ge(S["q_ready"], i + 1)
                pe.wait_ge(S["out_read"], i + 1)
                for e in range(2):
                    for qc in range(QC):
                        M(out[64 * e:64 * e + 64, 2 * e + qc, :], mat("zeros")[:, 0:64], qz[:, e, qc * 512:(qc + 1) * 512],
                          start=True, stop=True)
                scores(0)
                scores(1)

                def apply(u):
                    qc, kt, e = units[u]
                    o, _ = span(u)
                    if span(u)[1]:
                        pe.wait_ge(S["masked"], i * n_diag + sum(span(w)[1] for w in range(u + 1)))
                    else:
                        pe.wait_ge(S["weighed"], i * U + u + 1)
                    M(out[64 * e:64 * e + 64, 2 * e + qc, o:], vs[:, kt, 64 * e:64 * e + 64], att[:, u % SL, o:],
                      start=False, stop=True, skip_group_check=True).then_inc(S["applied"], 1)
                for u in range(U):
                    if u + 2 < U:
                        scores(u + 2)
                    o, _ = span(u)
                    pe.wait_ge(S["soft_done"], i * U + u + 1)
                    mm = M(score[:, u % SL, o:], mat("neg_from"), soft[:, u % SL, o:], start=False, stop=True,
                           skip_group_check=True)
                    if not first(u):
                        pe.wait_ge(S["run_done"], i * RU + runs(u - 2))
                        mm = M(score[:, u % SL, o:], mat("neg_ones"), run[:, units[u][2], o:], start=False, stop=True,
                               skip_group_check=True)
                    mm.then_inc(S["summed"], 1)
                    if u >= 1:
                        apply(u - 1)
                apply(U - 1)

        @block.scalar
        def _(act):
            A = nc.scalar.activation
            with act.Fori(0, PAIRS) as i:
                def softplus(u):
                    o, _ = span(u)
                    act.wait_ge(S["z_done"], i * U + u + 1)
                    if u >= SL:
                        act.wait_ge(S["run_done"], i * RU + runs(u - SL))
                        act.wait_ge(S["summed"], i * U + u - SL + 1)
                    A(ex[:, u % SL, o:], score[:, u % SL, o:], ACT.Abs).then_inc(S["absd"], 1)
                    act.wait_ge(S["absd"], i * U + u + 1)
                    A(ex[:, u % SL, o:], ex[:, u % SL, o:], ACT.Exp, scale=-1.0).then_inc(S["expd"], 1)
                    act.wait_ge(S["expd"], i * U + u + 1)
                    A(soft[:, u % SL, o:], ex[:, u % SL, o:], ACT.Ln, bias=1.0).then_inc(S["logd"], 1)

                def weigh(u):
                    o, _ = span(u)
                    act.wait_ge(S["summed"], i * U + u + 1)
                    if u >= SL:
                        act.wait_ge(S["applied"], i * U + u - SL + 1)
                    A(att[:, u % SL, o:], score[:, u % SL, o:], ACT.Exp).then_inc(S["weighed"], 1)
                softplus(0)
                for u in range(U):
                    if u + 1 < U:
                        softplus(u + 1)
                    weigh(u)

        @block.gpsimd
        def _(pool):
            pool.wait_ge(S["loaded"], 16 * len(names))
            with pool.Fori(0, PAIRS) as i:
                for u in range(U):
                    e, (o, _) = units[u][2], span(u)
                    if last(u):
                        continue
                    pool.wait_ge(S["soft_done"], i * U + u + 1)
                    pool.wait_ge(S["summed"], i * U + u + 1)
                    r = run[:, e, :]
                    if first(u):
                        nc.gpsimd.tensor_tensor(r[:, o:], soft[:, u % SL, o:], mat("zeros"), ALU.add)
                        nc.gpsimd.memset(r[:, 0:o], 0.0).then_inc(S["run_done"], 1)
                    else:
                        nc.gpsimd.tensor_tensor(r[:, o:], r[:, o:], soft[:, u % SL, o:], ALU.add).then_inc(S["run_done"], 1)
                    pool.wait_ge(S["run_done"], i * RU + runs(u))

        @block.vector
        def _(dve):
            V, T = nc.vector, nc.vector.tensor_tensor
            V.memset(qz[:, :, :], 0.0).then_inc(S["zeroed"], 1)
            dve.wait_ge(S["zeroed"], 1)
            dve.wait_ge(S["loaded"], 16 * len(names))
            dve.sem_inc(S["stage_used"], 1)
            dve.sem_inc(S["out_read"], 1)
            with dve.Fori(0, PAIRS) as i:
                for e in range(2):
                    half = slice(64 * e, 64 * e + 64)
                    q = V.tensor_scalar(qz[half, e, :], qk[half, bass.ds(i, 1), :].rearrange("p a n -> p (a n)"), 0.125, None, ALU.mult)
                q.then_inc(S["q_ready"], 1)

                def soft_of(u):
                    o, diag = span(u)
                    s = soft[:, u % SL, :]
                    dve.wait_ge(S["logd"], i * U + u + 1)
                    a = V.scalar_tensor_tensor(s[:, o:], score[:, u % SL, o:], 0.0, s[:, o:], ALU.max, ALU.add)
                    if diag:
                        a.then_inc(S["d"], 1)
                        dve.wait_ge(S["d"], i * n_diag + sum(span(w)[1] for w in range(u + 1)))
                        a = T(s[:, o:o + P], s[:, o:o + P], mat("before"), ALU.mult)
                    a.then_inc(S["soft_done"], 1)

                def mask_of(u):
                    o, diag = span(u)
                    if diag:
                        dve.wait_ge(S["weighed"], i * U + u + 1)
                        a = att[:, u % SL, o:o + P]
                        T(a, a, mat("before"), ALU.mult).then_inc(S["masked"], 1)
                soft_of(0)
                for u in range(U):
                    if u + 1 < U:
                        soft_of(u + 1)
                    mask_of(u)
                dve.wait_ge(S["applied"], i * U + U)
                for e in range(2):
                    half = slice(64 * e, 64 * e + 64)
                    c = V.tensor_copy(dst[half, bass.ds(i + 4, 1), :].rearrange("p a (q n) -> p (a q) n", n=512),
                                      out[half, 2 * e:2 * e + 2, :])
                c.then_inc(S["out_read"], 1)
                dve.sem_inc(S["stage_used"], 1)


def turn_rows(nc, dram, name, rows_in, n, dst):
    with Part(nc, name, dram) as part:
        ident = part.sb("ident", [P, 1, P])
        rows = part.sb("rows", [P, NT, n])
        cross = part.ps("cross", [P, 4, n // P, P])
        loaded, turned, moved = (part.sem(x) for x in ("loaded", "turned", "moved"))
        block = part.stack.enter_context(nc.Block())

        @block.sync
        def _(sp):
            part.load_matrices(sp, ident, ["ident"], loaded)
            sp.dma_start(rows[:, :, :], rows_in.rearrange("(t p) d -> p t d", p=P)).then_inc(loaded, 16)

        @block.tensor
        def _(pe):
            pe.wait_ge(loaded, 32)
            for t in range(0, NT):
                if t >= 2:
                    pe.wait_ge(moved, t - 1)
                for k in range(n // P):
                    mm = nc.tensor.transpose(cross[:, 2 * (t % 2), k, :], rows[:, t, k * P:(k + 1) * P], ident[:, 0, :])
                mm.then_inc(turned, 1)

        @block.vector
        def _(dve):
            for t in range(NT):
                dve.wait_ge(turned, t + 1)
                nc.vector.tensor_copy(dst[:, :, t * P:(t + 1) * P], cross[:, 2 * (t % 2)]).then_inc(moved, 1)


def second_block(nc, dram, hid):
    full = dict(src0=0, chunks=C2, width=W2)
    with Part(nc, "s2", dram) as p:
        mix = p.sb("mix", [P, KD, SEQ])
        with Part(nc, "s2a", dram) as a:
            conv = a.sb("conv", [P, 12, SEQ])
            v = a.sb("v", [P, NT, 512])
            m = a.sb("m", [P, KD, SEQ])
            normalise(nc, dram, "n2", hid, 0, dram["g_mix_2"], C2, W2, m)
            project(nc, dram, "p2c", m, 0, dram["w_in_2"], 0, KD, 12, C2, W2, conv, 0, 0, "copy")
            gated_conv(nc, dram, conv, mix)
            unit(nc, dram, "u2c", mix, 0, 4, "head_mean", dram["g_conv_out_2"], **full)
            project(nc, dram, "p2q", m, 0, dram["w_in_2"], 1536, KD, 8, C2, W2, conv, 0, 0, "copy")
            by_tokens(nc, dram, "p2v", m, dram["w_in_2"], 2560, 512, v, ACT.Copy)
            stick_breaking(nc, dram, conv, v, mix)
            unit(nc, dram, "u2a", mix, 4, 4, "head_mean", dram["g_attn_out_2"], **full)
        project(nc, dram, "p2o", mix, 0, dram["w_out_2"], 0, KD, 8, C2, W2, hid, 0, 0, "add")
    feed_forward(nc, dram, "2", hid, dram["g_mlp_2"], dram["w_up_2"], dram["w_down_2"])
    with Part(nc, "s2g", dram) as p:
        gate = p.sb("gate", [P, KD, SEQ])
        m = p.sb("m", [P, KD, SEQ])
        pt = p.sb("pt", [P, 2, SEQ])
        normalise(nc, dram, "n2g", hid, 0, dram["g_ple_2"], C2, W2, m)
        project(nc, dram, "p2g", m, 0, dram["w_ple_gate_2"], 0, KD, 8, C2, W2, gate, 0, 0, "sigmoid")
        turn_rows(nc, dram, "t2", dram["p_2"], 256, pt)
        project(nc, dram, "p2p", pt, 0, dram["w_ple_proj_2"], 0, 2, 8, C2, W2, hid, 0, 0, "gate_add", {"gate": gate})
    normalise(nc, dram, "n2f", hid, 0, dram["g_final_2"], C2, W2, hid)


def feed_forward(nc, dram, n, hid, gain, up, down):
    with Part(nc, "ff" + n, dram) as p:
        inner = p.sb("inner", [P, DFF // P, SEQ])
        with Part(nc, "ffm" + n, dram) as q:
            m = q.sb("m", [P, KD, SEQ])
            squares = inner[:, 0:KD, :].rearrange("p (a x) (y n) -> p a (x y) n", a=2, y=2)
            normalise(nc, dram, "nf" + n, hid, 0, gain, C2, W2, m, scratch=squares)
            project(nc, dram, "up" + n, m, 0, up, 0, KD, DFF // P, C2, W2, inner, 0, 0, "relu2")
        project(nc, dram, "down" + n, inner, 0, down, 0, DFF // P, KD, C2, W2, hid, 0, 0, "add")


def spatial_gate(nc, dram, sv, su, dst):
    G = 4
    with Part(nc, "sgu", dram) as part:
        ident = part.sb("ident", [P, 1, P])
        ws = part.sb("ws", [P, G, P])
        wt = part.sb("wt", [P, G, P])
        bs = part.sb("bs", [P, G, P])
        gain = part.sb("gain", [P, G])
        sq = part.sb("sq", [P, 32, P])
        ss = part.sb("ss", [P, 32])
        acc = part.ps("acc", [P, 4, NT, P])
        loaded, turned, moved, squared, summed, rooted, ready, mixed, read, step = (part.sem(x) for x in (
            "loaded", "turned", "moved", "squared", "summed", "rooted", "ready", "mixed", "read", "step"))
        block = part.stack.enter_context(nc.Block())
        svg = sv[:, :, :].rearrange("p t (g c) -> p (t g) c", g=G)

        @block.sync
        def _(sp):
            part.load_matrices(sp, ident, ["ident"], loaded)
            sp.dma_start(ws[:, :, :], dram["w_s_3"].rearrange("g p q -> p g q")).then_inc(loaded, 16)
            sp.dma_start(bs[:, :, :].rearrange("p g q -> p (g q)"), dram["b_s_3"].to_broadcast([P, 512])).then_inc(loaded, 16)
            sp.dma_start(gain[:, :], dram["sgu_norm_g_3"]).then_inc(loaded, 16)

        @block.tensor
        def _(pe):
            pe.wait_ge(loaded, 64)
            for g in range(G):
                mm = nc.tensor.transpose(acc[:, 0, g, :], ws[:, g, :], ident[:, 0, :])
            mm.then_inc(turned, 1)
            pe.wait_ge(moved, 1)
            pe.wait_ge(ready, 1)
            for g in range(G):
                for t in range(NT):
                    mm = nc.tensor.matmul(acc[:, g, t, :], sv[:, t, g * P:(g + 1) * P], wt[:, g, :], start=True, stop=True)
                mm.then_inc(mixed, 1)

        @block.scalar
        def _(act):
            nc.scalar.activation(sq[:, :, :], svg, ACT.Square).then_inc(squared, 1)
            act.wait_ge(turned, 1)
            nc.scalar.activation(wt[:, :, :], acc[:, 0, 0:4, :], ACT.Copy).then_inc(moved, 1)
            act.wait_ge(summed, 1)
            nc.scalar.activation(ss[:, :], ss[:, :], ACT.Ln, scale=1.0 / P, bias=EPS).then_inc(step, 1)
            act.wait_ge(step, 1)
            nc.scalar.activation(ss[:, :], ss[:, :], ACT.Exp, scale=-0.5).then_inc(rooted, 1)

        @block.vector
        def _(dve):
            V = nc.vector
            dve.wait_ge(squared, 1)
            V.tensor_reduce(ss[:, :], sq[:, :, :], mybir.AxisListType.X, ALU.add).then_inc(summed, 1)
            dve.wait_ge(rooted, 1)
            V.tensor_tensor(svg, svg, spread(ss[:, :], P), ALU.mult).then_inc(ready, 1)
            dve.wait_ge(loaded, 64)
            for g in range(G):
                dve.wait_ge(mixed, g + 1)
                o = dst[:, 4 + g, :].rearrange("p (t c) -> p t c", c=P)
                V.scalar_tensor_tensor(o, acc[:, g], gain[:, g:g + 1], over_heads(bs[:, g, :], NT), ALU.mult, ALU.add).then_inc(read, 1)
                dve.wait_ge(read, g + 1)
                V.tensor_tensor(dst[:, 4 + g, :], dst[:, 4 + g, :], su[:, g, :], ALU.mult)


def gla_decays(nc, dram, low, la):
    C, NCH = 64, SEQ // 64
    with Part(nc, "gdec", dram) as part:
        ones = part.sb("ones", [P, 1, P])
        w2 = part.sb("w2", [32, 512])
        bias = part.sb("bias", [1, 512])
        t = part.sb("t", [C, 2, 512])
        acc = part.ps("acc", [C, 2, 512])
        loaded, zeroed, product, absd, expd, logd, read, done = (part.sem(x) for x in (
            "loaded", "zeroed", "product", "absd", "expd", "logd", "read", "done"))
        block = part.stack.enter_context(nc.Block())

        @block.sync
        def _(sp):
            part.load_matrices(sp, ones, ["ones"], loaded)
            sp.wait_ge(zeroed, 1)
            sp.dma_start(w2[0:16, 0:256], dram["w_a2_fwd_3"]).then_inc(loaded, 16)
            sp.dma_start(w2[16:32, 256:512], dram["w_a2_bwd_3"]).then_inc(loaded, 16)
            sp.dma_start(bias[:, :], dram["b_a_3"]).then_inc(loaded, 16)

        @block.tensor
        def _(pe):
            pe.wait_ge(loaded, 64)
            for c in range(NCH):
                if c >= 2:
                    pe.wait_ge(read, c - 1)
                nc.tensor.matmul(acc[:, c % 2, :], low[0:32, 0, c * C:(c + 1) * C], w2[:, :], start=True, stop=False)
                nc.tensor.matmul(acc[:, c % 2, :], ones[0:1, 0, 0:C], bias[:, :], start=False, stop=True).then_inc(product, 1)

        @block.scalar
        def _(act):
            A = nc.scalar.activation
            for c in range(NCH):
                act.wait_ge(product, c + 1)
                if c >= 2:
                    act.wait_ge(read, c - 1)
                A(t[:, c % 2, :], acc[:, c % 2, :], ACT.Abs).then_inc(absd, 1)
                act.wait_ge(absd, c + 1)
                A(t[:, c % 2, :], t[:, c % 2, :], ACT.Exp, scale=-1.0).then_inc(expd, 1)
                act.wait_ge(expd, c + 1)
                A(t[:, c % 2, :], t[:, c % 2, :], ACT.Ln, bias=1.0).then_inc(logd, 1)

        @block.vector
        def _(dve):
            V = nc.vector
            V.memset(w2[:, :], 0.0).then_inc(zeroed, 1)
            for c in range(NCH):
                dve.wait_ge(logd, c + 1)
                V.scalar_tensor_tensor(la[:, c, :], acc[:, c % 2, :], 0.0, t[:, c % 2, :], ALU.min, ALU.subtract).then_inc(read, 1)
                dve.wait_ge(read, c + 1)
                V.tensor_scalar(la[:, c, :], la[:, c, :], 1.0 / 16.0, None, ALU.mult)


def gla(nc, dram, name, qk, v, la, osum, backward):
    C, H, F = 64, 4, 2
    off = 256 if backward else 0
    with Part(nc, name, dram) as part:
        names = ["ident", "from_mid64" if backward else "upto_mid64", "mid64", "after" if backward else "upto"]
        mt = part.sb("mats", [P, len(names), P])
        shift, mid, keep = mt[0:C, 1, 0:C], mt[0:C, 2, int(backward):int(backward) + 1], mt[0:C, 3, 0:C]
        las = part.sb("las", [C, 256])
        vs = part.sb("vs", [C, 512])
        e1, e3, kt = (part.sb(n, [P, F, C]) for n in ("e1", "e3", "kt"))
        em = part.sb("em", [P, F])
        qz = part.sb("qz", [P, F, 2, C])
        state, sm = (part.sb(n, [P, F, P]) for n in ("state", "sm"))
        at = part.sb("at", [C, H, C])
        ktok = part.sb("ktok", [C, F, P])
        bank = [part.ps(f"bank{i}", [P, 512]) for i in range(6)]
        S = {n: part.sem(n) for n in (
            "loaded", "staged", "stage_used", "turn", "decays", "exps", "scaled_in", "scores", "turned", "at_done",
            "ktok_done", "outputs", "d")}
        block = part.stack.enter_context(nc.Block())
        E = bank[0][:, 0:F * C].rearrange("p (f c) -> p f c", f=F)
        sc = bank[1][0:C, 0:H * C].rearrange("p (h c) -> p h c", h=H)
        kx = bank[2][0:C, 0:F * P].rearrange("p (f c) -> p f c", f=F)
        out = bank[3][:, 0:H * C].rearrange("p (h c) -> p h c", h=H)
        grow = bank[4][:, :].rearrange("p (f c) -> p f c", f=F)
        end = 0 if backward else C - 1

        def turns(eng, body):
            with eng.Fori(0, NT) as i:
                tile = (i - (NT - 1)) * (-1) if backward else i
                for j in range(2):
                    body(tile, 1 - j if backward else j, i * 2 + j)

        @block.sync
        def _(sp):
            part.load_matrices(sp, mt, names, S["loaded"])

            def body(t, s, n):
                sp.wait_ge(S["stage_used"], n + 1)
                sp.dma_start(las[:, :], la[:, bass.ds(t * 2 + s, 1), off:off + 256].rearrange("p a c -> p (a c)")).then_inc(S["staged"], 16)
                sp.dma_start(vs[:, :], v[64 * s:64 * s + 64, bass.ds(t, 1), :].rearrange("p a c -> p (a c)")).then_inc(S["staged"], 16)
            turns(sp, body)

        @block.tensor
        def _(pe):
            M = nc.tensor.matmul
            pe.wait_ge(S["loaded"], 16 * len(names))

            def body(t, s, n):
                pe.wait_ge(S["staged"], n * 32 + 32)
                pe.wait_ge(S["turn"], n + 1)
                for f in range(F):
                    M(E[:, f, :], las[:, f * P:(f + 1) * P], shift, start=True, stop=True)
                    mm = M(bank[0][:, F * C + f:F * C + f + 1], las[:, f * P:(f + 1) * P], mid, start=True, stop=True)
                mm.then_inc(S["decays"], 1)
                pe.wait_ge(S["scaled_in"], n + 1)
                for f in range(F):
                    M(sc[:, 2 * f:2 * f + 2, :], kt[:, f, :], qz[:, f, :, :], start=True, stop=True)
                mm = None
                for f in range(F):
                    mm = nc.tensor.transpose(kx[:, f, :], kt[:, f, :], mt[:, 0, :])
                mm.then_inc(S["turned"], 1)
                pe.wait_ge(S["at_done"], n + 1)
                for h in range(H):
                    M(out[:, h, :], vs[:, h * P:(h + 1) * P], at[:, h, :], start=True, stop=False)
                    M(out[:, h, :], sm[:, h // 2, :], qz[:, h // 2, h % 2, :], start=False, stop=True)
                pe.wait_ge(S["ktok_done"], n + 1)
                for f in range(F):
                    mm = M(grow[:, f, :], ktok[:, f, :], vs[:, f * 256:(f + 1) * 256], start=True, stop=True)
                mm.then_inc(S["outputs"], 1)
            turns(pe, body)

        @block.scalar
        def _(act):
            A = nc.scalar.activation

            def body(t, s, n):
                act.wait_ge(S["decays"], n + 1)
                A(e1[:, :, :], E, ACT.Exp).then_inc(S["exps"], 1)
                A(e3[:, :, :], E, ACT.Exp, scale=-1.0).then_inc(S["exps"], 1)
                A(em[:, :], bank[0][:, F * C:F * C + F], ACT.Exp).then_inc(S["exps"], 1)
                act.wait_ge(S["turned"], n + 1)
                A(ktok[:, :, :], kx, ACT.Copy).then_inc(S["ktok_done"], 1)
            turns(act, body)

        @block.vector
        def _(dve):
            V, T = nc.vector, nc.vector.tensor_tensor
            K = 3
            V.memset(qz[:, :, :, :], 0.0)
            V.memset(state[:, :, :], 0.0).then_inc(S["turn"], 1)
            dve.wait_ge(S["turn"], 1)
            dve.wait_ge(S["loaded"], 16 * len(names))
            dve.sem_inc(S["stage_used"], 1)

            def body(t, s, n):
                tok = bass.ds(t * P + s * C, C)
                dve.wait_ge(S["exps"], n * 3 + 3)
                T(sm[:, :, :], state[:, :, :], spread(em[:, :], P), ALU.mult)
                for e in range(2):
                    half = slice(64 * e, 64 * e + 64)
                    V.scalar_tensor_tensor(qz[half, :, e, :], qk[half, 0:2, tok], 0.125, e1[half, :, :], ALU.mult, ALU.mult)
                T(kt[:, :, :], qk[:, 2:4, tok], e3[:, :, :], ALU.mult).then_inc(S["scaled_in"], 1)
                dve.wait_ge(S["turned"], n + 1)
                T(at[:, :, :], sc, over_heads(keep, H), ALU.mult).then_inc(S["at_done"], 1)
                dve.wait_ge(S["outputs"], n + 1)
                for e in range(2):
                    half = slice(64 * e, 64 * e + 64)
                    i = T(state[half, :, :], sm[half, :, :], grow[half, :, e * P:(e + 1) * P], ALU.add)
                i.then_inc(S["d"], 1)
                if backward:
                    T(osum[:, :, tok], osum[:, :, tok], out, ALU.add).then_inc(S["d"], 1)
                else:
                    V.tensor_copy(osum[:, :, tok], out).then_inc(S["d"], 1)
                dve.wait_ge(S["d"], n * K + 2)
                T(state[:, :, :], state[:, :, :], e1[:, :, end:end + 1].to_broadcast([P, F, P]), ALU.mult).then_inc(S["d"], 1)
                dve.wait_ge(S["d"], n * K + 3)
                dve.sem_inc(S["stage_used"], 1)
                dve.sem_inc(S["turn"], 1)
            turns(dve, body)


def third_block(nc, dram, hid):
    full = dict(src0=0, chunks=C2, width=W2)
    w = dram["w_in_3"]
    with Part(nc, "s3", dram) as p:
        mix = p.sb("mix", [P, KD, SEQ])
        su = p.sb("su", [P, 4, SEQ])
        sv = p.sb("sv", [P, NT, 512])
        v = p.sb("v", [P, NT, 512])
        qk = p.sb("qk", [P, 4, SEQ])
        g = p.sb("g", [P, 4, SEQ])
        low = p.sb("low", [P, 1, SEQ])
        with Part(nc, "s3m", dram) as q:
            m = q.sb("m", [P, KD, SEQ])
            normalise(nc, dram, "n3", hid, 0, dram["norm_mix_g_3"], 4, 256, m)
            project(nc, dram, "p3q", m, 0, w, 0, KD, 4, C2, W2, qk, 0, 0, "copy")
            project(nc, dram, "p3g", m, 0, w, 1024, KD, 4, C2, W2, g, 0, 0, "silu")
            project(nc, dram, "p3a", m, 0, w, 1536, KD, 1, C2, W2, low, 0, 0, "copy")
            project(nc, dram, "p3u", m, 0, w, 1568, KD, 4, C2, W2, su, 0, 0, "gelu")
            by_tokens(nc, dram, "p3v", m, w, 512, 512, v, ACT.Copy)
            by_tokens(nc, dram, "p3s", m, w, 2080, 512, sv, ACT.Gelu)
        spatial_gate(nc, dram, sv, su, mix)
        with Part(nc, "s3l", dram) as q:
            la = q.sb("la", [64, SEQ // 64, 512])
            gla_decays(nc, dram, low, la)
            gla(nc, dram, "glaf", qk, v, la, mix[:, 0:4, :], False)
            gla(nc, dram, "glab", qk, v, la, mix[:, 0:4, :], True)
        unit(nc, dram, "u3", mix, 0, 4, "mean", dram["gla_norm_g_3"], times=g, **full)
        project(nc, dram, "p3o", mix, 0, dram["w_out_3"], 0, KD, 8, C2, W2, hid, 0, 0, "add")
    feed_forward(nc, dram, "3", hid, dram["norm_mlp_g_3"], dram["w_mlp1_3"], dram["w_mlp2_3"])
    normalise(nc, dram, "n3f", hid, 0, dram["final_norm_g_3"], C2, W2, hid)


def first_block(nc, dram):
    w = dram["w_in"]
    with Part(nc, "b1", dram) as p:
        decay = p.sb("decay", [P, NT1, H_A + H_C])
        beta = p.sb("beta", [P, NT1, H_A])
        dt = p.sb("dt", [P, NT1, H_C])
        pool = p.sb("pool", [P, 25, T1])
        with Part(nc, "b1h", dram) as q:
            hn = q.sb("hn", [P, KD, T1])
            rows = pool[:, KD:2 * KD].rearrange("p a t -> p (a t)").rearrange("p (t d) -> p t d", d=D)
            entry(nc, dram, pool[:, 0:KD], rows)
            copy_out(nc, dram, "keep", dram["hidden"].rearrange("(k p) t -> p k t", p=P), pool[:, 0:KD, T1 - SEQ:])
            normalise(nc, dram, "n1", pool[:, 0:KD], S1, dram["norm_pre"], C1, W1, hn)
            clear(nc, dram, "c1", pool[:, :, :S1], hn[:, :, :S1])
            gates(nc, dram, hn, decay, beta, dt)
            project(nc, dram, "pa", hn, S1, w, 0, KD, 18, C1, W1, pool, S1, 0, "conv", {"taps": dram["dn_conv"]})
            project(nc, dram, "pz", hn, S1, w, 18 * P, KD, 6, C1, W1, pool, S1, 18, "silu_gain", {"gain": dram["dn_norm"]})
            unit(nc, dram, "uq", pool, 0, 6, "ones", DH_A ** -0.5)
            unit(nc, dram, "uk", pool, 6, 6, "ones", 1.0)
            delta_rule(nc, dram, pool[:, 0:24], decay, beta)
            project(nc, dram, "pc", hn, S1, w, P_A + P_B, KD, 6, C1, W1, pool, S1, 0, "silu")
            project(nc, dram, "pd", hn, S1, w, P_A + P_B + D_C, KD, 14, C1, W1, pool, S1, 6, "conv",
                    {"taps": dram["mb_conv"], "bias": dram["mb_conv_b"]})
            mamba(nc, dram, pool, decay, dt)
            clear(nc, dram, "c3", pool[:, :, :S1])
            project(nc, dram, "pb", hn, S1, w, P_A, KD, 17, C1, W1, pool, S1, 0, "shift", {"mu": dram["rw_mu"]})
        b, rate, unit_k = pool[:, 0:17], pool[:, 17:21], pool[:, 21:25]
        rwkv_prepare(nc, dram, b, rate, unit_k)
        unit(nc, dram, "uu", unit_k, 0, 4, "head_ones", 1.0)
        rwkv(nc, dram, b, rate, unit_k)


def first_out(nc, dram, hid):
    with Part(nc, "b1o", dram) as p:
        mix = p.sb("mix", [P, 16, SEQ])
        o = p.sb("o", [P, KD, SEQ])
        copy_out(nc, dram, "ldm", mix[:, :, :], dram["mix"].rearrange("(f p) t -> p f t", p=P)[:, :, T1 - SEQ:])
        copy_out(nc, dram, "ldh", hid[:, :, :], dram["hidden"].rearrange("(k p) t -> p k t", p=P))
        project(nc, dram, "p1o", mix, 0, dram["w_out"], 0, 16, 8, C2, W2, o, 0, 0, "copy")
        normalise(nc, dram, "n1o", o, 0, dram["norm_post"], 4, 256, hid, add=True)


def program(nc, dram, out):
    dram["hidden"] = nc.dram_tensor("hidden", (D, SEQ), F32, kind="Internal").ap()
    dram["mix"] = nc.dram_tensor("mix", (2 * D, T1), F32, kind="Internal").ap()
    dram["log_w"] = nc.dram_tensor("log_w", (T1, D_B), F32, kind="Internal").ap()
    first_block(nc, dram)
    with Part(nc, "all", dram) as p:
        hid = p.sb("hid", [P, KD, SEQ])
        first_out(nc, dram, hid)
        second_block(nc, dram, hid)
        third_block(nc, dram, hid)
        leave(nc, dram, hid, out)


def pack(inputs):
    f = {k: np.asarray(v) for k, v in inputs.items()}
    cols = lambda v: np.ascontiguousarray(v.reshape(-1, P).T)
    taps = lambda v: np.ascontiguousarray(v.reshape(v.shape[0], -1, P).transpose(2, 0, 1))
    m = constant_matrices()
    d = {"matrices": np.concatenate([m[n] for n in NAMES]), "x": f["x"], "meta_tokens": f["meta_tokens"],
         "w_in": f["w_in"][0], "w_out": f["w_out"][0],
         "dn_conv": taps(f["dn_conv"][0]), "mb_conv": taps(f["mb_conv"][0]), "conv_w_2": taps(f["conv_w_2"][0]),
         "gate_bias": np.concatenate([f["dn_dt_bias"], f["mb_dt_bias"]], 1),
         "gate_log": np.concatenate([f["dn_A_log"], f["mb_A_log"]], 1),
         "g_final_2": cols(f["g_final_2"]), "final_norm_g_3": cols(f["final_norm_g_3"]),
         "mb_D": cols(np.repeat(f["mb_D"][0], DH_C)), "rw_w0": f["rw_w0"],
         "p_2": f["p_2"][0, 0], "b_s_3": f["b_s_3"].reshape(1, -1),
         "b_a_3": np.concatenate([f["b_a_fwd_3"], f["b_a_bwd_3"]], 1)}
    d["dn_norm"] = cols(np.tile(f["dn_norm"][0], H_A))
    for n in ("norm_pre", "norm_post", "mb_conv_b", "rw_mu", "rw_a0", "rw_k_k", "rw_k_a", "rw_r_k",
              "rw_ln_w", "rw_ln_b", "mb_norm", "g_mix_2", "g_conv_out_2", "g_attn_out_2", "g_mlp_2", "g_ple_2",
              "norm_mix_g_3", "gla_norm_g_3", "sgu_norm_g_3", "norm_mlp_g_3"):
        d[n] = cols(f[n][0])
    for n in ("rw_w2", "rw_a2", "w_in_2", "w_out_2", "w_up_2", "w_down_2", "w_ple_gate_2", "w_ple_proj_2",
              "w_in_3", "w_a2_fwd_3", "w_a2_bwd_3", "w_s_3", "w_out_3", "w_mlp1_3", "w_mlp2_3"):
        d[n] = f[n][0]
    return d



def kernel(**inputs):
    import concourse.bacc as _bacc
    from concourse.bass_utils import run_bass_kernel_spmd as _run

    nc = _bacc.Bacc("TRN2", target_bir_lowering=False, num_devices=1)
    arrays = pack(inputs)
    dram = {n: nc.dram_tensor(n + "_dram", a.shape, mybir.dt.from_np(a.dtype), kind="ExternalInput").ap()
            for n, a in arrays.items()}
    out = nc.dram_tensor("out_dram", (SEQ, D), F32, kind="ExternalOutput").ap()
    program(nc, dram, out)
    r = _run(nc, [{n + "_dram": a for n, a in arrays.items()}], core_ids=[0])
    return r.results[0]["out_dram"].reshape(1, SEQ, D)
```

```python
import math
from contextlib import ExitStack

import numpy as np

import concourse.bass as bass
from concourse import mybir

F32 = mybir.dt.float32
ACT = mybir.ActivationFunctionType
ALU = mybir.AluOpType

P = 128
D = 1024
KD = D // P
SEQ = 1024
META = 16
FRONT = P - META
T1 = FRONT + META + SEQ
NT1 = T1 // P
NT = SEQ // P
W1 = 352
C1 = 3
S1 = T1 - C1 * W1
LIVE = C1 * W1
W2 = 512
C2 = SEQ // W2
NORM_EPS = 1e-6

H_A, DH_A = 6, 128
D_A = H_A * DH_A
H_B, DH_B = 8, 64
D_B = H_B * DH_B
H_C, DH_C, G_C, N_C = 12, 64, 4, 128
D_C = H_C * DH_C
P_A = 4 * D_A + 2 * H_A
P_B = 4 * D_B + 128
P_C = 2 * D_C + 2 * G_C * N_C + H_C
GN_EPS = 64e-5

LEVELS = 7


def constant_matrices():
    r = np.arange(P)[:, None]
    c = np.arange(P)[None, :]
    m = {
        "ident": r == c,
        "ones": np.ones((P, P)),
        "zeros": np.zeros((P, P)),
        "upto": r <= c,
        "before": r < c,
        "after": r > c,
        "from": r >= c,
        "neg_before": -1.0 * (r < c),
        "neg_from": -1.0 * (r >= c),
        "neg_ones": -np.ones((P, P)),
        "upto_mid": 1.0 * (r <= c) - (r <= P // 2 - 1),
        "before_mid": 1.0 * (r < c) - (r <= P // 2 - 1),
        "head_mean": (r // 64 == c // 64) / 64.0,
        "head_ones": r // 64 == c // 64,
        "upto_mid64": 1.0 * (r <= c) - (r <= 32),
        "from_mid64": 1.0 * (r >= c) - (r >= 31),
        "mid64": np.where(c == 0, r <= 32, (c == 1) & (r >= 31)),
        "real": r >= FRONT,
        "mean": np.full((P, P), 1.0 / P),
        "mid": (r <= P // 2 - 1) & (c == 0),
    }
    for l in range(LEVELS):
        b = 2 ** l
        pair = (r // (2 * b) == c // (2 * b)) & (r // b % 2 == 1) & (c // b % 2 == 0)
        m[f"join{l}"] = pair | (r == c)
    m["join0T"] = m["join0"].T
    g = lambda tile, i: (tile * P + i) // 192
    for a in range(3):
        for b in range(3):
            if abs(a - b) < 2:
                m[f"group{a}{b}"] = (g(a, r) == g(b, c)) / 192.0
    return {k: np.broadcast_to(v, (P, P)).astype(np.float32) for k, v in m.items()}


NAMES = list(constant_matrices())


class Part:

    def __init__(self, nc, name, dram):
        self.nc, self.name, self.dram, self.stack = nc, name, dram, ExitStack()
        self.sems = []

    def __enter__(self):
        return self

    def __exit__(self, *a):
        self.stack.close()
        if self.sems:
            self.nc.clear_and_free_semaphores(self.sems)
            self.nc.all_engine_barrier()

    def sb(self, name, shape, dt=F32):
        return self.stack.enter_context(self.nc.sbuf_tensor(f"{self.name}_{name}", list(shape), dt))

    def ps(self, name, shape):
        return self.stack.enter_context(self.nc.psum_tensor(f"{self.name}_{name}", list(shape), F32))

    def sem(self, name):
        s = self.nc.alloc_semaphore(f"{self.name}_{name}")
        self.sems.append(s)
        return s

    def load_matrices(self, eng, where, names, sem):
        for i, n in enumerate(names):
            j = NAMES.index(n)
            eng.dma_start(where[:, i, :], self.dram["matrices"][j * P:(j + 1) * P, :]).then_inc(sem, 16)
        return 16 * len(names)


def spread(ap, n):
    return ap.unsqueeze(2).to_broadcast([ap.shape[0], ap.shape[1], n])


def project(nc, dram, name, src, src0, weights, col0, k_tiles, n_tiles, chunks, width, dst, dst0,
            dst_tile0, mode, extra=None):
    live = chunks * width
    halo = {"conv": 3, "shift": 1}.get(mode, 0)
    with Part(nc, name, dram) as part:
        w = [part.sb(f"w{s}", [P, k_tiles, P]) for s in range(2)]
        acc = [part.ps(f"acc{s}", [P, chunks, 512]) for s in range(2)]
        w_ready = [part.sem(f"w_ready{s}") for s in range(2)]
        params_ready = part.sem("params_ready")
        product_done = part.sem("product_done")
        acc_free = part.sem("acc_free")
        raw_ready = part.sem("raw_ready")
        vector_done = part.sem("vector_done")
        tile_done = part.sem("tile_done")
        step = part.sem("step")
        n_params, params = 0, {}
        if halo:
            raw = [part.sb(f"raw{s}", [P, halo + live]) for s in range(2)]
        if mode in ("conv", "shift"):
            tmp = [part.sb(f"tmp{s}", [P, live]) for s in range(2)]
        if mode in ("silu_gain", "gate_add"):
            tmp = [part.sb(f"tmp{s}", [P, chunks, width]) for s in range(2)]
        if mode == "conv":
            params["taps"] = part.sb("taps", [P, 4, n_tiles])
            if extra.get("bias") is not None:
                params["bias"] = part.sb("bias", [P, n_tiles])
        if mode == "shift":
            params["mu"] = part.sb("mu", [P, n_tiles])
            params["keep"] = part.sb("keep", [P, n_tiles])
        if mode == "silu_gain":
            params["gain"] = part.sb("gain", [P, n_tiles])
        block = part.stack.enter_context(nc.Block())
        w_view = weights.rearrange("(k p) c -> p k c", p=P)

        def each_tile(eng, body):
            if n_tiles >= 2:
                with eng.Fori(0, n_tiles // 2) as i:
                    for s in range(2):
                        body(i * 2 + s, s, i)
            if n_tiles % 2:
                body(n_tiles - 1, 0, n_tiles // 2)

        @block.sync
        def _(sp):
            if mode == "conv":
                for j in range(4):
                    sp.dma_start(params["taps"][:, j, :], extra["taps"][:, j, :]).then_inc(params_ready, 16)
                if "bias" in params:
                    sp.dma_start(params["bias"][:, :], extra["bias"]).then_inc(params_ready, 16)
            if mode == "shift":
                sp.dma_start(params["mu"][:, :], extra["mu"]).then_inc(params_ready, 16)
            if mode == "silu_gain":
                sp.dma_start(params["gain"][:, :], extra["gain"]).then_inc(params_ready, 16)

            def load(f, s, i):
                sp.wait_ge(product_done, f + 1)
                sp.dma_start(w[s][:, :, :], w_view[:, :, bass.ds(f * P + col0, P)]).then_inc(w_ready[s], 16)
            each_tile(sp, load)

        n_params = {"conv": 5 if "bias" in params else 4, "shift": 1, "silu_gain": 1}.get(mode, 0) * 16

        @block.tensor
        def _(pe):
            pe.sem_inc(product_done, 2)

            def multiply(f, s, i):
                pe.wait_ge(w_ready[s], i * 16 + 16)
                pe.wait_ge(acc_free, f + 1)
                for c in range(chunks):
                    for k in range(k_tiles):
                        mm = nc.tensor.matmul(acc[s][:, c, :width], w[s][:, k, :],
                                              src[:, k, src0 + c * width:src0 + (c + 1) * width],
                                              start=(k == 0), stop=(k == k_tiles - 1))
                mm.then_inc(product_done, 1)
            each_tile(pe, multiply)

        def out(f):
            return dst[:, f + dst_tile0, dst0:dst0 + live]

        def out3(f):
            return out(f).rearrange("p (c n) -> p c n", c=chunks)

        def a3(s):
            return acc[s][:, :, :width]

        @block.scalar
        def _(act):
            if mode in ("conv", "shift"):
                act.sem_inc(acc_free, 2)

                def finish(f, s, i):
                    act.wait_ge(product_done, f + 3)
                    act.wait_ge(vector_done, f + 1)
                    nc.scalar.activation(raw[s][:, halo:].rearrange("p (c n) -> p c n", c=chunks), a3(s),
                                         ACT.Copy).then_inc(acc_free, 1)
                    if mode == "conv":
                        act.wait_ge(vector_done, f + 3)
                        bias = params["bias"][:, bass.ds(f, 1)] if "bias" in params else 0.0
                        nc.scalar.activation(out(f), tmp[s][:, :], ACT.Silu, bias=bias).then_inc(tile_done, 1)
                if mode == "conv":
                    act.sem_inc(tile_done, 2)
                    act.wait_ge(params_ready, n_params)
                each_tile(act, finish)
            elif mode in ("silu_gain", "relu2"):
                if mode == "silu_gain":
                    act.sem_inc(acc_free, 2)

                def finish(f, s, i):
                    act.wait_ge(product_done, f + 3)
                    if mode == "silu_gain":
                        act.wait_ge(vector_done, f + 1)
                    a = nc.scalar.activation(tmp[s][:, :, :] if mode == "silu_gain" else out3(f), a3(s),
                                             ACT.Silu if mode == "silu_gain" else ACT.Relu)
                    a.then_inc(acc_free if mode == "silu_gain" else raw_ready, 1)
                each_tile(act, finish)
            elif mode in ("copy", "gelu", "sigmoid", "silu"):
                act.sem_inc(acc_free, 2)
                func = {"copy": ACT.Copy, "gelu": ACT.Gelu, "sigmoid": ACT.Sigmoid, "silu": ACT.Silu}[mode]

                def finish(f, s, i):
                    act.wait_ge(product_done, f + 3)
                    nc.scalar.activation(out3(f), a3(s), func).then_inc(acc_free, 1)
                each_tile(act, finish)

        @block.vector
        def _(dve):
            if n_params:
                dve.wait_ge(params_ready, n_params)
            if mode == "conv":
                for s in range(2):
                    nc.vector.memset(raw[s][:, 0:halo], 0.0)
                dve.sem_inc(vector_done, 2)

                def finish(f, s, i):
                    dve.wait_ge(acc_free, f + 3)
                    dve.wait_ge(tile_done, f + 1)
                    tap = lambda j: params["taps"][:, j, bass.ds(f, 1)]
                    nc.vector.tensor_scalar(tmp[s][:, :], raw[s][:, 3:3 + live], tap(3), None, ALU.mult).then_inc(step, 1)
                    for n, j in enumerate((2, 1, 0)):
                        dve.wait_ge(step, f * 3 + n + 1)
                        nc.vector.scalar_tensor_tensor(tmp[s][:, :], raw[s][:, j:j + live], tap(j), tmp[s][:, :],
                                                       ALU.mult, ALU.add).then_inc(step if j else vector_done, 1)
                each_tile(dve, finish)
            if mode == "shift":
                for s in range(2):
                    nc.vector.memset(raw[s][:, 0:halo], 0.0)
                nc.vector.tensor_scalar(params["keep"][:, :], params["mu"][:, :], -1.0, 1.0, ALU.mult, ALU.add).then_inc(step, 1)
                dve.wait_ge(step, 1)
                dve.sem_inc(vector_done, 2)

                def finish(f, s, i):
                    dve.wait_ge(acc_free, f + 3)
                    nc.vector.tensor_scalar(tmp[s][:, :], raw[s][:, 0:live], params["mu"][:, bass.ds(f, 1)], None,
                                            ALU.mult).then_inc(step, 1)
                    dve.wait_ge(step, f + 2)
                    nc.vector.scalar_tensor_tensor(out(f), raw[s][:, 1:1 + live], params["keep"][:, bass.ds(f, 1)],
                                                   tmp[s][:, :], ALU.mult, ALU.add).then_inc(vector_done, 1)
                each_tile(dve, finish)
            if mode == "silu_gain":
                dve.sem_inc(vector_done, 2)

                def finish(f, s, i):
                    dve.wait_ge(acc_free, f + 3)
                    nc.vector.tensor_scalar(out3(f), tmp[s][:, :, :], params["gain"][:, bass.ds(f, 1)], None,
                                            ALU.mult).then_inc(vector_done, 1)
                each_tile(dve, finish)
            if mode == "relu2":
                dve.sem_inc(vector_done, 2)
                dve.sem_inc(acc_free, 2)

                def finish(f, s, i):
                    dve.wait_ge(raw_ready, f + 1)
                    nc.vector.tensor_tensor(out3(f), out3(f), a3(s), ALU.mult).then_inc(vector_done, 1)
                    dve.wait_ge(vector_done, f + 3)
                    dve.sem_inc(acc_free, 1)
                each_tile(dve, finish)
            if mode == "add":
                dve.sem_inc(acc_free, 2)

                def finish(f, s, i):
                    dve.wait_ge(product_done, f + 3)
                    nc.vector.tensor_tensor(out3(f), out3(f), a3(s), ALU.add).then_inc(acc_free, 1)
                each_tile(dve, finish)
            if mode == "gate_add":
                dve.sem_inc(acc_free, 2)
                gate = extra["gate"]

                def finish(f, s, i):
                    dve.wait_ge(product_done, f + 3)
                    nc.vector.tensor_tensor(tmp[s][:, :, :], gate[:, f, :].rearrange("p (c n) -> p c n", c=chunks),
                                            a3(s), ALU.mult).then_inc(acc_free, 1)
                    dve.wait_ge(acc_free, f + 3)
                    nc.vector.tensor_tensor(out3(f), out3(f), tmp[s][:, :, :], ALU.add).then_inc(step, 1)
                    dve.wait_ge(step, f + 1)
                each_tile(dve, finish)


def normalise(nc, dram, name, src, src0, gain, chunks, width, dst, add=False, scratch=None):
    with Part(nc, name, dram) as part:
        mats = part.sb("mats", [P, 1, P])
        gains = part.sb("gains", [P, KD])
        square = part.sb("square", [P, 2, KD, width]) if scratch is None else scratch
        scale = part.sb("scale", [P, 2, width])
        total = part.ps("total", [P, 2, 512])
        grown = part.sb("grown", [P, KD, width]) if add else None
        loaded, squared, summed, logged, scaled, out_done, step = (part.sem(n) for n in (
            "loaded", "squared", "summed", "logged", "scaled", "out_done", "step"))
        block = part.stack.enter_context(nc.Block())

        @block.sync
        def _(sp):
            part.load_matrices(sp, mats, ["ones"], loaded)
            sp.dma_start(gains[:, :], gain).then_inc(loaded, 16)

        cols = lambda c: slice(src0 + c * width, src0 + (c + 1) * width)

        @block.scalar
        def _(act):
            nc.scalar.preload_act_table_set("natural_log_exp_and_others")
            def square_of(c):
                if c >= 2:
                    act.wait_ge(summed, c - 1)
                nc.scalar.activation(square[:, c % 2], src[:, :, cols(c)], ACT.Square).then_inc(squared, 1)

            square_of(0)
            for c in range(chunks):
                if c + 1 < chunks:
                    square_of(c + 1)
                act.wait_ge(summed, c + 1)
                if c >= 2:
                    act.wait_ge(out_done, KD * (c - 1))
                nc.scalar.activation(scale[:, c % 2], total[:, c % 2, :width], ACT.Ln, scale=1.0 / D, bias=NORM_EPS).then_inc(logged, 1)
                act.wait_ge(logged, c + 1)
                nc.scalar.activation(scale[:, c % 2], scale[:, c % 2], ACT.Exp, scale=-0.5).then_inc(scaled, 1)

        @block.tensor
        def _(pe):
            pe.wait_ge(loaded, 32)
            for c in range(chunks):
                pe.wait_ge(squared, c + 1)
                if c >= 2:
                    pe.wait_ge(logged, c - 1)
                for k in range(KD):
                    mm = nc.tensor.matmul(total[:, c % 2, :width], mats[:, 0, :], square[:, c % 2, k, :],
                                          start=(k == 0), stop=(k == KD - 1))
                mm.then_inc(summed, 1)

        @block.vector
        def _(dve):
            dve.wait_ge(loaded, 32)
            for c in range(chunks):
                dve.wait_ge(scaled, c + 1)
                for k in range(KD):
                    if add:
                        if c >= 1:
                            dve.wait_ge(out_done, KD * (c - 1) + k + 1)
                        nc.vector.scalar_tensor_tensor(grown[:, k, :], src[:, k, cols(c)], gains[:, k:k + 1],
                                                       scale[:, c % 2], ALU.mult, ALU.mult).then_inc(step, 1)
                        dve.wait_ge(step, KD * c + k + 1)
                        nc.vector.tensor_tensor(dst[:, k, cols(c)], dst[:, k, cols(c)], grown[:, k, :], ALU.add).then_inc(out_done, 1)
                        continue
                    nc.vector.scalar_tensor_tensor(dst[:, k, cols(c)], src[:, k, cols(c)], gains[:, k:k + 1],
                                                   scale[:, c % 2], ALU.mult, ALU.mult).then_inc(out_done, 1)


def entry(nc, dram, frame, rows):
    with Part(nc, "entry", dram) as part:
        ident = part.sb("ident", [P, 1, P])
        cross = part.ps("cross", [P, 4, KD, P])
        loaded, cleared, turned, moved = (part.sem(n) for n in ("loaded", "cleared", "turned", "moved"))
        block = part.stack.enter_context(nc.Block())

        @block.sync
        def _(sp):
            part.load_matrices(sp, ident, ["ident"], loaded)
            sp.wait_ge(cleared, 1)
            sp.dma_start(rows[FRONT:P, 0, :], dram["meta_tokens"][:, :]).then_inc(loaded, 16)
            sp.dma_start(rows[:, 1:, :], dram["x"][0].rearrange("(t p) d -> p t d", p=P)).then_inc(loaded, 16)

        @block.gpsimd
        def _(pool):
            nc.gpsimd.memset(rows[:, 0, :], 0.0).then_inc(cleared, 1)

        @block.tensor
        def _(pe):
            pe.wait_ge(loaded, 48)
            for t in range(NT1):
                if t >= 4:
                    pe.wait_ge(moved, t - 3)
                for k in range(KD):
                    mm = nc.tensor.transpose(cross[:, t % 4, k, :], rows[:, t, k * P:(k + 1) * P], ident[:, 0, :])
                mm.then_inc(turned, 1)

        @block.vector
        def _(dve):
            for t in range(NT1):
                dve.wait_ge(turned, t + 1)
                nc.vector.tensor_copy(frame[:, :, t * P:(t + 1) * P], cross[:, t % 4]).then_inc(moved, 1)


def leave(nc, dram, hidden, out):
    with Part(nc, "leave", dram) as part:
        ident = part.sb("ident", [P, 1, P])
        rows = part.sb("rows", [P, 2, D])
        cross = part.ps("cross", [P, 4, KD, P])
        loaded, turned, moved = (part.sem(n) for n in ("loaded", "turned", "moved"))
        stored = [part.sem(f"stored{s}") for s in range(2)]
        block = part.stack.enter_context(nc.Block())

        @block.sync
        def _(sp):
            part.load_matrices(sp, ident, ["ident"], loaded)
            for t in range(NT):
                sp.wait_ge(moved, t + 1)
                sp.dma_start(out[t * P:(t + 1) * P, :], rows[:, t % 2, :]).then_inc(stored[t % 2], 16)
            for s in range(2):
                sp.wait_ge(stored[s], 16 * (NT // 2))

        @block.tensor
        def _(pe):
            pe.wait_ge(loaded, 16)
            for t in range(NT):
                if t >= 4:
                    pe.wait_ge(moved, t - 3)
                for k in range(KD):
                    mm = nc.tensor.transpose(cross[:, t % 4, k, :], hidden[:, k, t * P:(t + 1) * P], ident[:, 0, :])
                mm.then_inc(turned, 1)

        @block.vector
        def _(dve):
            for t in range(NT):
                dve.wait_ge(turned, t + 1)
                if t >= 2:
                    dve.wait_ge(stored[t % 2], 16 * (t // 2))
                nc.vector.tensor_copy(rows[:, t % 2, :], cross[:, t % 4].rearrange("p k n -> p (k n)")).then_inc(moved, 1)


def over_heads(m, n):
    return m.unsqueeze(1).to_broadcast([m.shape[0], n, m.shape[1]])


def gates(nc, dram, hn, decay, beta, dt):
    HS = H_A + H_C
    with Part(nc, "gates", dram) as part:
        w = part.sb("w", [P, KD, 24])
        real = part.sb("real", [P, 1, P])
        rows = part.sb("rows", [P, 2, HS])
        v, u, w1, d1, eq, lg = (part.sb(n, [P, NT1, HS]) for n in ("v", "u", "w1", "d1", "eq", "lg"))
        e = part.sb("e", [P, NT1, H_A])
        ea = part.sb("ea", [P, HS])
        acc = part.ps("acc", [P, 2, 512])
        raw = acc[:, 0, :NT1 * 24].rearrange("p (t c) -> p t c", c=24)
        loaded, product, biased, absolute, small, plus1, logged, grown, betas, step = (part.sem(n) for n in (
            "loaded", "product", "biased", "absolute", "small", "plus1", "logged", "grown", "betas", "step"))
        block = part.stack.enter_context(nc.Block())
        w_in = dram["w_in"].rearrange("(k p) c -> p k c", p=P)

        @block.sync
        def _(sp):
            with nc.allow_non_contiguous_dma(reason="24 columns of gates"):
                sp.dma_start(w[:, :, 0:6], w_in[:, :, 4 * D_A:4 * D_A + 6]).then_inc(loaded, 16)
                sp.dma_start(w[:, :, 6:18], w_in[:, :, P_A + P_B + P_C - H_C:P_A + P_B + P_C]).then_inc(loaded, 16)
                sp.dma_start(w[:, :, 18:24], w_in[:, :, 4 * D_A + 6:4 * D_A + 12]).then_inc(loaded, 16)
            sp.dma_start(rows[:, 0, :], dram["gate_bias"].to_broadcast([P, HS])).then_inc(loaded, 16)
            sp.dma_start(rows[:, 1, :], dram["gate_log"].to_broadcast([P, HS])).then_inc(loaded, 16)
            part.load_matrices(sp, real, ["real"], loaded)

        @block.tensor
        def _(pe):
            pe.wait_ge(loaded, 96)
            for t in range(NT1):
                for k in range(KD):
                    mm = nc.tensor.matmul(raw[:, t, :], hn[:, k, t * P:(t + 1) * P], w[:, k, :],
                                          start=(k == 0), stop=(k == KD - 1))
            mm.then_inc(product, 1)

        @block.scalar
        def _(act):
            nc.scalar.preload_act_table_set("natural_log_exp_and_others")
            act.wait_ge(loaded, 96)
            nc.scalar.activation(ea[:, :], rows[:, 1, :], ACT.Exp).then_inc(grown, 1)
            act.wait_ge(biased, 1)
            nc.scalar.activation(e[:, :, :], raw[:, :, 18:24], ACT.Exp, scale=-1.0).then_inc(betas, 1)
            nc.scalar.activation(u[:, :, :], v[:, :, :], ACT.Abs).then_inc(absolute, 1)
            act.wait_ge(absolute, 1)
            nc.scalar.activation(u[:, :, :], u[:, :, :], ACT.Exp, scale=-1.0).then_inc(small, 1)
            act.wait_ge(plus1, 1)
            nc.scalar.activation(lg[:, :, :], w1[:, :, :], ACT.Ln).then_inc(logged, 1)

        @block.vector
        def _(dve):
            n = [0]

            def then(i):
                n[0] += 1
                i.then_inc(step, 1)
                dve.wait_ge(step, n[0])
            V = nc.vector
            over = lambda r: over_heads(r, NT1)
            dve.wait_ge(product, 1)
            dve.wait_ge(loaded, 96)
            V.tensor_tensor(v[:, :, :], raw[:, :, 0:HS], over(rows[:, 0, :]), ALU.add).then_inc(biased, 1)
            dve.wait_ge(betas, 1)
            then(V.tensor_scalar(e[:, :, :], e[:, :, :], 1.0, None, ALU.add))
            V.reciprocal(beta[:, :, :], e[:, :, :])
            dve.wait_ge(small, 1)
            V.tensor_scalar(w1[:, :, :], u[:, :, :], 1.0, None, ALU.add).then_inc(plus1, 1)
            dve.wait_ge(plus1, 1)
            then(V.tensor_scalar(d1[:, :, :], w1[:, :, :], -1.0, None, ALU.add))
            then(V.tensor_scalar(eq[:, :, :], d1[:, :, :], 0.0, None, ALU.is_equal))
            then(V.tensor_tensor(d1[:, :, :], d1[:, :, :], eq[:, :, :], ALU.add))
            then(V.reciprocal(d1[:, :, :], d1[:, :, :]))
            dve.wait_ge(logged, 1)
            then(V.tensor_tensor(d1[:, :, :], d1[:, :, :], lg[:, :, :], ALU.mult))
            then(V.tensor_tensor(d1[:, :, :], d1[:, :, :], eq[:, :, :], ALU.add))
            then(V.tensor_tensor(u[:, :, :], u[:, :, :], d1[:, :, :], ALU.mult))
            then(V.scalar_tensor_tensor(v[:, :, :], v[:, :, :], 0.0, u[:, :, :], ALU.max, ALU.add))
            dve.wait_ge(grown, 1)
            V.scalar_tensor_tensor(decay[:, :, :], v[:, :, :], -1.0, over(ea[:, :]), ALU.mult, ALU.mult)
            then(V.tensor_copy(dt[:, :, :], v[:, :, H_A:]))
            V.tensor_scalar(dt[:, 0, :], dt[:, 0, :], real[:, 0, 0:1], None, ALU.mult)


def unit(nc, dram, name, buf, first, n_tiles, matrix, scale, eps=1e-6, times=None, src0=S1, chunks=C1, width=W1):
    live = chunks * width
    with Part(nc, name, dram) as part:
        mats = part.sb("mats", [P, 1, P])
        square = part.sb("square", [P, 2, live])
        root = part.sb("root", [P, 2, chunks, width])
        total = part.ps("total", [P, 2, 4, 512])
        gains = None if isinstance(scale, float) else part.sb("gains", [P, n_tiles])
        loaded, squared, summed, logged, scaled, out_done, step = (part.sem(n) for n in (
            "loaded", "squared", "summed", "logged", "scaled", "out_done", "step"))
        block = part.stack.enter_context(nc.Block())
        tile = lambda f: buf[:, f + first, src0:src0 + live]
        sums = lambda s: total[:, s, :chunks, :width]

        @block.sync
        def _(sp):
            part.load_matrices(sp, mats, [matrix], loaded)
            if gains is not None:
                sp.dma_start(gains[:, :], scale).then_inc(loaded, 16)

        @block.scalar
        def _(act):
            nc.scalar.preload_act_table_set("natural_log_exp_and_others")
            with act.Fori(0, n_tiles // 2) as i:
                for s in range(2):
                    nc.scalar.activation(square[:, s], tile(i * 2 + s), ACT.Square).then_inc(squared, 1)
                for s in range(2):
                    act.wait_ge(summed, i * 2 + s + 1)
                    act.wait_ge(out_done, i * 2 + s + 1)
                    nc.scalar.activation(root[:, s], sums(s), ACT.Ln, bias=eps).then_inc(logged, 1)
                    act.wait_ge(logged, i * 2 + s + 1)
                    nc.scalar.activation(root[:, s], root[:, s], ACT.Exp, scale=-0.5).then_inc(scaled, 1)

        @block.tensor
        def _(pe):
            pe.wait_ge(loaded, 16 if gains is None else 32)
            with pe.Fori(0, n_tiles // 2) as i:
                for s in range(2):
                    pe.wait_ge(squared, i * 2 + s + 1)
                    for c in range(chunks):
                        mm = nc.tensor.matmul(total[:, s, c, :width], mats[:, 0, :], square[:, s, c * width:(c + 1) * width],
                                              start=True, stop=True)
                    mm.then_inc(summed, 1)

        @block.vector
        def _(dve):
            dve.wait_ge(loaded, 16 if gains is None else 32)
            dve.sem_inc(out_done, 2)
            with dve.Fori(0, n_tiles // 2) as i:
                for s in range(2):
                    f = i * 2 + s
                    dve.wait_ge(scaled, f + 1)
                    r = root[:, s].rearrange("p c n -> p (c n)")
                    if times is not None:
                        nc.vector.tensor_tensor(r, r, times[:, f, :], ALU.mult).then_inc(step, 1)
                        dve.wait_ge(step, f + 1)
                    nc.vector.scalar_tensor_tensor(tile(f), tile(f), scale if gains is None else gains[:, bass.ds(f, 1)],
                                                   r, ALU.mult, ALU.mult).then_inc(out_done, 1)


class Inverse:

    LAST = LEVELS - 1

    def __init__(self, nc, part, half, flip, x, x_t, part_x, mat, region):
        self.nc, self.half = nc, half
        self.flip, self.x, self.x_t, self.part_x, self.mat, self.region = flip, x, x_t, part_x, mat, region
        self.start_t, self.product, self.masked, self.joined, self.x_ready, self.xt_ready = (
            part.sem("inv_" + n) for n in ("start_t", "product", "masked", "joined", "x_ready", "xt_ready"))

    @staticmethod
    def count(t, per_tile, step, c):
        return t * (2 * per_tile) + (2 * step + c + 1)

    def tensor(self, pe, t):
        nc, L, n = self.nc, self.LAST, self.count
        for c in range(2):
            pe.wait_ge(self.start_t, n(t, 1, 0, c))
            for i, h in enumerate(self.half(c)):
                mm = nc.tensor.transpose(self.region(2, c)[:, i, :], self.x_t[:, h, :], self.mat("ident"))
            mm.then_inc(self.joined, 1)
        for l in range(1, LEVELS):
            for c in range(2):
                pe.wait_ge(self.x_ready, n(t, L, l - 1, c))
                for i, h in enumerate(self.half(c)):
                    mm = nc.tensor.matmul(self.region(1, c)[:, i, :], self.flip[:, h, :], self.x[:, h, :], start=True, stop=True)
                mm.then_inc(self.product, 1)
            for c in range(2):
                pe.wait_ge(self.masked, n(t, L, l - 1, c))
                if l > 1:
                    pe.wait_ge(self.xt_ready, n(t, L, l - 2, c))
                for i, h in enumerate(self.half(c)):
                    if l < L:
                        nc.tensor.matmul(self.region(2, c)[:, i, :], self.x_t[:, h, :], self.part_x[:, h, :], start=True, stop=True)
                    mm = nc.tensor.matmul(self.region(3, c)[:, i, :], self.part_x[:, h, :], self.x_t[:, h, :], start=True, stop=True)
                mm.then_inc(self.joined, 1)

    def scalar(self, act, t):
        for l in range(LEVELS - 1):
            for c in range(2):
                act.wait_ge(self.joined, self.count(t, LEVELS, l, c))
                h = self.half(c)
                self.nc.scalar.activation(self.x[:, h[0]:h[-1] + 1, :], self.region(2, c), ACT.Copy).then_inc(self.x_ready, 1)

    def vector(self, dve, t, meanwhile=None):
        V, L = self.nc.vector, self.LAST
        for c in range(2):
            h = slice(self.half(c)[0], self.half(c)[-1] + 1)
            V.tensor_tensor(self.x_t[:, h, :], self.flip[:, h, :], over_heads(self.mat("join0T"), len(self.half(c))), ALU.mult).then_inc(self.start_t, 1)
        if meanwhile:
            meanwhile()
        for l in range(1, LEVELS):
            for c in range(2):
                h = slice(self.half(c)[0], self.half(c)[-1] + 1)
                dve.wait_ge(self.product, self.count(t, L, l - 1, c))
                V.tensor_tensor(self.part_x[:, h, :], self.region(1, c), over_heads(self.mat(f"join{l}"), len(self.half(c))), ALU.mult).then_inc(self.masked, 1)
            for c in range(2):
                h = slice(self.half(c)[0], self.half(c)[-1] + 1)
                dve.wait_ge(self.joined, self.count(t, LEVELS, l, c))
                V.tensor_copy(self.x_t[:, h, :], self.region(3, c)).then_inc(self.xt_ready, 1)


def delta_rule(nc, dram, act_a, decay, beta):
    H, HH = H_A, H_A // 2
    with Part(nc, "delta", dram) as part:
        names = ["ident", "ones", "upto", "after", "neg_before", "join0T"] + [f"join{l}" for l in range(1, LEVELS)]
        mt = part.sb("mats", [P, len(names), P])
        mat = lambda n: mt[:, names.index(n), :]
        over = lambda n: over_heads(mat(n), HH)
        head = lambda n: part.sb(n, [P, H, P])
        stage = part.sb("stage", [P, 3 * H, P])
        q, k, v = (stage[:, i * H:(i + 1) * H, :] for i in range(3))
        state = head("state")
        gm, dec, eg, pt, dn, flip, x, xt, px, kt, vt = (head(n) for n in (
            "gm", "dec", "eg", "pt", "dn", "flip", "x", "xt", "px", "kt", "vt"))
        gs = part.sb("gs", [P, 2, 3, HH])
        vn, qd = gm, eg
        R = [part.ps(f"r{i}", [P, 8, P]) for i in range(4)]
        r = lambda i, c: R[i][:, 4 * c:4 * c + HH, :]
        small = lambda c: R[0][:, 4 * c + HH, 0:3 * HH].rearrange("p (a h) -> p a h", a=3)
        half = lambda c: range(HH * c, HH * c + HH)
        sl = lambda c: slice(HH * c, HH * c + HH)
        S = {n: part.sem(n) for n in (
            "loaded", "staged", "decays_spread", "segments", "exps", "keys", "flip_ready", "turned", "kt_done",
            "vt_done", "ks", "rhs", "fresh", "fresh_read", "outputs", "grown", "state_done", "d")}
        inv = Inverse(nc, part, half, flip, x, xt, px, mat, r)
        block = part.stack.enter_context(nc.Block())

        def nth(t, c):
            return t * 2 + (c + 1)

        @block.sync
        def _(sp):
            part.load_matrices(sp, mt, names, S["loaded"])
            sp.dma_start(stage[:, :, :], act_a[:, 0:3 * H, 0:P]).then_inc(S["staged"], 16)
            with sp.Fori(1, NT1) as t:
                sp.wait_ge(S["ks"], t * 2)
                sp.dma_start(stage[:, :, :], act_a[:, 0:3 * H, bass.ts(t, P)]).then_inc(S["staged"], 16)

        @block.tensor
        def _(pe):
            M = nc.tensor.matmul
            pe.wait_ge(S["loaded"], 16 * len(names))
            with pe.Fori(0, NT1) as t:
                for c in range(2):
                    pe.wait_ge(S["decays_spread"], nth(t, c))
                    for i, m in ((0, "after"), (1, "ones")):
                        M(r(i, c), mat(m), gm[:, sl(c), :], start=True, stop=True)
                    for i, m in enumerate(("upto", "ones", "after")):
                        mm = M(small(c)[:, i, :], mat(m), decay[:, bass.ds(t, 1), sl(c)].rearrange("p a h -> p (a h)"), start=True, stop=True)
                    mm.then_inc(S["segments"], 1)
                pe.wait_ge(S["staged"], t * 16 + 16)
                for c in range(2):
                    for i, h in enumerate(half(c)):
                        M(r(2, c)[:, i, :], k[:, h, :], k[:, h, :], start=True, stop=True)
                        mm = M(r(3, c)[:, i, :], k[:, h, :], q[:, h, :], start=True, stop=True)
                    mm.then_inc(S["keys"], 1)
                for c in range(2):
                    pe.wait_ge(S["exps"], t * 6 + 3 * c + 3)
                    for i, h in enumerate(half(c)):
                        nc.tensor.transpose(r(0, c)[:, i, :], k[:, h, :], mat("ident"))
                        mm = nc.tensor.transpose(r(1, c)[:, i, :], v[:, h, :], mat("ident"))
                    mm.then_inc(S["turned"], 1)
                for c in range(2):
                    pe.wait_ge(S["vt_done"], nth(t, c))
                    pe.wait_ge(S["flip_ready"], nth(t, c))
                inv.tensor(pe, t)
                for c in range(2):
                    pe.wait_ge(S["kt_done"], nth(t, c))
                    for i, h in enumerate(half(c)):
                        mm = M(r(0, c)[:, i, :], k[:, h, :], state[:, h, :], start=True, stop=True)
                    mm.then_inc(S["ks"], 1)
                for c in range(2):
                    pe.wait_ge(S["rhs"], nth(t, c))
                    pe.wait_ge(inv.xt_ready, inv.count(t, 6, 5, c))
                    for i, h in enumerate(half(c)):
                        mm = M(r(1, c)[:, i, :], xt[:, h, :], px[:, h, :], start=True, stop=True)
                    mm.then_inc(S["fresh"], 1)
                for c in range(2):
                    pe.wait_ge(S["fresh_read"], nth(t, c))
                    for i, h in enumerate(half(c)):
                        mm = M(r(2, c)[:, i, :], kt[:, h, :], vn[:, h, :], start=True, stop=True)
                    mm.then_inc(S["grown"], 1)
                    for i, h in enumerate(half(c)):
                        M(r(0, c)[:, i, :], vn[:, h, :], pt[:, h, :], start=True, stop=False)
                        mm = M(r(0, c)[:, i, :], state[:, h, :], qd[:, h, :], start=False, stop=True)
                    mm.then_inc(S["outputs"], 1)

        @block.scalar
        def _(act):
            A = nc.scalar.activation
            nc.scalar.preload_act_table_set("natural_log_exp_and_others")
            with act.Fori(0, NT1) as t:
                for c in range(2):
                    act.wait_ge(S["segments"], nth(t, c))
                    A(dec[:, sl(c), :], r(0, c), ACT.Exp).then_inc(S["exps"], 1)
                    A(gs[:, c, :, :], small(c), ACT.Exp).then_inc(S["exps"], 1)
                    A(eg[:, sl(c), :], r(1, c), ACT.Exp).then_inc(S["exps"], 1)
                for c in range(2):
                    act.wait_ge(S["turned"], nth(t, c))
                    A(vt[:, sl(c), :], r(1, c), ACT.Copy).then_inc(S["vt_done"], 1)
                inv.scalar(act, t)
                for c in range(2):
                    act.wait_ge(S["outputs"], nth(t, c))
                    A(act_a[:, sl(c), bass.ts(t, P)], r(0, c), ACT.Copy).then_inc(S["state_done"], 1)

        @block.vector
        def _(dve):
            V, T = nc.vector, nc.vector.tensor_tensor
            V.memset(state[:, :, :], 0.0).then_inc(S["state_done"], 2)
            dve.wait_ge(S["state_done"], 2)
            dve.wait_ge(S["loaded"], 16 * len(names))
            K = 12
            with dve.Fori(0, NT1) as t:
                n = [0]

                def then(i):
                    n[0] += 1
                    i.then_inc(S["d"], 1)
                    dve.wait_ge(S["d"], t * K + n[0])
                per_head = lambda a: spread(a, P)
                beta_h = lambda c: per_head(beta[:, bass.ds(t, 1), sl(c)].rearrange("p a h -> p (a h)"))
                decay_h = lambda c: per_head(decay[:, bass.ds(t, 1), sl(c)].rearrange("p a h -> p (a h)"))
                for c in range(2):
                    dve.wait_ge(S["state_done"], nth(t, c))
                    T(gm[:, sl(c), :], over("upto"), decay_h(c), ALU.mult).then_inc(S["decays_spread"], 1)
                for c in range(2):
                    a = sl(c)
                    dve.wait_ge(S["exps"], t * 6 + 3 * c + 3)
                    T(dn[:, a, :], dec[:, a, :], over("neg_before"), ALU.mult)
                    then(T(dec[:, a, :], dec[:, a, :], over("upto"), ALU.mult))
                    then(T(dn[:, a, :], dn[:, a, :], beta_h(c), ALU.mult))
                    dve.wait_ge(S["keys"], nth(t, c))
                    T(pt[:, a, :], r(3, c), dec[:, a, :], ALU.mult)
                    then(T(flip[:, a, :], r(2, c), dn[:, a, :], ALU.mult))
                    T(qd[:, a, :], q[:, a, :], eg[:, a, :], ALU.mult)
                    T(flip[:, a, :], flip[:, a, :], over("ident"), ALU.add).then_inc(S["flip_ready"], 1)
                    dve.wait_ge(S["flip_ready"], nth(t, c))
                inv.vector(dve, t, lambda: [
                    (dve.wait_ge(S["turned"], nth(t, c)),
                     T(kt[:, sl(c), :], r(0, c), per_head(gs[:, c, 2, :]), ALU.mult).then_inc(S["kt_done"], 1)) for c in range(2)])
                for c in range(2):
                    dve.wait_ge(S["ks"], nth(t, c))
                    then(T(px[:, sl(c), :], r(0, c), per_head(gs[:, c, 0, :]), ALU.mult))
                    T(px[:, sl(c), :], vt[:, sl(c), :], px[:, sl(c), :], ALU.subtract).then_inc(S["rhs"], 1)
                for c in range(2):
                    dve.wait_ge(S["fresh"], nth(t, c))
                    T(vn[:, sl(c), :], r(1, c), beta_h(c), ALU.mult).then_inc(S["fresh_read"], 1)
                for c in range(2):
                    a = sl(c)
                    dve.wait_ge(S["outputs"], nth(t, c))
                    then(T(state[:, a, :], state[:, a, :], per_head(gs[:, c, 1, :]), ALU.mult))
                    then(T(state[:, a, :], state[:, a, :], r(2, c), ALU.add))
                assert n[0] == K, n[0]


def rwkv_prepare(nc, dram, b, rate, unit_k):
    F = 4
    with Part(nc, "rwprep", dram) as part:
        a2 = part.sb("a2", [P, D_B])
        w2 = part.sb("w2", [64, D_B])
        w0 = part.sb("w0", [1, D_B])
        mt = part.sb("mats", [P, 1, P])
        par = part.sb("par", [P, 4, F])
        mixk = part.sb("mixk", [P, 2, LIVE])
        lw = part.sb("lw", [P, 2, D_B])
        acc = [part.ps(f"acc{s}", [P, C1, 512]) for s in range(2)]
        dec = part.ps("dec", [P, 2, 512])
        loaded, squashed, product, rate_done, dec_done, dec_read, scaled, stored, mixed, used, step = (part.sem(n) for n in (
            "loaded", "squashed", "product", "rate_done", "dec_done", "dec_read", "scaled", "stored", "mixed", "used", "step"))
        stored = [stored, mixed]
        block = part.stack.enter_context(nc.Block())

        @block.sync
        def _(sp):
            sp.dma_start(a2[64:128, :], dram["rw_a2"][:, :]).then_inc(loaded, 16)
            sp.dma_start(w2[:, :], dram["rw_w2"][:, :]).then_inc(loaded, 16)
            sp.dma_start(w0[:, :], dram["rw_w0"][:, :]).then_inc(loaded, 16)
            for i, n in enumerate(("rw_a0", "rw_k_k", "rw_k_a")):
                sp.dma_start(par[:, i, :], dram[n]).then_inc(loaded, 16)
            part.load_matrices(sp, mt, ["ones"], loaded)
            for t in range(NT1):
                sp.wait_ge(scaled, t + 1)
                sp.dma_start(dram["log_w"][t * P:(t + 1) * P, :], lw[:, t % 2, :]).then_inc(stored[t % 2], 16)
            sp.wait_ge(stored[0], 16 * ((NT1 + 1) // 2))
            sp.wait_ge(stored[1], 16 * (NT1 // 2))

        @block.scalar
        def _(act):
            A = nc.scalar.activation
            act.wait_ge(loaded, 112)
            A(b[0:64, 16, :], b[0:64, 16, :], ACT.Tanh).then_inc(squashed, 1)
            for f in range(F):
                act.wait_ge(product, f + 1)
                A(rate[:, f, S1:].rearrange("p (c n) -> p c n", c=C1), acc[f % 2][:, :, :W1], ACT.Sigmoid,
                  bias=par[:, 0, f:f + 1]).then_inc(rate_done, 1)
            for t in range(NT1):
                act.wait_ge(dec_done, t + 1)
                if t >= 2:
                    act.wait_ge(stored[t % 2], 16 * (t // 2))
                A(lw[:, t % 2, :], dec[:, t % 2, :], ACT.Sigmoid).then_inc(dec_read, 1)
                act.wait_ge(dec_read, t + 1)
                A(lw[:, t % 2, :], lw[:, t % 2, :], ACT.Copy, scale=-math.exp(-0.5)).then_inc(scaled, 1)
            A(b[:, 12:16, :], b[:, 12:16, :], ACT.Silu)

        @block.tensor
        def _(pe):
            M = nc.tensor.matmul
            pe.wait_ge(loaded, 112)
            for f in range(F):
                if f >= 2:
                    pe.wait_ge(rate_done, f - 1)
                for c in range(C1):
                    mm = M(acc[f % 2][:, c, :W1], a2[64:128, f * P:(f + 1) * P],
                           b[64:128, 16, S1 + c * W1:S1 + (c + 1) * W1], start=True, stop=True)
                mm.then_inc(product, 1)
            pe.wait_ge(squashed, 1)
            for t in range(NT1):
                if t >= 2:
                    pe.wait_ge(dec_read, t - 1)
                M(dec[:, t % 2, :], b[0:64, 16, t * P:(t + 1) * P], w2[:, :], start=True, stop=False)
                M(dec[:, t % 2, :], mt[0:1, 0, :], w0[:, :], start=False, stop=True).then_inc(dec_done, 1)

        @block.vector
        def _(dve):
            V = nc.vector
            dve.wait_ge(loaded, 112)
            V.tensor_scalar(par[:, 3, :], par[:, 2, :], -1.0, 1.0, ALU.mult, ALU.add).then_inc(step, 1)
            dve.wait_ge(step, 1)
            for f in range(F):
                dve.wait_ge(rate_done, f + 1)
                V.tensor_scalar(unit_k[:, f, S1:], b[:, 4 + f, S1:], par[:, 1, f:f + 1], None, ALU.mult)
                V.tensor_scalar(mixk[:, f % 2, :], rate[:, f, S1:], par[:, 2, f:f + 1], par[:, 3, f:f + 1],
                                ALU.mult, ALU.add).then_inc(step, 1)
                dve.wait_ge(step, 2 * f + 2)
                V.tensor_tensor(b[:, 4 + f, S1:], b[:, 4 + f, S1:], mixk[:, f % 2, :], ALU.mult).then_inc(step, 1)
                dve.wait_ge(step, 2 * f + 3)


def rwkv(nc, dram, b, rate, unit_k):
    H, F = H_B, 4
    BIG = 1e38
    with Part(nc, "rwkv", dram) as part:
        names = ["ident", "upto_mid", "before_mid", "mid", "upto", "before", "join0T"] + \
                [f"join{l}" for l in range(1, LEVELS)]
        mt = part.sb("mats", [P, len(names), P])
        mat = lambda n: mt[:, names.index(n), :]
        over = lambda n: over_heads(mat(n), H // 2)
        lw, vst, bt, kt, e1, e2, e3 = (part.sb(n, [P, F, P]) for n in (
            "lw", "vst", "bt", "kt", "e1", "e2", "e3"))
        rz, az = (part.sb(n, [P, F, 2, P]) for n in ("rz", "az"))
        flip, x, xt, px, ak, pb, pk = (part.sb(n, [P, H, P]) for n in ("flip", "x", "xt", "px", "ak", "pb", "pk"))
        tok = part.sb("tok", [P, 3, F, P])
        em = part.sb("em", [P, F])
        state, hm = (part.sb(n, [P, F, 64]) for n in ("state", "hm"))
        rhs, u = e2, e3
        heads = lambda a: a.rearrange("p f (e c) -> p (f e) c", e=2)
        R = [part.ps(f"r{i}", [P, 8, P]) for i in range(4)]
        r = lambda i, c: R[i][:, 4 * c:4 * c + 4, :]
        half = lambda c: range(4 * c, 4 * c + 4)
        hs = lambda c: slice(4 * c, 4 * c + 4)
        pairs = lambda c: range(2 * c, 2 * c + 2)
        fs = lambda c: slice(2 * c, 2 * c + 2)
        S = {n: part.sem(n) for n in (
            "loaded", "staged", "start", "decays", "exps", "scaled_in", "scores", "scores_read",
            "turned", "tokens", "hm_done", "rhs_done", "rhs_read", "u_done", "u_read", "outputs",
            "grown", "stored", "state_done", "d")}
        inv = Inverse(nc, part, half, flip, x, xt, px, mat, r)
        block = part.stack.enter_context(nc.Block())

        def nth(t, c):
            return t * 2 + (c + 1)

        def stage(sp, t):
            sp.dma_start(lw[:, :, :].rearrange("p f c -> p (f c)"), dram["log_w"][bass.ts(t, P), :]).then_inc(S["staged"], 16)
            sp.dma_start(vst[:, :, :], b[:, 8:12, bass.ts(t, P)]).then_inc(S["staged"], 16)

        @block.sync
        def _(sp):
            part.load_matrices(sp, mt, names, S["loaded"])
            stage(sp, 0)
            with sp.Fori(1, NT1) as t:
                sp.wait_ge(S["turned"], t * 2)
                stage(sp, t)

        @block.tensor
        def _(pe):
            M = nc.tensor.matmul
            pe.wait_ge(S["loaded"], 16 * len(names))
            with pe.Fori(0, NT1) as t:
                pe.wait_ge(S["staged"], t * 32 + 32)
                for c in range(2):
                    pe.wait_ge(S["state_done"], nth(t, c))
                    for i, f in enumerate(pairs(c)):
                        M(r(0, c)[:, i, :], lw[:, f, :], mat("upto_mid"), start=True, stop=True)
                        M(r(0, c)[:, 2 + i, :], lw[:, f, :], mat("before_mid"), start=True, stop=True)
                        mm = M(r(1, c)[:, 0, i:i + 1], lw[:, f, :], mat("mid")[:, 0:1], start=True, stop=True)
                    mm.then_inc(S["decays"], 1)
                for c in range(2):
                    pe.wait_ge(S["scaled_in"], nth(t, c))
                    for p, f in enumerate(pairs(c)):
                        for i, (l, right) in enumerate(((bt, az), (kt, az), (bt, rz), (kt, rz))):
                            mm = M(r(i, c)[:, 2 * p:2 * p + 2, :], l[:, f, :], right[:, f, :, :], start=True, stop=True)
                    mm.then_inc(S["scores"], 1)
                for c in range(2):
                    pe.wait_ge(S["scores_read"], nth(t, c))
                    for i, f in enumerate(pairs(c)):
                        nc.tensor.transpose(r(0, c)[:, i, :], vst[:, f, :], mat("ident"))
                        nc.tensor.transpose(r(0, c)[:, 2 + i, :], bt[:, f, :], mat("ident"))
                        mm = nc.tensor.transpose(r(1, c)[:, i, :], kt[:, f, :], mat("ident"))
                    mm.then_inc(S["turned"], 1)
                for c in range(2):
                    pe.wait_ge(S["tokens"], t * 4 + (2 * c + 2))
                inv.tensor(pe, t)
                for c in range(2):
                    pe.wait_ge(S["hm_done"], nth(t, c))
                    out = heads(r(0, c)[:, 0:2, :])
                    for i, h in enumerate(half(c)):
                        M(out[:, i, :], az[:, h // 2, h % 2, :], hm[:, h // 2, :], start=True, stop=False)
                        mm = M(out[:, i, :], ak[:, h, :], heads(tok[:, 0])[:, h, :], start=False, stop=True)
                    mm.then_inc(S["rhs_done"], 1)
                for c in range(2):
                    pe.wait_ge(S["rhs_read"], nth(t, c))
                    pe.wait_ge(inv.xt_ready, inv.count(t, 6, 5, c))
                    out = heads(r(1, c)[:, 0:2, :])
                    for i, h in enumerate(half(c)):
                        mm = M(out[:, i, :], xt[:, h, :], heads(rhs[:, :, :])[:, h, :], start=True, stop=True)
                    mm.then_inc(S["u_done"], 1)
                for c in range(2):
                    pe.wait_ge(S["u_read"], nth(t, c))
                    for i, f in enumerate(pairs(c)):
                        M(r(3, c)[:, i, :], tok[:, 1, f, :], u[:, f, :], start=True, stop=False)
                        mm = M(r(3, c)[:, i, :], tok[:, 2, f, :], tok[:, 0, f, :], start=False, stop=True)
                    mm.then_inc(S["grown"], 1)
                    for i, h in enumerate(half(c)):
                        o = r(2, c)[(h % 2) * 64:(h % 2) * 64 + 64, i // 2, :]
                        M(o, heads(u[:, :, :])[:, h, :], pb[:, h, :], start=True, stop=False)
                        M(o, heads(tok[:, 0])[:, h, :], pk[:, h, :], start=False, stop=False)
                        mm = M(o, hm[:, h // 2, :], rz[:, h // 2, h % 2, :], start=False, stop=True)
                    mm.then_inc(S["outputs"], 1)

        @block.scalar
        def _(act):
            nc.scalar.preload_act_table_set("natural_log_exp_and_others")
            A = nc.scalar.activation
            with act.Fori(0, NT1) as t:
                for c in range(2):
                    act.wait_ge(S["decays"], nth(t, c))
                    A(e1[:, fs(c), :], r(0, c)[:, 0:2, :], ACT.Exp).then_inc(S["exps"], 1)
                    A(e3[:, fs(c), :], r(0, c)[:, 0:2, :], ACT.Exp, scale=-1.0).then_inc(S["exps"], 1)
                    A(e2[:, fs(c), :], r(0, c)[:, 2:4, :], ACT.Exp).then_inc(S["exps"], 1)
                    A(em[:, fs(c)], r(1, c)[:, 0, 0:2], ACT.Exp).then_inc(S["exps"], 1)
                for c in range(2):
                    act.wait_ge(S["turned"], nth(t, c))
                    A(tok[:, 0:2, fs(c), :], r(0, c).rearrange("p (a f) c -> p a f c", a=2), ACT.Copy).then_inc(S["tokens"], 1)
                    A(tok[:, 2, fs(c), :], r(1, c)[:, 0:2, :], ACT.Copy).then_inc(S["tokens"], 1)
                inv.scalar(act, t)
                for c in range(2):
                    act.wait_ge(S["rhs_done"], nth(t, c))
                    A(rhs[:, fs(c), :], r(0, c)[:, 0:2, :], ACT.Copy).then_inc(S["rhs_read"], 1)
                for c in range(2):
                    act.wait_ge(S["u_done"], nth(t, c))
                    A(u[:, fs(c), :], r(1, c)[:, 0:2, :], ACT.Copy).then_inc(S["u_read"], 1)
                for c in range(2):
                    act.wait_ge(S["outputs"], nth(t, c))
                    act.wait_ge(S["state_done"], nth(t, c) + 2)
                    A(unit_k[:, fs(c), bass.ts(t, P)], r(2, c)[:, 0:2, :], ACT.Copy).then_inc(S["stored"], 1)

        @block.vector
        def _(dve):
            V, T, STT = nc.vector, nc.vector.tensor_tensor, nc.vector.scalar_tensor_tensor
            K = 12
            V.memset(rz[:, :, :, :], 0.0)
            V.memset(az[:, :, :, :], 0.0)
            V.memset(state[:, :, :], 0.0).then_inc(S["state_done"], 2)
            dve.wait_ge(S["state_done"], 2)
            dve.wait_ge(S["loaded"], 16 * len(names))
            with dve.Fori(0, NT1) as t:
                n = [0]

                def then(i):
                    n[0] += 1
                    i.then_inc(S["d"], 1)
                    dve.wait_ge(S["d"], t * K + n[0])
                at = bass.ts(t, P)
                for c in range(2):
                    a, k2 = fs(c), b[:, 4 + 2 * c:6 + 2 * c, at]
                    dve.wait_ge(S["exps"], t * 8 + (4 * c + 4))
                    T(bt[:, a, :], unit_k[:, a, at], e3[:, a, :], ALU.mult).then_inc(S["d"], 1)
                    n[0] += 1
                    for e in range(2):
                        part_e = slice(64 * e, 64 * e + 64)
                        T(rz[part_e, a, e, :], b[part_e, fs(c), at], e1[part_e, a, :], ALU.mult)
                        STT(az[part_e, a, e, :], unit_k[part_e, a, at], -1.0, e2[part_e, a, :], ALU.mult, ALU.mult)
                    dve.wait_ge(S["d"], t * K + n[0])
                    T(kt[:, a, :], k2, e3[:, a, :], ALU.mult)
                    T(bt[:, a, :], bt[:, a, :], rate[:, a, at], ALU.mult).then_inc(S["scaled_in"], 1)
                    T(hm[:, a, :], state[:, a, :], spread(em[:, a], 64), ALU.mult).then_inc(S["hm_done"], 1)
                for c in range(2):
                    a = hs(c)
                    dve.wait_ge(S["scores"], nth(t, c))
                    then(STT(flip[:, a, :], r(0, c), BIG, over("before"), ALU.min, ALU.mult))
                    then(T(flip[:, a, :], flip[:, a, :], over("ident"), ALU.add))
                    STT(ak[:, a, :], r(1, c), BIG, over("before"), ALU.min, ALU.mult)
                    STT(pb[:, a, :], r(2, c), BIG, over("upto"), ALU.min, ALU.mult)
                    STT(pk[:, a, :], r(3, c), BIG, over("upto"), ALU.min, ALU.mult).then_inc(S["scores_read"], 1)
                dve.wait_ge(S["scores_read"], t * 2 + 2)
                inv.vector(dve, t)
                for c in range(2):
                    a = fs(c)
                    dve.wait_ge(S["grown"], nth(t, c))
                    for e in range(2):
                        part_e = slice(64 * e, 64 * e + 64)
                        then(T(state[part_e, a, :], hm[part_e, a, :], r(3, c)[part_e, 0:2, part_e], ALU.add))
                    T(state[:, a, :], state[:, a, :], e1[:, a, P - 1:P].to_broadcast([P, 2, 64]), ALU.mult).then_inc(S["d"], 1)
                    n[0] += 1
                    dve.wait_ge(S["d"], t * K + n[0])
                    dve.sem_inc(S["state_done"], 1)
                assert n[0] == K, n[0]


def rwkv_finish(nc, dram, b, out):
    F = 4
    with Part(nc, "rwend", dram) as part:
        names = ["head_mean", "head_ones"]
        mt = part.sb("mats", [P, 2, P])
        par = part.sb("par", [P, 3, F])
        rk, sq = (part.sb(n, [P, 2, LIVE]) for n in ("rk", "sq"))
        ps = [part.ps(f"ps{s}", [P, C1, 512]) for s in range(2)]
        cut = lambda a: a.rearrange("p (c n) -> p c n", c=C1)
        loaded, products, means, bonuses, bonus_used, centred, squared, sums, logged, roots, d, stored = (part.sem(n) for n in (
            "loaded", "products", "means", "bonuses", "bonus_used", "centred", "squared", "sums", "logged", "roots", "d", "stored"))
        block = part.stack.enter_context(nc.Block())
        tile = lambda a, f: a[:, f, S1:]

        @block.sync
        def _(sp):
            part.load_matrices(sp, mt, names, loaded)
            for i, n in enumerate(("rw_r_k", "rw_ln_w", "rw_ln_b")):
                sp.dma_start(par[:, i, :], dram[n]).then_inc(loaded, 16)

        @block.tensor
        def _(pe):
            def product(m, f, right, sem):
                for c in range(C1):
                    mm = nc.tensor.matmul(ps[f % 2][:, c, :W1], mt[:, m, :], right[:, c * W1:(c + 1) * W1], start=True, stop=True)
                mm.then_inc(sem, 1)
            pe.wait_ge(loaded, 80)
            for f0 in range(0, F, 2):
                for f in (f0, f0 + 1):
                    if f >= 2:
                        pe.wait_ge(logged, f - 1)
                    product(0, f, tile(out, f), means)
                for f in (f0, f0 + 1):
                    pe.wait_ge(products, f + 1)
                    pe.wait_ge(centred, f + 1)
                    product(1, f, rk[:, f % 2, :], bonuses)
                for f in (f0, f0 + 1):
                    pe.wait_ge(squared, f + 1)
                    pe.wait_ge(bonus_used, f + 1)
                    product(0, f, sq[:, f % 2, :], sums)

        @block.scalar
        def _(act):
            nc.scalar.preload_act_table_set("natural_log_exp_and_others")
            A = nc.scalar.activation
            for f0 in range(0, F, 2):
                for f in (f0, f0 + 1):
                    act.wait_ge(centred, f + 1)
                    A(sq[:, f % 2, :], tile(out, f), ACT.Square).then_inc(squared, 1)
                for f in (f0, f0 + 1):
                    act.wait_ge(sums, f + 1)
                    A(cut(sq[:, f % 2, :]), ps[f % 2][:, :, :W1], ACT.Ln, bias=GN_EPS).then_inc(logged, 1)
                    act.wait_ge(logged, f + 1)
                    A(sq[:, f % 2, :], sq[:, f % 2, :], ACT.Exp, scale=-0.5).then_inc(roots, 1)

        @block.vector
        def _(dve):
            T, STT = nc.vector.tensor_tensor, nc.vector.scalar_tensor_tensor
            n = [0]

            def then(i):
                n[0] += 1
                i.then_inc(d, 1)
                dve.wait_ge(d, n[0])
            dve.wait_ge(loaded, 80)
            for f0 in range(0, F, 2):
                for f in (f0, f0 + 1):
                    STT(rk[:, f % 2, :], tile(b, f), par[:, 0, f:f + 1], tile(b, 4 + f), ALU.mult, ALU.mult).then_inc(products, 1)
                for f in (f0, f0 + 1):
                    dve.wait_ge(means, f + 1)
                    T(cut(tile(out, f)), cut(tile(out, f)), ps[f % 2][:, :, :W1], ALU.subtract).then_inc(centred, 1)
                for f in (f0, f0 + 1):
                    dve.wait_ge(bonuses, f + 1)
                    T(cut(rk[:, f % 2, :]), cut(tile(b, 8 + f)), ps[f % 2][:, :, :W1], ALU.mult).then_inc(bonus_used, 1)
                for f in (f0, f0 + 1):
                    o = tile(out, f)
                    dve.wait_ge(roots, f + 1)
                    then(STT(o, o, par[:, 1, f:f + 1], sq[:, f % 2, :], ALU.mult, ALU.mult))
                    dve.wait_ge(bonus_used, f + 1)
                    then(STT(o, o, par[:, 2, f:f + 1], rk[:, f % 2, :], ALU.add, ALU.add))
                    then(T(o, o, tile(b, 12 + f), ALU.mult))


def clear(nc, dram, name, *where):
    with Part(nc, name, dram) as part:
        block = part.stack.enter_context(nc.Block())

        @block.gpsimd
        def _(pool):
            for w in where:
                nc.gpsimd.memset(w, 0.0)


def copy_out(nc, dram, name, to, what):
    with Part(nc, name, dram) as part:
        moved = part.sem("moved")
        block = part.stack.enter_context(nc.Block())

        @block.sync
        def _(sp):
            sp.dma_start(to, what).then_inc(moved, 16)
            sp.wait_ge(moved, 16)


def mamba(nc, dram, c_in, decay, dt):
    H, G, F = H_C, G_C, D_C // P
    with Part(nc, "mamba", dram) as part:
        groups = [f"group{a}{b}" for a in range(3) for b in range(3) if abs(a - b) < 2]
        names = ["ident", "ones", "upto", "after"] + groups
        mt = part.sb("mats", [P, len(names), P])
        mat = lambda n: mt[:, names.index(n), :]
        par = part.sb("par", [P, 2, F])
        stage = part.sb("stage", [P, 14, P])
        xs, bs, cs = stage[:, 0:6, :], stage[:, 6:10, :], stage[:, 10:14, :]
        gm, dec, pt = (part.sb(n, [P, H, P]) for n in ("gm", "dec", "pt"))
        cd = gm
        y, sq, skip, rs = (part.sb(n, [P, F, P]) for n in ("y", "sq", "skip", "rs"))
        xdt, xdd, state = (part.sb(n, [P, H, DH_C]) for n in ("xdt", "xdd", "state"))
        btok = part.sb("btok", [P, G, P])
        gs = part.sb("gs", [P, 2, H])
        bank = [part.ps(f"bank{i}", [P, n, 512]) for i, n in ((0, 3), (3, 2), (5, 2), (7, 1))]
        flat = lambda a: a.rearrange("p b (s c) -> p (b s) c", c=P)
        seg, ys, cb = flat(bank[0]), flat(bank[1]), flat(bank[3])
        small = bank[2][:, 1, 0:2 * H].rearrange("p (a h) -> p a h", a=2)
        grow = bank[2][:, :, :].rearrange("p b (s c) -> p (b s) c", c=256)[:, :, 0:192]
        S = {n: part.sem(n) for n in (
            "loaded", "staged", "stage_used", "turn", "decays_spread", "segments", "exps", "cb_done",
            "dec_read", "turned", "bt_done", "x_done", "ready", "outputs", "grown", "squared", "sums",
            "logs", "roots", "gated", "stored", "d")}
        block = part.stack.enter_context(nc.Block())
        n_loads = 16 * (len(names) + 2)

        @block.sync
        def _(sp):
            part.load_matrices(sp, mt, names, S["loaded"])
            sp.dma_start(par[:, 0, :], dram["mb_D"]).then_inc(S["loaded"], 16)
            sp.dma_start(par[:, 1, :], dram["mb_norm"]).then_inc(S["loaded"], 16)
            with sp.Fori(0, NT1) as t:
                sp.wait_ge(S["stage_used"], t + 1)
                sp.dma_start(stage[:, :, :], c_in[:, 6:20, bass.ts(t, P)]).then_inc(S["staged"], 16)
                sp.wait_ge(S["gated"], t * 2 + 2)
                sp.dma_start(dram["mix"].rearrange("(f p) t -> p f t", p=P)[:, 10:16, bass.ts(t, P)], y[:, :, :]).then_inc(S["stored"], 16)
            sp.wait_ge(S["stored"], 16 * NT1 + 16)

        @block.tensor
        def _(pe):
            M = nc.tensor.matmul
            pe.wait_ge(S["loaded"], n_loads)
            with pe.Fori(0, NT1) as t:
                pe.wait_ge(S["decays_spread"], t + 1)
                for b in range(3):
                    M(seg[:, 4 * b:4 * b + 4, :], mat("after"), gm[:, 4 * b:4 * b + 4, :], start=True, stop=True)
                for b in range(2):
                    M(ys[:, 4 * b:4 * b + 4, :], mat("ones"), gm[:, 4 * b:4 * b + 4, :], start=True, stop=True)
                M(flat(bank[2])[:, 0:4, :], mat("ones"), gm[:, 8:12, :], start=True, stop=True)
                for i, m in enumerate(("ones", "after")):
                    mm = M(small[:, i, :], mat(m), decay[:, bass.ds(t, 1), H_A:].rearrange("p a h -> p (a h)"), start=True, stop=True)
                mm.then_inc(S["segments"], 1)
                pe.wait_ge(S["staged"], t * 16 + 16)
                for g in range(G):
                    mm = M(cb[:, g, :], bs[:, g, :], cs[:, g, :], start=True, stop=True)
                mm.then_inc(S["cb_done"], 1)
                pe.wait_ge(S["exps"], t * 4 + 4)
                for f in range(F):
                    nc.tensor.transpose(seg[:, f, :], xs[:, f, :], mat("ident"))
                for g in range(G):
                    mm = nc.tensor.transpose(seg[:, 8 + g, :], bs[:, g, :], mat("ident"))
                mm.then_inc(S["turned"], 1)
                pe.wait_ge(S["bt_done"], t + 1)
                pe.wait_ge(S["ready"], t + 1)
                for h in range(H):
                    o = ys[(h % 2) * 64:(h % 2) * 64 + 64, h // 2, :]
                    M(o, xdt[:, h, :], pt[:, h, :], start=True, stop=False)
                    mm = M(o, state[:, h, :], cd[:, h, :], start=False, stop=True)
                mm.then_inc(S["outputs"], 1)
                for g in range(G):
                    mm = M(grow[:, g, :], btok[:, g, :], xdd[:, 3 * g:3 * g + 3, :], start=True, stop=True)
                mm.then_inc(S["grown"], 1)
                pe.wait_ge(S["squared"], t + 1)
                for m in range(3):
                    near = [f for f in range(3) if abs(f - m) < 2]
                    for f in near:
                        mm = M(bank[0][:, m, 0:256], mat(f"group{f}{m}"),
                               sq[:, :, :].rearrange("p (a f) c -> p a f c", a=2)[:, :, f, :],
                               start=(f == near[0]), stop=(f == near[-1]))
                mm.then_inc(S["sums"], 1)

        @block.scalar
        def _(act):
            nc.scalar.preload_act_table_set("natural_log_exp_and_others")
            A = nc.scalar.activation
            with act.Fori(0, NT1) as t:
                act.wait_ge(S["segments"], t + 1)
                act.wait_ge(S["turn"], t + 1)
                A(dec[:, :, :], seg, ACT.Exp).then_inc(S["exps"], 1)
                A(cd[:, 0:8, :], ys, ACT.Exp).then_inc(S["exps"], 1)
                A(cd[:, 8:12, :], flat(bank[2])[:, 0:4, :], ACT.Exp).then_inc(S["exps"], 1)
                A(gs[:, :, :], small, ACT.Exp).then_inc(S["exps"], 1)
                act.wait_ge(S["turned"], t + 1)
                A(btok[:, :, :], seg[:, 8:12, :], ACT.Copy).then_inc(S["bt_done"], 1)
                act.wait_ge(S["gated"], t * 2 + 1)
                A(sq[:, :, :], y[:, :, :], ACT.Square).then_inc(S["squared"], 1)
                act.wait_ge(S["sums"], t + 1)
                rs3 = rs[:, :, :].rearrange("p (m a) c -> p m (a c)", m=3)
                A(rs3, bank[0][:, :, 0:256], ACT.Ln, bias=NORM_EPS).then_inc(S["logs"], 1)
                act.wait_ge(S["logs"], t + 1)
                A(rs3, rs3, ACT.Exp, scale=-0.5).then_inc(S["roots"], 1)

        @block.vector
        def _(dve):
            V, T = nc.vector, nc.vector.tensor_tensor
            K = 9
            V.memset(state[:, :, :], 0.0).then_inc(S["turn"], 1)
            dve.sem_inc(S["stage_used"], 1)
            dve.sem_inc(S["stored"], 16)
            dve.wait_ge(S["loaded"], n_loads)
            with dve.Fori(0, NT1) as t:
                n = [0]

                def then(i):
                    n[0] += 1
                    i.then_inc(S["d"], 1)
                    dve.wait_ge(S["d"], t * K + n[0])
                row = lambda a: a.rearrange("p a h -> p (a h)")
                dve.wait_ge(S["turn"], t + 1)
                T(gm[:, :, :], over_heads(mat("upto"), H), spread(row(decay[:, bass.ds(t, 1), H_A:]), P), ALU.mult).then_inc(S["decays_spread"], 1)
                dve.wait_ge(S["staged"], t * 16 + 16)
                T(skip[:, :, :], xs, spread(par[:, 0, :], P), ALU.mult)
                dve.wait_ge(S["exps"], t * 4 + 4)
                then(T(dec[:, :, :], dec[:, :, :], over_heads(mat("upto"), H), ALU.mult))
                grouped = lambda a: a.rearrange("p (g e) c -> p g e c", g=G)
                by_group = lambda a: a.unsqueeze(2).to_broadcast([P, G, H // G, P])
                T(grouped(cd[:, :, :]), grouped(cd[:, :, :]), by_group(cs), ALU.mult)
                dve.wait_ge(S["cb_done"], t + 1)
                T(grouped(pt[:, :, :]), by_group(cb), grouped(dec[:, :, :]), ALU.mult)
                dve.wait_ge(S["turned"], t + 1)
                then(T(xdt[:, :, :], seg[:, 0:6, :].rearrange("p f (e c) -> p (f e) c", e=2), spread(row(dt[:, bass.ds(t, 1), :]), DH_C), ALU.mult))
                then(T(xdd[:, :, :], xdt[:, :, :], spread(gs[:, 1, :], DH_C), ALU.mult))
                dve.sem_inc(S["ready"], 1)
                dve.wait_ge(S["outputs"], t + 1)
                dve.wait_ge(S["stored"], t * 16 + 16)
                then(T(y[:, :, :], ys[:, 0:6, :], skip[:, :, :], ALU.add))
                then(T(y[:, :, :], y[:, :, :], c_in[:, 0:6, bass.ts(t, P)], ALU.mult))
                dve.sem_inc(S["gated"], 1)
                dve.wait_ge(S["grown"], t + 1)
                then(T(state[:, :, :], state[:, :, :], spread(gs[:, 0, :], DH_C), ALU.mult))
                then(T(state[:, :, :].rearrange("p (g e) c -> p g (e c)", g=G), state[:, :, :].rearrange("p (g e) c -> p g (e c)", g=G), grow, ALU.add))
                dve.wait_ge(S["roots"], t + 1)
                turned = y[:, :, :].rearrange("p (a m) c -> p m a c", a=2)
                then(T(turned, turned, rs[:, :, :].rearrange("p (m a) c -> p m a c", m=3), ALU.mult))
                then(T(y[:, :, :], y[:, :, :], spread(par[:, 1, :], P), ALU.mult))
                dve.sem_inc(S["gated"], 1)
                dve.sem_inc(S["stage_used"], 1)
                dve.sem_inc(S["turn"], 1)
                assert n[0] == K, n[0]


W_CONV = 512
HEADS2 = 8
DFF = 4096
EPS = 1e-6


def by_tokens(nc, dram, name, src, weights, col0, n, dst, func):
    with Part(nc, name, dram) as part:
        w = part.sb("w", [P, KD, n])
        acc = part.ps("acc", [P, 4, 512])
        loaded, product, read = (part.sem(x) for x in ("loaded", "product", "read"))
        block = part.stack.enter_context(nc.Block())

        @block.sync
        def _(sp):
            sp.dma_start(w[:, :, :], weights.rearrange("(k p) c -> p k c", p=P)[:, :, col0:col0 + n]).then_inc(loaded, 16)

        @block.tensor
        def _(pe):
            pe.wait_ge(loaded, 16)
            for t in range(NT):
                if t >= 4:
                    pe.wait_ge(read, t - 3)
                for k in range(KD):
                    mm = nc.tensor.matmul(acc[:, t % 4, :n], src[:, k, t * P:(t + 1) * P], w[:, k, :],
                                          start=(k == 0), stop=(k == KD - 1))
                mm.then_inc(product, 1)

        @block.scalar
        def _(act):
            for t in range(NT):
                act.wait_ge(product, t + 1)
                nc.scalar.activation(dst[:, t, :], acc[:, t % 4, :n], func).then_inc(read, 1)


def gated_conv(nc, dram, proj, dst):
    F, N = 4, SEQ
    with Part(nc, "gconv", dram) as part:
        taps = part.sb("taps", [P, 3, F])
        v = part.sb("v", [P, 2, 2 + N])
        loaded, step = part.sem("loaded"), part.sem("step")
        block = part.stack.enter_context(nc.Block())

        @block.sync
        def _(sp):
            sp.dma_start(taps[:, :, :], dram["conv_w_2"]).then_inc(loaded, 16)

        @block.vector
        def _(dve):
            V, n = nc.vector, [0]

            def then(i):
                n[0] += 1
                i.then_inc(step, 1)
                dve.wait_ge(step, n[0])
            dve.wait_ge(loaded, 16)
            then(V.memset(v[:, :, 0:2], 0.0))
            for f in range(F):
                s, out = f % 2, dst[:, f, :]
                then(V.tensor_tensor(v[:, s, 2:], proj[:, 4 + f, :], proj[:, 8 + f, :], ALU.mult))
                then(V.tensor_scalar(out, v[:, s, 2:], taps[:, 2, f:f + 1], None, ALU.mult))
                then(V.scalar_tensor_tensor(out, v[:, s, 1:1 + N], taps[:, 1, f:f + 1], out, ALU.mult, ALU.add))
                then(V.scalar_tensor_tensor(out, v[:, s, 0:N], taps[:, 0, f:f + 1], out, ALU.mult, ALU.add))
                then(V.tensor_tensor(out, out, proj[:, f, :], ALU.mult))


def stick_breaking(nc, dram, qk, v, dst):
    PAIRS, QC = HEADS2 // 2, SEQ // 512
    units = [(qc, kt, e) for qc in range(QC) for kt in range(4 * qc + 3, -1, -1) for e in range(2)]
    U, SL = len(units), 4

    def span(u):
        qc, kt, _ = units[u]
        return max(kt * P - qc * 512, 0), kt >= 4 * qc
    first = lambda u: units[u][1] == 4 * units[u][0] + 3
    last = lambda u: units[u][1] == 0
    runs = lambda u: sum(not last(w) for w in range(u + 1))
    RU = runs(U - 1)
    with Part(nc, "stick", dram) as part:
        names = ["neg_from", "neg_ones", "before", "zeros"]
        mt = part.sb("mats", [P, len(names), P])
        mat = lambda n: mt[:, names.index(n), :]
        k = part.sb("k", [P, SEQ])
        vs = part.sb("vs", [P, NT, P])
        qz = part.sb("qz", [P, 2, SEQ])
        ex, soft, att = (part.sb(n, [P, SL, 512]) for n in ("ex", "soft", "att"))
        run = part.sb("run", [P, 2, 512])
        score = part.ps("score", [P, SL, 512])
        out = part.ps("out", [P, 4, 512])
        S = {n: part.sem(n) for n in (
            "loaded", "staged", "stage_used", "zeroed", "q_ready", "z_done", "absd", "expd", "logd", "soft_done",
            "summed", "weighed", "masked", "run_done", "applied", "out_read", "d")}
        block = part.stack.enter_context(nc.Block())
        n_diag = sum(span(u)[1] for u in range(U))

        @block.sync
        def _(sp):
            part.load_matrices(sp, mt, names, S["loaded"])
            with sp.Fori(0, PAIRS) as i:
                sp.wait_ge(S["stage_used"], i + 1)
                sp.dma_start(k[:, :], qk[:, bass.ds(i + 4, 1), :].rearrange("p a n -> p (a n)")).then_inc(S["staged"], 16)
                sp.dma_start(vs[:, :, :], v[:, :, bass.ts(i, P)]).then_inc(S["staged"], 16)

        @block.tensor
        def _(pe):
            M = nc.tensor.matmul
            pe.wait_ge(S["loaded"], 16 * len(names))
            with pe.Fori(0, PAIRS) as i:
                def scores(u):
                    qc, kt, e = units[u]
                    o, _ = span(u)
                    if u >= SL:
                        pe.wait_ge(S["weighed"], i * U + u - SL + 1)
                    M(score[:, u % SL, o:], k[:, kt * P:(kt + 1) * P], qz[:, e, qc * 512 + o:(qc + 1) * 512],
                      start=True, stop=True).then_inc(S["z_done"], 1)
                pe.wait_ge(S["staged"], i * 32 + 32)
                pe.wait_ge(S["q_ready"], i + 1)
                pe.wait_ge(S["out_read"], i + 1)
                for e in range(2):
                    for qc in range(QC):
                        M(out[64 * e:64 * e + 64, 2 * e + qc, :], mat("zeros")[:, 0:64], qz[:, e, qc * 512:(qc + 1) * 512],
                          start=True, stop=True)
                scores(0)
                scores(1)

                def apply(u):
                    qc, kt, e = units[u]
                    o, _ = span(u)
                    if span(u)[1]:
                        pe.wait_ge(S["masked"], i * n_diag + sum(span(w)[1] for w in range(u + 1)))
                    else:
                        pe.wait_ge(S["weighed"], i * U + u + 1)
                    M(out[64 * e:64 * e + 64, 2 * e + qc, o:], vs[:, kt, 64 * e:64 * e + 64], att[:, u % SL, o:],
                      start=False, stop=True, skip_group_check=True).then_inc(S["applied"], 1)
                for u in range(U):
                    if u + 2 < U:
                        scores(u + 2)
                    o, _ = span(u)
                    pe.wait_ge(S["soft_done"], i * U + u + 1)
                    mm = M(score[:, u % SL, o:], mat("neg_from"), soft[:, u % SL, o:], start=False, stop=True,
                           skip_group_check=True)
                    if not first(u):
                        pe.wait_ge(S["run_done"], i * RU + runs(u - 2))
                        mm = M(score[:, u % SL, o:], mat("neg_ones"), run[:, units[u][2], o:], start=False, stop=True,
                               skip_group_check=True)
                    mm.then_inc(S["summed"], 1)
                    if u >= 1:
                        apply(u - 1)
                apply(U - 1)

        @block.scalar
        def _(act):
            nc.scalar.preload_act_table_set("natural_log_exp_and_others")
            A = nc.scalar.activation
            with act.Fori(0, PAIRS) as i:
                def softplus(u):
                    o, _ = span(u)
                    act.wait_ge(S["z_done"], i * U + u + 1)
                    if u >= SL:
                        act.wait_ge(S["run_done"], i * RU + runs(u - SL))
                        act.wait_ge(S["summed"], i * U + u - SL + 1)
                    A(ex[:, u % SL, o:], score[:, u % SL, o:], ACT.Abs).then_inc(S["absd"], 1)
                    act.wait_ge(S["absd"], i * U + u + 1)
                    A(ex[:, u % SL, o:], ex[:, u % SL, o:], ACT.Exp, scale=-1.0).then_inc(S["expd"], 1)
                    act.wait_ge(S["expd"], i * U + u + 1)
                    A(soft[:, u % SL, o:], ex[:, u % SL, o:], ACT.Ln, bias=1.0).then_inc(S["logd"], 1)

                def weigh(u):
                    o, _ = span(u)
                    act.wait_ge(S["summed"], i * U + u + 1)
                    if u >= SL:
                        act.wait_ge(S["applied"], i * U + u - SL + 1)
                    A(att[:, u % SL, o:], score[:, u % SL, o:], ACT.Exp).then_inc(S["weighed"], 1)
                softplus(0)
                for u in range(U):
                    if u + 1 < U:
                        softplus(u + 1)
                    weigh(u)

        @block.gpsimd
        def _(pool):
            pool.wait_ge(S["loaded"], 16 * len(names))
            with pool.Fori(0, PAIRS) as i:
                for u in range(U):
                    e, (o, _) = units[u][2], span(u)
                    if last(u):
                        continue
                    pool.wait_ge(S["soft_done"], i * U + u + 1)
                    pool.wait_ge(S["summed"], i * U + u + 1)
                    r = run[:, e, :]
                    if first(u):
                        nc.gpsimd.tensor_tensor(r[:, o:], soft[:, u % SL, o:], mat("zeros"), ALU.add)
                        nc.gpsimd.memset(r[:, 0:o], 0.0).then_inc(S["run_done"], 1)
                    else:
                        nc.gpsimd.tensor_tensor(r[:, o:], r[:, o:], soft[:, u % SL, o:], ALU.add).then_inc(S["run_done"], 1)
                    pool.wait_ge(S["run_done"], i * RU + runs(u))

        @block.vector
        def _(dve):
            V, T = nc.vector, nc.vector.tensor_tensor
            V.memset(qz[:, :, :], 0.0).then_inc(S["zeroed"], 1)
            dve.wait_ge(S["zeroed"], 1)
            dve.wait_ge(S["loaded"], 16 * len(names))
            dve.sem_inc(S["stage_used"], 1)
            dve.sem_inc(S["out_read"], 1)
            with dve.Fori(0, PAIRS) as i:
                for e in range(2):
                    half = slice(64 * e, 64 * e + 64)
                    q = V.tensor_scalar(qz[half, e, :], qk[half, bass.ds(i, 1), :].rearrange("p a n -> p (a n)"), 0.125, None, ALU.mult)
                q.then_inc(S["q_ready"], 1)

                def soft_of(u):
                    o, diag = span(u)
                    s = soft[:, u % SL, :]
                    dve.wait_ge(S["logd"], i * U + u + 1)
                    a = V.scalar_tensor_tensor(s[:, o:], score[:, u % SL, o:], 0.0, s[:, o:], ALU.max, ALU.add)
                    if diag:
                        a.then_inc(S["d"], 1)
                        dve.wait_ge(S["d"], i * n_diag + sum(span(w)[1] for w in range(u + 1)))
                        a = T(s[:, o:o + P], s[:, o:o + P], mat("before"), ALU.mult)
                    a.then_inc(S["soft_done"], 1)

                def mask_of(u):
                    o, diag = span(u)
                    if diag:
                        dve.wait_ge(S["weighed"], i * U + u + 1)
                        a = att[:, u % SL, o:o + P]
                        T(a, a, mat("before"), ALU.mult).then_inc(S["masked"], 1)
                soft_of(0)
                for u in range(U):
                    if u + 1 < U:
                        soft_of(u + 1)
                    mask_of(u)
                dve.wait_ge(S["applied"], i * U + U)
                for e in range(2):
                    half = slice(64 * e, 64 * e + 64)
                    c = V.tensor_copy(dst[half, bass.ds(i + 4, 1), :].rearrange("p a (q n) -> p (a q) n", n=512),
                                      out[half, 2 * e:2 * e + 2, :])
                c.then_inc(S["out_read"], 1)
                dve.sem_inc(S["stage_used"], 1)


def turn_rows(nc, dram, name, rows_in, n, dst):
    with Part(nc, name, dram) as part:
        ident = part.sb("ident", [P, 1, P])
        rows = part.sb("rows", [P, NT, n])
        cross = part.ps("cross", [P, 4, n // P, P])
        loaded, turned, moved = (part.sem(x) for x in ("loaded", "turned", "moved"))
        block = part.stack.enter_context(nc.Block())

        @block.sync
        def _(sp):
            part.load_matrices(sp, ident, ["ident"], loaded)
            sp.dma_start(rows[:, :, :], rows_in.rearrange("(t p) d -> p t d", p=P)).then_inc(loaded, 16)

        @block.tensor
        def _(pe):
            pe.wait_ge(loaded, 32)
            for t in range(0, NT):
                if t >= 2:
                    pe.wait_ge(moved, t - 1)
                for k in range(n // P):
                    mm = nc.tensor.transpose(cross[:, 2 * (t % 2), k, :], rows[:, t, k * P:(k + 1) * P], ident[:, 0, :])
                mm.then_inc(turned, 1)

        @block.vector
        def _(dve):
            for t in range(NT):
                dve.wait_ge(turned, t + 1)
                nc.vector.tensor_copy(dst[:, :, t * P:(t + 1) * P], cross[:, 2 * (t % 2)]).then_inc(moved, 1)


def second_block(nc, dram, hid):
    full = dict(src0=0, chunks=C2, width=W2)
    with Part(nc, "s2", dram) as p:
        mix = p.sb("mix", [P, KD, SEQ])
        with Part(nc, "s2a", dram) as a:
            conv = a.sb("conv", [P, 12, SEQ])
            v = a.sb("v", [P, NT, 512])
            m = a.sb("m", [P, KD, SEQ])
            normalise(nc, dram, "n2", hid, 0, dram["g_mix_2"], C2, W2, m)
            project(nc, dram, "p2c", m, 0, dram["w_in_2"], 0, KD, 12, C2, W2, conv, 0, 0, "copy")
            gated_conv(nc, dram, conv, mix)
            unit(nc, dram, "u2c", mix, 0, 4, "head_mean", dram["g_conv_out_2"], **full)
            project(nc, dram, "p2q", m, 0, dram["w_in_2"], 1536, KD, 8, C2, W2, conv, 0, 0, "copy")
            by_tokens(nc, dram, "p2v", m, dram["w_in_2"], 2560, 512, v, ACT.Copy)
            stick_breaking(nc, dram, conv, v, mix)
            unit(nc, dram, "u2a", mix, 4, 4, "head_mean", dram["g_attn_out_2"], **full)
        project(nc, dram, "p2o", mix, 0, dram["w_out_2"], 0, KD, 8, C2, W2, hid, 0, 0, "add")
    feed_forward(nc, dram, "2", hid, dram["g_mlp_2"], dram["w_up_2"], dram["w_down_2"])
    with Part(nc, "s2g", dram) as p:
        gate = p.sb("gate", [P, KD, SEQ])
        m = p.sb("m", [P, KD, SEQ])
        pt = p.sb("pt", [P, 2, SEQ])
        normalise(nc, dram, "n2g", hid, 0, dram["g_ple_2"], C2, W2, m)
        project(nc, dram, "p2g", m, 0, dram["w_ple_gate_2"], 0, KD, 8, C2, W2, gate, 0, 0, "sigmoid")
        turn_rows(nc, dram, "t2", dram["p_2"], 256, pt)
        project(nc, dram, "p2p", pt, 0, dram["w_ple_proj_2"], 0, 2, 8, C2, W2, hid, 0, 0, "gate_add", {"gate": gate})
    normalise(nc, dram, "n2f", hid, 0, dram["g_final_2"], C2, W2, hid)


def feed_forward(nc, dram, n, hid, gain, up, down):
    with Part(nc, "ff" + n, dram) as p:
        inner = p.sb("inner", [P, DFF // P, SEQ])
        with Part(nc, "ffm" + n, dram) as q:
            m = q.sb("m", [P, KD, SEQ])
            squares = inner[:, 0:KD, :].rearrange("p (a x) (y n) -> p a (x y) n", a=2, y=2)
            normalise(nc, dram, "nf" + n, hid, 0, gain, C2, W2, m, scratch=squares)
            project(nc, dram, "up" + n, m, 0, up, 0, KD, DFF // P, C2, W2, inner, 0, 0, "relu2")
        project(nc, dram, "down" + n, inner, 0, down, 0, DFF // P, KD, C2, W2, hid, 0, 0, "add")


def spatial_gate(nc, dram, sv, su, dst):
    G = 4
    with Part(nc, "sgu", dram) as part:
        ident = part.sb("ident", [P, 1, P])
        ws = part.sb("ws", [P, G, P])
        wt = part.sb("wt", [P, G, P])
        bs = part.sb("bs", [P, G, P])
        gain = part.sb("gain", [P, G])
        sq = part.sb("sq", [P, 32, P])
        ss = part.sb("ss", [P, 32])
        acc = part.ps("acc", [P, 4, NT, P])
        loaded, turned, moved, squared, summed, rooted, ready, mixed, read, step = (part.sem(x) for x in (
            "loaded", "turned", "moved", "squared", "summed", "rooted", "ready", "mixed", "read", "step"))
        block = part.stack.enter_context(nc.Block())
        svg = sv[:, :, :].rearrange("p t (g c) -> p (t g) c", g=G)

        @block.sync
        def _(sp):
            part.load_matrices(sp, ident, ["ident"], loaded)
            sp.dma_start(ws[:, :, :], dram["w_s_3"].rearrange("g p q -> p g q")).then_inc(loaded, 16)
            sp.dma_start(bs[:, :, :].rearrange("p g q -> p (g q)"), dram["b_s_3"].to_broadcast([P, 512])).then_inc(loaded, 16)
            sp.dma_start(gain[:, :], dram["sgu_norm_g_3"]).then_inc(loaded, 16)

        @block.tensor
        def _(pe):
            pe.wait_ge(loaded, 64)
            for g in range(G):
                mm = nc.tensor.transpose(acc[:, 0, g, :], ws[:, g, :], ident[:, 0, :])
            mm.then_inc(turned, 1)
            pe.wait_ge(moved, 1)
            pe.wait_ge(ready, 1)
            for g in range(G):
                for t in range(NT):
                    mm = nc.tensor.matmul(acc[:, g, t, :], sv[:, t, g * P:(g + 1) * P], wt[:, g, :], start=True, stop=True)
                mm.then_inc(mixed, 1)

        @block.scalar
        def _(act):
            nc.scalar.preload_act_table_set("natural_log_exp_and_others")
            nc.scalar.activation(sq[:, :, :], svg, ACT.Square).then_inc(squared, 1)
            act.wait_ge(turned, 1)
            nc.scalar.activation(wt[:, :, :], acc[:, 0, 0:4, :], ACT.Copy).then_inc(moved, 1)
            act.wait_ge(summed, 1)
            nc.scalar.activation(ss[:, :], ss[:, :], ACT.Ln, scale=1.0 / P, bias=EPS).then_inc(step, 1)
            act.wait_ge(step, 1)
            nc.scalar.activation(ss[:, :], ss[:, :], ACT.Exp, scale=-0.5).then_inc(rooted, 1)

        @block.vector
        def _(dve):
            V = nc.vector
            dve.wait_ge(squared, 1)
            V.tensor_reduce(ss[:, :], sq[:, :, :], mybir.AxisListType.X, ALU.add).then_inc(summed, 1)
            dve.wait_ge(rooted, 1)
            V.tensor_tensor(svg, svg, spread(ss[:, :], P), ALU.mult).then_inc(ready, 1)
            dve.wait_ge(loaded, 64)
            for g in range(G):
                dve.wait_ge(mixed, g + 1)
                o = dst[:, 4 + g, :].rearrange("p (t c) -> p t c", c=P)
                V.scalar_tensor_tensor(o, acc[:, g], gain[:, g:g + 1], over_heads(bs[:, g, :], NT), ALU.mult, ALU.add).then_inc(read, 1)
                dve.wait_ge(read, g + 1)
                V.tensor_tensor(dst[:, 4 + g, :], dst[:, 4 + g, :], su[:, g, :], ALU.mult)


def gla_decays(nc, dram, low, la):
    C, NCH = 64, SEQ // 64
    with Part(nc, "gdec", dram) as part:
        ones = part.sb("ones", [P, 1, P])
        w2 = part.sb("w2", [32, 512])
        bias = part.sb("bias", [1, 512])
        t = part.sb("t", [C, 2, 512])
        acc = part.ps("acc", [C, 2, 512])
        loaded, zeroed, product, absd, expd, logd, read, done = (part.sem(x) for x in (
            "loaded", "zeroed", "product", "absd", "expd", "logd", "read", "done"))
        block = part.stack.enter_context(nc.Block())

        @block.sync
        def _(sp):
            part.load_matrices(sp, ones, ["ones"], loaded)
            sp.wait_ge(zeroed, 1)
            sp.dma_start(w2[0:16, 0:256], dram["w_a2_fwd_3"]).then_inc(loaded, 16)
            sp.dma_start(w2[16:32, 256:512], dram["w_a2_bwd_3"]).then_inc(loaded, 16)
            sp.dma_start(bias[:, :], dram["b_a_3"]).then_inc(loaded, 16)

        @block.tensor
        def _(pe):
            pe.wait_ge(loaded, 64)
            for c in range(NCH):
                if c >= 2:
                    pe.wait_ge(read, c - 1)
                nc.tensor.matmul(acc[:, c % 2, :], low[0:32, 0, c * C:(c + 1) * C], w2[:, :], start=True, stop=False)
                nc.tensor.matmul(acc[:, c % 2, :], ones[0:1, 0, 0:C], bias[:, :], start=False, stop=True).then_inc(product, 1)

        @block.scalar
        def _(act):
            nc.scalar.preload_act_table_set("natural_log_exp_and_others")
            A = nc.scalar.activation
            for c in range(NCH):
                act.wait_ge(product, c + 1)
                if c >= 2:
                    act.wait_ge(read, c - 1)
                A(t[:, c % 2, :], acc[:, c % 2, :], ACT.Abs).then_inc(absd, 1)
                act.wait_ge(absd, c + 1)
                A(t[:, c % 2, :], t[:, c % 2, :], ACT.Exp, scale=-1.0).then_inc(expd, 1)
                act.wait_ge(expd, c + 1)
                A(t[:, c % 2, :], t[:, c % 2, :], ACT.Ln, bias=1.0).then_inc(logd, 1)

        @block.vector
        def _(dve):
            V = nc.vector
            V.memset(w2[:, :], 0.0).then_inc(zeroed, 1)
            for c in range(NCH):
                dve.wait_ge(logd, c + 1)
                V.scalar_tensor_tensor(la[:, c, :], acc[:, c % 2, :], 0.0, t[:, c % 2, :], ALU.min, ALU.subtract).then_inc(read, 1)
                dve.wait_ge(read, c + 1)
                V.tensor_scalar(la[:, c, :], la[:, c, :], 1.0 / 16.0, None, ALU.mult)


def gla(nc, dram, name, qk, v, la, osum, backward):
    C, H, F = 64, 4, 2
    off = 256 if backward else 0
    with Part(nc, name, dram) as part:
        names = ["ident", "from_mid64" if backward else "upto_mid64", "mid64", "after" if backward else "upto"]
        mt = part.sb("mats", [P, len(names), P])
        shift, mid, keep = mt[0:C, 1, 0:C], mt[0:C, 2, int(backward):int(backward) + 1], mt[0:C, 3, 0:C]
        las = part.sb("las", [C, 256])
        vs = part.sb("vs", [C, 512])
        e1, e3, kt = (part.sb(n, [P, F, C]) for n in ("e1", "e3", "kt"))
        em = part.sb("em", [P, F])
        qz = part.sb("qz", [P, F, 2, C])
        state, sm = (part.sb(n, [P, F, P]) for n in ("state", "sm"))
        at = part.sb("at", [C, H, C])
        ktok = part.sb("ktok", [C, F, P])
        bank = [part.ps(f"bank{i}", [P, 512]) for i in range(6)]
        S = {n: part.sem(n) for n in (
            "loaded", "staged", "stage_used", "turn", "decays", "exps", "scaled_in", "scores", "turned", "at_done",
            "ktok_done", "outputs", "d")}
        block = part.stack.enter_context(nc.Block())
        E = bank[0][:, 0:F * C].rearrange("p (f c) -> p f c", f=F)
        sc = bank[1][0:C, 0:H * C].rearrange("p (h c) -> p h c", h=H)
        kx = bank[2][0:C, 0:F * P].rearrange("p (f c) -> p f c", f=F)
        out = bank[3][:, 0:H * C].rearrange("p (h c) -> p h c", h=H)
        grow = bank[4][:, :].rearrange("p (f c) -> p f c", f=F)
        end = 0 if backward else C - 1

        def turns(eng, body):
            with eng.Fori(0, NT) as i:
                tile = (i - (NT - 1)) * (-1) if backward else i
                for j in range(2):
                    body(tile, 1 - j if backward else j, i * 2 + j)

        @block.sync
        def _(sp):
            part.load_matrices(sp, mt, names, S["loaded"])

            def body(t, s, n):
                sp.wait_ge(S["stage_used"], n + 1)
                sp.dma_start(las[:, :], la[:, bass.ds(t * 2 + s, 1), off:off + 256].rearrange("p a c -> p (a c)")).then_inc(S["staged"], 16)
                sp.dma_start(vs[:, :], v[64 * s:64 * s + 64, bass.ds(t, 1), :].rearrange("p a c -> p (a c)")).then_inc(S["staged"], 16)
            turns(sp, body)

        @block.tensor
        def _(pe):
            M = nc.tensor.matmul
            pe.wait_ge(S["loaded"], 16 * len(names))

            def body(t, s, n):
                pe.wait_ge(S["staged"], n * 32 + 32)
                pe.wait_ge(S["turn"], n + 1)
                for f in range(F):
                    M(E[:, f, :], las[:, f * P:(f + 1) * P], shift, start=True, stop=True)
                    mm = M(bank[0][:, F * C + f:F * C + f + 1], las[:, f * P:(f + 1) * P], mid, start=True, stop=True)
                mm.then_inc(S["decays"], 1)
                pe.wait_ge(S["scaled_in"], n + 1)
                for f in range(F):
                    M(sc[:, 2 * f:2 * f + 2, :], kt[:, f, :], qz[:, f, :, :], start=True, stop=True)
                mm = None
                for f in range(F):
                    mm = nc.tensor.transpose(kx[:, f, :], kt[:, f, :], mt[:, 0, :])
                mm.then_inc(S["turned"], 1)
                pe.wait_ge(S["at_done"], n + 1)
                for h in range(H):
                    M(out[:, h, :], vs[:, h * P:(h + 1) * P], at[:, h, :], start=True, stop=False)
                    M(out[:, h, :], sm[:, h // 2, :], qz[:, h // 2, h % 2, :], start=False, stop=True)
                pe.wait_ge(S["ktok_done"], n + 1)
                for f in range(F):
                    mm = M(grow[:, f, :], ktok[:, f, :], vs[:, f * 256:(f + 1) * 256], start=True, stop=True)
                mm.then_inc(S["outputs"], 1)
            turns(pe, body)

        @block.scalar
        def _(act):
            A = nc.scalar.activation

            def body(t, s, n):
                act.wait_ge(S["decays"], n + 1)
                A(e1[:, :, :], E, ACT.Exp).then_inc(S["exps"], 1)
                A(e3[:, :, :], E, ACT.Exp, scale=-1.0).then_inc(S["exps"], 1)
                A(em[:, :], bank[0][:, F * C:F * C + F], ACT.Exp).then_inc(S["exps"], 1)
                act.wait_ge(S["turned"], n + 1)
                A(ktok[:, :, :], kx, ACT.Copy).then_inc(S["ktok_done"], 1)
            turns(act, body)

        @block.vector
        def _(dve):
            V, T = nc.vector, nc.vector.tensor_tensor
            K = 3
            V.memset(qz[:, :, :, :], 0.0)
            V.memset(state[:, :, :], 0.0).then_inc(S["turn"], 1)
            dve.wait_ge(S["turn"], 1)
            dve.wait_ge(S["loaded"], 16 * len(names))
            dve.sem_inc(S["stage_used"], 1)

            def body(t, s, n):
                tok = bass.ds(t * P + s * C, C)
                dve.wait_ge(S["exps"], n * 3 + 3)
                T(sm[:, :, :], state[:, :, :], spread(em[:, :], P), ALU.mult)
                for e in range(2):
                    half = slice(64 * e, 64 * e + 64)
                    V.scalar_tensor_tensor(qz[half, :, e, :], qk[half, 0:2, tok], 0.125, e1[half, :, :], ALU.mult, ALU.mult)
                T(kt[:, :, :], qk[:, 2:4, tok], e3[:, :, :], ALU.mult).then_inc(S["scaled_in"], 1)
                dve.wait_ge(S["turned"], n + 1)
                T(at[:, :, :], sc, over_heads(keep, H), ALU.mult).then_inc(S["at_done"], 1)
                dve.wait_ge(S["outputs"], n + 1)
                for e in range(2):
                    half = slice(64 * e, 64 * e + 64)
                    i = T(state[half, :, :], sm[half, :, :], grow[half, :, e * P:(e + 1) * P], ALU.add)
                i.then_inc(S["d"], 1)
                if backward:
                    T(osum[:, :, tok], osum[:, :, tok], out, ALU.add).then_inc(S["d"], 1)
                else:
                    V.tensor_copy(osum[:, :, tok], out).then_inc(S["d"], 1)
                dve.wait_ge(S["d"], n * K + 2)
                T(state[:, :, :], state[:, :, :], e1[:, :, end:end + 1].to_broadcast([P, F, P]), ALU.mult).then_inc(S["d"], 1)
                dve.wait_ge(S["d"], n * K + 3)
                dve.sem_inc(S["stage_used"], 1)
                dve.sem_inc(S["turn"], 1)
            turns(dve, body)


def third_block(nc, dram, hid):
    full = dict(src0=0, chunks=C2, width=W2)
    w = dram["w_in_3"]
    with Part(nc, "s3", dram) as p:
        mix = p.sb("mix", [P, KD, SEQ])
        su = p.sb("su", [P, 4, SEQ])
        sv = p.sb("sv", [P, NT, 512])
        v = p.sb("v", [P, NT, 512])
        qk = p.sb("qk", [P, 4, SEQ])
        g = p.sb("g", [P, 4, SEQ])
        low = p.sb("low", [P, 1, SEQ])
        with Part(nc, "s3m", dram) as q:
            m = q.sb("m", [P, KD, SEQ])
            normalise(nc, dram, "n3", hid, 0, dram["norm_mix_g_3"], 4, 256, m)
            project(nc, dram, "p3q", m, 0, w, 0, KD, 4, C2, W2, qk, 0, 0, "copy")
            project(nc, dram, "p3g", m, 0, w, 1024, KD, 4, C2, W2, g, 0, 0, "silu")
            project(nc, dram, "p3a", m, 0, w, 1536, KD, 1, C2, W2, low, 0, 0, "copy")
            project(nc, dram, "p3u", m, 0, w, 1568, KD, 4, C2, W2, su, 0, 0, "gelu")
            by_tokens(nc, dram, "p3v", m, w, 512, 512, v, ACT.Copy)
            by_tokens(nc, dram, "p3s", m, w, 2080, 512, sv, ACT.Gelu)
        spatial_gate(nc, dram, sv, su, mix)
        with Part(nc, "s3l", dram) as q:
            la = q.sb("la", [64, SEQ // 64, 512])
            gla_decays(nc, dram, low, la)
            gla(nc, dram, "glaf", qk, v, la, mix[:, 0:4, :], False)
            gla(nc, dram, "glab", qk, v, la, mix[:, 0:4, :], True)
        unit(nc, dram, "u3", mix, 0, 4, "mean", dram["gla_norm_g_3"], times=g, **full)
        project(nc, dram, "p3o", mix, 0, dram["w_out_3"], 0, KD, 8, C2, W2, hid, 0, 0, "add")
    feed_forward(nc, dram, "3", hid, dram["norm_mlp_g_3"], dram["w_mlp1_3"], dram["w_mlp2_3"])
    normalise(nc, dram, "n3f", hid, 0, dram["final_norm_g_3"], C2, W2, hid)


def rows_of(a):
    return a.rearrange("(f p) t -> p f t", p=P)


def first_block(nc, dram):
    w = dram["w_in"]
    with Part(nc, "b1", dram) as p:
        decay = p.sb("decay", [P, NT1, H_A + H_C])
        beta = p.sb("beta", [P, NT1, H_A])
        dt = p.sb("dt", [P, NT1, H_C])
        pool = p.sb("pool", [P, 25, T1])
        with Part(nc, "b1h", dram) as q:
            hn = q.sb("hn", [P, KD, T1])
            rows = pool[:, KD:2 * KD].rearrange("p a t -> p (a t)").rearrange("p (t d) -> p t d", d=D)
            entry(nc, dram, pool[:, 0:KD], rows)
            copy_out(nc, dram, "keep", dram["hidden"].rearrange("(k p) t -> p k t", p=P), pool[:, 0:KD, T1 - SEQ:])
            normalise(nc, dram, "n1", pool[:, 0:KD], S1, dram["norm_pre"], C1, W1, hn)
            clear(nc, dram, "c1", pool[:, :, :S1], hn[:, :, :S1])
            gates(nc, dram, hn, decay, beta, dt)
            project(nc, dram, "pa", hn, S1, w, 0, KD, 18, C1, W1, pool, S1, 0, "conv", {"taps": dram["dn_conv"]})
            project(nc, dram, "pz", hn, S1, w, 18 * P, KD, 6, C1, W1, pool, S1, 18, "silu_gain", {"gain": dram["dn_norm"]})
            unit(nc, dram, "uq", pool, 0, 6, "ones", DH_A ** -0.5)
            unit(nc, dram, "uk", pool, 6, 6, "ones", 1.0)
            delta_rule(nc, dram, pool[:, 0:18], decay, beta)
            unit(nc, dram, "uo", pool, 0, 6, "mean", 1.0, times=pool[:, 18:24, S1:])
            copy_out(nc, dram, "oa", rows_of(dram["mix"])[:, 0:6, S1:], pool[:, 0:6, S1:])
            project(nc, dram, "pc", hn, S1, w, P_A + P_B, KD, 6, C1, W1, pool, S1, 0, "silu")
            project(nc, dram, "pd", hn, S1, w, P_A + P_B + D_C, KD, 14, C1, W1, pool, S1, 6, "conv",
                    {"taps": dram["mb_conv"], "bias": dram["mb_conv_b"]})
            mamba(nc, dram, pool, decay, dt)
            clear(nc, dram, "c3", pool[:, :, :S1])
            project(nc, dram, "pb", hn, S1, w, P_A, KD, 17, C1, W1, pool, S1, 0, "shift", {"mu": dram["rw_mu"]})
        b, rate, unit_k = pool[:, 0:17], pool[:, 17:21], pool[:, 21:25]
        rwkv_prepare(nc, dram, b, rate, unit_k)
        unit(nc, dram, "uu", unit_k, 0, 4, "head_ones", 1.0)
        rwkv(nc, dram, b, rate, unit_k)
        rwkv_finish(nc, dram, b, unit_k)
        copy_out(nc, dram, "ob", rows_of(dram["mix"])[:, 6:10, S1:], unit_k[:, :, S1:])


def first_out(nc, dram, hid):
    with Part(nc, "b1o", dram) as p:
        mix = p.sb("mix", [P, 16, SEQ])
        o = p.sb("o", [P, KD, SEQ])
        copy_out(nc, dram, "ldm", mix[:, :, :], dram["mix"].rearrange("(f p) t -> p f t", p=P)[:, :, T1 - SEQ:])
        copy_out(nc, dram, "ldh", hid[:, :, :], dram["hidden"].rearrange("(k p) t -> p k t", p=P))
        project(nc, dram, "p1o", mix, 0, dram["w_out"], 0, 16, 8, C2, W2, o, 0, 0, "copy")
        normalise(nc, dram, "n1o", o, 0, dram["norm_post"], 4, 256, hid, add=True)


def program(nc, dram, out):
    dram["hidden"] = nc.dram_tensor("hidden", (D, SEQ), F32, kind="Internal").ap()
    dram["mix"] = nc.dram_tensor("mix", (2 * D, T1), F32, kind="Internal").ap()
    dram["log_w"] = nc.dram_tensor("log_w", (T1, D_B), F32, kind="Internal").ap()
    first_block(nc, dram)
    with Part(nc, "all", dram) as p:
        hid = p.sb("hid", [P, KD, SEQ])
        first_out(nc, dram, hid)
        second_block(nc, dram, hid)
        third_block(nc, dram, hid)
        leave(nc, dram, hid, out)


def pack(inputs):
    f = {k: np.asarray(v) for k, v in inputs.items()}
    cols = lambda v: np.ascontiguousarray(v.reshape(-1, P).T)
    taps = lambda v: np.ascontiguousarray(v.reshape(v.shape[0], -1, P).transpose(2, 0, 1))
    m = constant_matrices()
    d = {"matrices": np.concatenate([m[n] for n in NAMES]), "x": f["x"], "meta_tokens": f["meta_tokens"],
         "w_in": f["w_in"][0], "w_out": f["w_out"][0],
         "dn_conv": taps(f["dn_conv"][0]), "mb_conv": taps(f["mb_conv"][0]), "conv_w_2": taps(f["conv_w_2"][0]),
         "gate_bias": np.concatenate([f["dn_dt_bias"], f["mb_dt_bias"]], 1),
         "gate_log": np.concatenate([f["dn_A_log"], f["mb_A_log"]], 1),
         "g_final_2": cols(f["g_final_2"]), "final_norm_g_3": cols(f["final_norm_g_3"]),
         "mb_D": cols(np.repeat(f["mb_D"][0], DH_C)), "rw_w0": f["rw_w0"],
         "p_2": f["p_2"][0, 0], "b_s_3": f["b_s_3"].reshape(1, -1),
         "b_a_3": np.concatenate([f["b_a_fwd_3"], f["b_a_bwd_3"]], 1)}
    d["dn_norm"] = cols(np.tile(f["dn_norm"][0], H_A))
    for n in ("norm_pre", "norm_post", "mb_conv_b", "rw_mu", "rw_a0", "rw_k_k", "rw_k_a", "rw_r_k",
              "rw_ln_w", "rw_ln_b", "mb_norm", "g_mix_2", "g_conv_out_2", "g_attn_out_2", "g_mlp_2", "g_ple_2",
              "norm_mix_g_3", "gla_norm_g_3", "sgu_norm_g_3", "norm_mlp_g_3"):
        d[n] = cols(f[n][0])
    for n in ("rw_w2", "rw_a2", "w_in_2", "w_out_2", "w_up_2", "w_down_2", "w_ple_gate_2", "w_ple_proj_2",
              "w_in_3", "w_a2_fwd_3", "w_a2_bwd_3", "w_s_3", "w_out_3", "w_mlp1_3", "w_mlp2_3"):
        d[n] = f[n][0]
    return d



def kernel(**inputs):
    import concourse.bacc as _bacc
    from concourse.bass_utils import run_bass_kernel_spmd as _run

    nc = _bacc.Bacc("TRN2", target_bir_lowering=False, num_devices=1)
    arrays = pack(inputs)
    dram = {n: nc.dram_tensor(n + "_dram", a.shape, mybir.dt.from_np(a.dtype), kind="ExternalInput").ap()
            for n, a in arrays.items()}
    out = nc.dram_tensor("out_dram", (SEQ, D), F32, kind="ExternalOutput").ap()
    program(nc, dram, out)
    r = _run(nc, [{n + "_dram": a for n, a in arrays.items()}], core_ids=[0])
    return r.results[0]["out_dram"].reshape(1, SEQ, D)
```

```python
import math
from contextlib import ExitStack

import numpy as np

import concourse.bass as bass
from concourse import mybir

F32 = mybir.dt.float32
F32R = mybir.dt.float32r
ACT = mybir.ActivationFunctionType
ALU = mybir.AluOpType

P = 128
D = 1024
KD = D // P
SEQ = 1024
META = 16
FRONT = P - META
T1 = FRONT + META + SEQ
NT1 = T1 // P
NT = SEQ // P
W1 = 352
C1 = 3
S1 = T1 - C1 * W1
LIVE = C1 * W1
W2 = 512
C2 = SEQ // W2
NORM_EPS = 1e-6

H_A, DH_A = 6, 128
D_A = H_A * DH_A
H_B, DH_B = 8, 64
D_B = H_B * DH_B
H_C, DH_C, G_C, N_C = 12, 64, 4, 128
D_C = H_C * DH_C
P_A = 4 * D_A + 2 * H_A
P_B = 4 * D_B + 128
P_C = 2 * D_C + 2 * G_C * N_C + H_C
GN_EPS = 64e-5

LEVELS = 7


def constant_matrices():
    r = np.arange(P)[:, None]
    c = np.arange(P)[None, :]
    m = {
        "ident": r == c,
        "ones": np.ones((P, P)),
        "zeros": np.zeros((P, P)),
        "upto": r <= c,
        "before": r < c,
        "after": r > c,
        "from": r >= c,
        "neg_before": -1.0 * (r < c),
        "neg_from": -1.0 * (r >= c),
        "neg_ones": -np.ones((P, P)),
        "upto_mid": 1.0 * (r <= c) - (r <= P // 2 - 1),
        "before_mid": 1.0 * (r < c) - (r <= P // 2 - 1),
        "head_mean": (r // 64 == c // 64) / 64.0,
        "head_ones": r // 64 == c // 64,
        "upto_mid64": 1.0 * (r <= c) - (r <= 32),
        "from_mid64": 1.0 * (r >= c) - (r >= 31),
        "mid64": np.where(c == 0, r <= 32, (c == 1) & (r >= 31)),
        "real": r >= FRONT,
        "mean": np.full((P, P), 1.0 / P),
        "mid": (r <= P // 2 - 1) & (c == 0),
    }
    for l in range(LEVELS):
        b = 2 ** l
        pair = (r // (2 * b) == c // (2 * b)) & (r // b % 2 == 1) & (c // b % 2 == 0)
        m[f"join{l}"] = pair | (r == c)
    m["join0T"] = m["join0"].T
    g = lambda tile, i: (tile * P + i) // 192
    for a in range(3):
        for b in range(3):
            if abs(a - b) < 2:
                m[f"group{a}{b}"] = (g(a, r) == g(b, c)) / 192.0
    return {k: np.broadcast_to(v, (P, P)).astype(np.float32) for k, v in m.items()}


NAMES = list(constant_matrices())


class Part:

    places = {}
    twins = {}

    def __init__(self, nc, name, dram):
        self.nc, self.name, self.dram, self.stack = nc, name, dram, ExitStack()
        self.sems = []

    def __enter__(self):
        return self

    def __exit__(self, *a):
        self.stack.close()
        if self.sems:
            self.nc.clear_and_free_semaphores(self.sems)
            self.nc.all_engine_barrier()

    def sb(self, name, shape, dt=F32):
        tensor = self.stack.enter_context(self.nc.sbuf_tensor(f"{self.name}_{name}", list(shape), dt))
        size = int(np.prod(shape[1:])) * 4
        Part.places[tensor.name] = (self.nc, self.nc.sbuf_base - size, list(shape))
        Part.twins.pop(tensor.name, None)
        return tensor

    def ps(self, name, shape):
        return self.stack.enter_context(self.nc.psum_tensor(f"{self.name}_{name}", list(shape), F32))

    def sem(self, name):
        s = self.nc.alloc_semaphore(f"{self.name}_{name}")
        self.sems.append(s)
        return s

    def load_matrices(self, eng, where, names, sem):
        for i, n in enumerate(names):
            j = NAMES.index(n)
            eng.dma_start(where[:, i, :], self.dram["matrices"][j * P:(j + 1) * P, :]).then_inc(sem, 16)
        return 16 * len(names)


def spread(ap, n):
    return ap.unsqueeze(2).to_broadcast([ap.shape[0], ap.shape[1], n])


def rounded(a):
    name = a.tensor.name
    nc, place, shape = Part.places[name]
    if name not in Part.twins:
        Part.twins[name] = nc.alloc_sbuf_tensor_at(name + "_rounded", shape, F32R, offset=place)
    return bass.AP(Part.twins[name], a.offset, a.ap)


def project(nc, dram, name, src, src0, weights, col0, k_tiles, n_tiles, chunks, width, dst, dst0,
            dst_tile0, mode, extra=None, hi=None, split_already=False):
    live = chunks * width
    halo = {"conv": 3, "shift": 1}.get(mode, 0)
    with Part(nc, name, dram) as part:
        w = [part.sb(f"w{s}", [P, k_tiles, P]) for s in range(2)]
        acc = [part.ps(f"acc{s}", [P, chunks, 512]) for s in range(2)]
        w_ready = [part.sem(f"w_ready{s}") for s in range(2)]
        if hi is not None:
            w_hi = [part.sb(f"w_hi{s}", [P, k_tiles, P]) for s in range(2)]
            w_rounded, w_split, src_rounded, src_split = (part.sem(x) for x in (
                "w_rounded", "w_split", "src_rounded", "src_split"))
        params_ready = part.sem("params_ready")
        product_done = part.sem("product_done")
        acc_free = part.sem("acc_free")
        raw_ready = part.sem("raw_ready")
        vector_done = part.sem("vector_done")
        tile_done = part.sem("tile_done")
        step = part.sem("step")
        n_params, params = 0, {}
        if halo:
            raw = [part.sb(f"raw{s}", [P, halo + live]) for s in range(2)]
        if mode in ("conv", "shift"):
            tmp = [part.sb(f"tmp{s}", [P, live]) for s in range(2)]
        if mode in ("silu_gain", "gate_add"):
            tmp = [part.sb(f"tmp{s}", [P, chunks, width]) for s in range(2)]
        if mode == "conv":
            params["taps"] = part.sb("taps", [P, 4, n_tiles])
            if extra.get("bias") is not None:
                params["bias"] = part.sb("bias", [P, n_tiles])
        if mode == "shift":
            params["mu"] = part.sb("mu", [P, n_tiles])
            params["keep"] = part.sb("keep", [P, n_tiles])
        if mode == "silu_gain":
            params["gain"] = part.sb("gain", [P, n_tiles])
        block = part.stack.enter_context(nc.Block())
        w_view = weights.rearrange("(k p) c -> p k c", p=P)

        def each_tile(eng, body):
            if n_tiles >= 2:
                with eng.Fori(0, n_tiles // 2) as i:
                    for s in range(2):
                        body(i * 2 + s, s, i)
            if n_tiles % 2:
                body(n_tiles - 1, 0, n_tiles // 2)

        def finish_tiles(eng, ahead, finish):
            if hi is None:
                if finish:
                    each_tile(eng, finish)
                return
            ahead(0, 0)

            def body(f, s, i, more):
                if more:
                    ahead(f + 1, 1 - s)
                if finish:
                    finish(f, s, i)
            final = 2 - n_tiles % 2
            if n_tiles > final:
                with eng.Fori(0, (n_tiles - final) // 2) as i:
                    for s in range(2):
                        body(i * 2 + s, s, i, True)
            for f in range(n_tiles - final, n_tiles):
                body(f, f % 2, f // 2, f < n_tiles - 1)

        def round_weights(f, s):
            nc.scalar.wait_ge(w_ready[s], f * 8 + (16 - 8 * s))
            nc.scalar.wait_ge(product_done, f + 1)
            nc.scalar.activation(rounded(w_hi[s][:, :, :]), w[s][:, :, :], ACT.Copy).then_inc(w_rounded, 1)

        def split_weights(f, s):
            nc.vector.wait_ge(w_rounded, f + 1)
            nc.vector.tensor_tensor(rounded(w[s][:, :, :]), w[s][:, :, :], rounded(w_hi[s][:, :, :]), ALU.subtract).then_inc(w_split, 1)

        covered = slice(src0, src0 + live)

        @block.sync
        def _(sp):
            if mode == "conv":
                for j in range(4):
                    sp.dma_start(params["taps"][:, j, :], extra["taps"][:, j, :]).then_inc(params_ready, 16)
                if "bias" in params:
                    sp.dma_start(params["bias"][:, :], extra["bias"]).then_inc(params_ready, 16)
            if mode == "shift":
                sp.dma_start(params["mu"][:, :], extra["mu"]).then_inc(params_ready, 16)
            if mode == "silu_gain":
                sp.dma_start(params["gain"][:, :], extra["gain"]).then_inc(params_ready, 16)

            def load(f, s, i):
                sp.wait_ge(product_done, f + 1)
                sp.dma_start(w[s][:, :, :], w_view[:, :, bass.ds(f * P + col0, P)]).then_inc(w_ready[s], 16)
            each_tile(sp, load)

        n_params = {"conv": 5 if "bias" in params else 4, "shift": 1, "silu_gain": 1}.get(mode, 0) * 16

        @block.tensor
        def _(pe):
            pe.sem_inc(product_done, 2)

            def multiply(f, s, i):
                if hi is not None:
                    pe.wait_ge(w_split, f + 1)
                else:
                    pe.wait_ge(w_ready[s], i * 16 + 16)
                pe.wait_ge(acc_free, f + 1)
                for c in range(chunks):
                    for k in range(k_tiles):
                        if hi is not None:
                            if c == 0 and not split_already:
                                pe.wait_ge(src_split, k + 1)
                            at = slice(src0 + c * width, src0 + (c + 1) * width)
                            for j, (l, r) in enumerate(((w_hi[s], hi), (w[s], hi), (w_hi[s], src))):
                                mm = nc.tensor.matmul(acc[s][:, c, :width], rounded(l[:, k, :]), rounded(r[:, k, at]),
                                                      start=(k == 0 and j == 0), stop=(k == k_tiles - 1 and j == 2))
                            continue
                        mm = nc.tensor.matmul(acc[s][:, c, :width], w[s][:, k, :],
                                              src[:, k, src0 + c * width:src0 + (c + 1) * width],
                                              start=(k == 0), stop=(k == k_tiles - 1))
                mm.then_inc(product_done, 1)
            each_tile(pe, multiply)

        def out(f):
            return dst[:, f + dst_tile0, dst0:dst0 + live]

        def out3(f):
            return out(f).rearrange("p (c n) -> p c n", c=chunks)

        def a3(s):
            return acc[s][:, :, :width]

        @block.scalar
        def _(act):
            finish = None
            if hi is not None and not split_already:
                for k in range(k_tiles):
                    nc.scalar.activation(rounded(hi[:, k, covered]), src[:, k, covered], ACT.Copy).then_inc(src_rounded, 1)
            if mode in ("conv", "shift"):
                act.sem_inc(acc_free, 2)

                def finish(f, s, i):
                    act.wait_ge(product_done, f + 3)
                    act.wait_ge(vector_done, f + 1)
                    nc.scalar.activation(raw[s][:, halo:].rearrange("p (c n) -> p c n", c=chunks), a3(s),
                                         ACT.Copy).then_inc(acc_free, 1)
                    if mode == "conv":
                        act.wait_ge(vector_done, f + 3)
                        bias = params["bias"][:, bass.ds(f, 1)] if "bias" in params else 0.0
                        nc.scalar.activation(out(f), tmp[s][:, :], ACT.Silu, bias=bias).then_inc(tile_done, 1)
                if mode == "conv":
                    act.sem_inc(tile_done, 2)
                    act.wait_ge(params_ready, n_params)
            elif mode in ("silu_gain", "relu2"):
                if mode == "silu_gain":
                    act.sem_inc(acc_free, 2)

                def finish(f, s, i):
                    act.wait_ge(product_done, f + 3)
                    if mode == "silu_gain":
                        act.wait_ge(vector_done, f + 1)
                    a = nc.scalar.activation(tmp[s][:, :, :] if mode == "silu_gain" else out3(f), a3(s),
                                             ACT.Silu if mode == "silu_gain" else ACT.Relu)
                    a.then_inc(acc_free if mode == "silu_gain" else raw_ready, 1)
            elif mode in ("copy", "gelu", "sigmoid", "silu"):
                act.sem_inc(acc_free, 2)
                func = {"copy": ACT.Copy, "gelu": ACT.Gelu, "sigmoid": ACT.Sigmoid, "silu": ACT.Silu}[mode]

                def finish(f, s, i):
                    act.wait_ge(product_done, f + 3)
                    nc.scalar.activation(out3(f), a3(s), func).then_inc(acc_free, 1)

            finish_tiles(act, round_weights, finish)

        @block.vector
        def _(dve):
            finish = None
            if hi is not None and not split_already:
                for k in range(k_tiles):
                    dve.wait_ge(src_rounded, k + 1)
                    nc.vector.tensor_tensor(rounded(src[:, k, covered]), src[:, k, covered], rounded(hi[:, k, covered]),
                                            ALU.subtract).then_inc(src_split, 1)
            if n_params:
                dve.wait_ge(params_ready, n_params)
            if mode == "conv":
                for s in range(2):
                    nc.vector.memset(raw[s][:, 0:halo], 0.0)
                dve.sem_inc(vector_done, 2)

                def finish(f, s, i):
                    dve.wait_ge(acc_free, f + 3)
                    dve.wait_ge(tile_done, f + 1)
                    tap = lambda j: params["taps"][:, j, bass.ds(f, 1)]
                    nc.vector.tensor_scalar(tmp[s][:, :], raw[s][:, 3:3 + live], tap(3), None, ALU.mult).then_inc(step, 1)
                    for n, j in enumerate((2, 1, 0)):
                        dve.wait_ge(step, f * 3 + n + 1)
                        nc.vector.scalar_tensor_tensor(tmp[s][:, :], raw[s][:, j:j + live], tap(j), tmp[s][:, :],
                                                       ALU.mult, ALU.add).then_inc(step if j else vector_done, 1)
            if mode == "shift":
                for s in range(2):
                    nc.vector.memset(raw[s][:, 0:halo], 0.0)
                nc.vector.tensor_scalar(params["keep"][:, :], params["mu"][:, :], -1.0, 1.0, ALU.mult, ALU.add).then_inc(step, 1)
                dve.wait_ge(step, 1)
                dve.sem_inc(vector_done, 2)

                def finish(f, s, i):
                    dve.wait_ge(acc_free, f + 3)
                    nc.vector.tensor_scalar(tmp[s][:, :], raw[s][:, 0:live], params["mu"][:, bass.ds(f, 1)], None,
                                            ALU.mult).then_inc(step, 1)
                    dve.wait_ge(step, f + 2)
                    nc.vector.scalar_tensor_tensor(out(f), raw[s][:, 1:1 + live], params["keep"][:, bass.ds(f, 1)],
                                                   tmp[s][:, :], ALU.mult, ALU.add).then_inc(vector_done, 1)
            if mode == "silu_gain":
                dve.sem_inc(vector_done, 2)

                def finish(f, s, i):
                    dve.wait_ge(acc_free, f + 3)
                    nc.vector.tensor_scalar(out3(f), tmp[s][:, :, :], params["gain"][:, bass.ds(f, 1)], None,
                                            ALU.mult).then_inc(vector_done, 1)
            if mode == "relu2":
                dve.sem_inc(vector_done, 2)
                dve.sem_inc(acc_free, 2)

                def finish(f, s, i):
                    dve.wait_ge(raw_ready, f + 1)
                    nc.vector.tensor_tensor(out3(f), out3(f), a3(s), ALU.mult).then_inc(vector_done, 1)
                    dve.wait_ge(vector_done, f + 3)
                    dve.sem_inc(acc_free, 1)
            if mode == "add":
                dve.sem_inc(acc_free, 2)

                def finish(f, s, i):
                    dve.wait_ge(product_done, f + 3)
                    nc.vector.tensor_tensor(out3(f), out3(f), a3(s), ALU.add).then_inc(acc_free, 1)
            if mode == "gate_add":
                dve.sem_inc(acc_free, 2)
                gate = extra["gate"]

                def finish(f, s, i):
                    dve.wait_ge(product_done, f + 3)
                    nc.vector.tensor_tensor(tmp[s][:, :, :], gate[:, f, :].rearrange("p (c n) -> p c n", c=chunks),
                                            a3(s), ALU.mult).then_inc(acc_free, 1)
                    dve.wait_ge(acc_free, f + 3)
                    nc.vector.tensor_tensor(out3(f), out3(f), tmp[s][:, :, :], ALU.add).then_inc(step, 1)
                    dve.wait_ge(step, f + 1)
            finish_tiles(dve, split_weights, finish)


def normalise(nc, dram, name, src, src0, gain, chunks, width, dst, add=False, scratch=None):
    with Part(nc, name, dram) as part:
        mats = part.sb("mats", [P, 1, P])
        gains = part.sb("gains", [P, KD])
        buffers = part.sb("square", [P, 2, KD, width]) if scratch is None else None
        square = scratch or [buffers[:, s] for s in range(2)]
        scale = part.sb("scale", [P, 2, width])
        total = part.ps("total", [P, 2, 512])
        grown = part.sb("grown", [P, KD, width]) if add else None
        loaded, squared, summed, logged, scaled, out_done, step = (part.sem(n) for n in (
            "loaded", "squared", "summed", "logged", "scaled", "out_done", "step"))
        block = part.stack.enter_context(nc.Block())

        @block.sync
        def _(sp):
            part.load_matrices(sp, mats, ["ones"], loaded)
            sp.dma_start(gains[:, :], gain).then_inc(loaded, 16)

        cols = lambda c: slice(src0 + c * width, src0 + (c + 1) * width)

        @block.scalar
        def _(act):
            nc.scalar.preload_act_table_set("natural_log_exp_and_others")
            def square_of(c):
                if c >= 2:
                    act.wait_ge(summed, c - 1)
                nc.scalar.activation(square[c % 2], src[:, :, cols(c)], ACT.Square).then_inc(squared, 1)

            square_of(0)
            for c in range(chunks):
                if c + 1 < chunks:
                    square_of(c + 1)
                act.wait_ge(summed, c + 1)
                if c >= 2:
                    act.wait_ge(out_done, KD * (c - 1))
                nc.scalar.activation(scale[:, c % 2], total[:, c % 2, :width], ACT.Ln, scale=1.0 / D, bias=NORM_EPS).then_inc(logged, 1)
                act.wait_ge(logged, c + 1)
                nc.scalar.activation(scale[:, c % 2], scale[:, c % 2], ACT.Exp, scale=-0.5).then_inc(scaled, 1)

        @block.tensor
        def _(pe):
            pe.wait_ge(loaded, 32)
            for c in range(chunks):
                pe.wait_ge(squared, c + 1)
                if c >= 2:
                    pe.wait_ge(logged, c - 1)
                for k in range(KD):
                    mm = nc.tensor.matmul(total[:, c % 2, :width], mats[:, 0, :], square[c % 2][:, k, :],
                                          start=(k == 0), stop=(k == KD - 1))
                mm.then_inc(summed, 1)

        @block.vector
        def _(dve):
            dve.wait_ge(loaded, 32)
            for c in range(chunks):
                dve.wait_ge(scaled, c + 1)
                for k in range(KD):
                    if add:
                        if c >= 1:
                            dve.wait_ge(out_done, KD * (c - 1) + k + 1)
                        nc.vector.scalar_tensor_tensor(grown[:, k, :], src[:, k, cols(c)], gains[:, k:k + 1],
                                                       scale[:, c % 2], ALU.mult, ALU.mult).then_inc(step, 1)
                        dve.wait_ge(step, KD * c + k + 1)
                        nc.vector.tensor_tensor(dst[:, k, cols(c)], dst[:, k, cols(c)], grown[:, k, :], ALU.add).then_inc(out_done, 1)
                        continue
                    nc.vector.scalar_tensor_tensor(dst[:, k, cols(c)], src[:, k, cols(c)], gains[:, k:k + 1],
                                                   scale[:, c % 2], ALU.mult, ALU.mult).then_inc(out_done, 1)


def entry(nc, dram, frame, rows):
    with Part(nc, "entry", dram) as part:
        ident = part.sb("ident", [P, 1, P])
        cross = part.ps("cross", [P, 4, KD, P])
        loaded, cleared, turned, moved = (part.sem(n) for n in ("loaded", "cleared", "turned", "moved"))
        block = part.stack.enter_context(nc.Block())

        @block.sync
        def _(sp):
            part.load_matrices(sp, ident, ["ident"], loaded)
            sp.wait_ge(cleared, 1)
            sp.dma_start(rows[FRONT:P, 0, :], dram["meta_tokens"][:, :]).then_inc(loaded, 16)
            sp.dma_start(rows[:, 1:, :], dram["x"][0].rearrange("(t p) d -> p t d", p=P)).then_inc(loaded, 16)

        @block.gpsimd
        def _(pool):
            nc.gpsimd.memset(rows[:, 0, :], 0.0).then_inc(cleared, 1)

        @block.tensor
        def _(pe):
            pe.wait_ge(loaded, 48)
            for t in range(NT1):
                if t >= 4:
                    pe.wait_ge(moved, t - 3)
                for k in range(KD):
                    mm = nc.tensor.transpose(cross[:, t % 4, k, :], rows[:, t, k * P:(k + 1) * P], ident[:, 0, :])
                mm.then_inc(turned, 1)

        @block.vector
        def _(dve):
            for t in range(NT1):
                dve.wait_ge(turned, t + 1)
                nc.vector.tensor_copy(frame[:, :, t * P:(t + 1) * P], cross[:, t % 4]).then_inc(moved, 1)


def leave(nc, dram, hidden, out):
    with Part(nc, "leave", dram) as part:
        ident = part.sb("ident", [P, 1, P])
        rows = part.sb("rows", [P, 2, D])
        cross = part.ps("cross", [P, 4, KD, P])
        loaded, turned, moved = (part.sem(n) for n in ("loaded", "turned", "moved"))
        stored = [part.sem(f"stored{s}") for s in range(2)]
        block = part.stack.enter_context(nc.Block())

        @block.sync
        def _(sp):
            part.load_matrices(sp, ident, ["ident"], loaded)
            for t in range(NT):
                sp.wait_ge(moved, t + 1)
                sp.dma_start(out[t * P:(t + 1) * P, :], rows[:, t % 2, :]).then_inc(stored[t % 2], 16)
            for s in range(2):
                sp.wait_ge(stored[s], 16 * (NT // 2))

        @block.tensor
        def _(pe):
            pe.wait_ge(loaded, 16)
            for t in range(NT):
                if t >= 4:
                    pe.wait_ge(moved, t - 3)
                for k in range(KD):
                    mm = nc.tensor.transpose(cross[:, t % 4, k, :], hidden[:, k, t * P:(t + 1) * P], ident[:, 0, :])
                mm.then_inc(turned, 1)

        @block.vector
        def _(dve):
            for t in range(NT):
                dve.wait_ge(turned, t + 1)
                if t >= 2:
                    dve.wait_ge(stored[t % 2], 16 * (t // 2))
                nc.vector.tensor_copy(rows[:, t % 2, :], cross[:, t % 4].rearrange("p k n -> p (k n)")).then_inc(moved, 1)


def over_heads(m, n):
    return m.unsqueeze(1).to_broadcast([m.shape[0], n, m.shape[1]])


def gates(nc, dram, hn, decay, beta, dt):
    HS = H_A + H_C
    with Part(nc, "gates", dram) as part:
        w = part.sb("w", [P, KD, 24])
        real = part.sb("real", [P, 1, P])
        rows = part.sb("rows", [P, 2, HS])
        v, u, w1, d1, eq, lg = (part.sb(n, [P, NT1, HS]) for n in ("v", "u", "w1", "d1", "eq", "lg"))
        e = part.sb("e", [P, NT1, H_A])
        ea = part.sb("ea", [P, HS])
        acc = part.ps("acc", [P, 2, 512])
        raw = acc[:, 0, :NT1 * 24].rearrange("p (t c) -> p t c", c=24)
        loaded, product, biased, absolute, small, plus1, logged, grown, betas, step = (part.sem(n) for n in (
            "loaded", "product", "biased", "absolute", "small", "plus1", "logged", "grown", "betas", "step"))
        block = part.stack.enter_context(nc.Block())
        w_in = dram["w_in"].rearrange("(k p) c -> p k c", p=P)

        @block.sync
        def _(sp):
            with nc.allow_non_contiguous_dma(reason="24 columns of gates"):
                sp.dma_start(w[:, :, 0:6], w_in[:, :, 4 * D_A:4 * D_A + 6]).then_inc(loaded, 16)
                sp.dma_start(w[:, :, 6:18], w_in[:, :, P_A + P_B + P_C - H_C:P_A + P_B + P_C]).then_inc(loaded, 16)
                sp.dma_start(w[:, :, 18:24], w_in[:, :, 4 * D_A + 6:4 * D_A + 12]).then_inc(loaded, 16)
            sp.dma_start(rows[:, 0, :], dram["gate_bias"].to_broadcast([P, HS])).then_inc(loaded, 16)
            sp.dma_start(rows[:, 1, :], dram["gate_log"].to_broadcast([P, HS])).then_inc(loaded, 16)
            part.load_matrices(sp, real, ["real"], loaded)

        @block.tensor
        def _(pe):
            pe.wait_ge(loaded, 96)
            for t in range(NT1):
                for k in range(KD):
                    mm = nc.tensor.matmul(raw[:, t, :], hn[:, k, t * P:(t + 1) * P], w[:, k, :],
                                          start=(k == 0), stop=(k == KD - 1))
            mm.then_inc(product, 1)

        @block.scalar
        def _(act):
            nc.scalar.preload_act_table_set("natural_log_exp_and_others")
            act.wait_ge(loaded, 96)
            nc.scalar.activation(ea[:, :], rows[:, 1, :], ACT.Exp).then_inc(grown, 1)
            act.wait_ge(biased, 1)
            nc.scalar.activation(e[:, :, :], raw[:, :, 18:24], ACT.Exp, scale=-1.0).then_inc(betas, 1)
            nc.scalar.activation(u[:, :, :], v[:, :, :], ACT.Abs).then_inc(absolute, 1)
            act.wait_ge(absolute, 1)
            nc.scalar.activation(u[:, :, :], u[:, :, :], ACT.Exp, scale=-1.0).then_inc(small, 1)
            act.wait_ge(plus1, 1)
            nc.scalar.activation(lg[:, :, :], w1[:, :, :], ACT.Ln).then_inc(logged, 1)

        @block.vector
        def _(dve):
            n = [0]

            def then(i):
                n[0] += 1
                i.then_inc(step, 1)
                dve.wait_ge(step, n[0])
            V = nc.vector
            over = lambda r: over_heads(r, NT1)
            dve.wait_ge(product, 1)
            dve.wait_ge(loaded, 96)
            V.tensor_tensor(v[:, :, :], raw[:, :, 0:HS], over(rows[:, 0, :]), ALU.add).then_inc(biased, 1)
            dve.wait_ge(betas, 1)
            then(V.tensor_scalar(e[:, :, :], e[:, :, :], 1.0, None, ALU.add))
            V.reciprocal(beta[:, :, :], e[:, :, :])
            dve.wait_ge(small, 1)
            V.tensor_scalar(w1[:, :, :], u[:, :, :], 1.0, None, ALU.add).then_inc(plus1, 1)
            dve.wait_ge(plus1, 1)
            then(V.tensor_scalar(d1[:, :, :], w1[:, :, :], -1.0, None, ALU.add))
            then(V.tensor_scalar(eq[:, :, :], d1[:, :, :], 0.0, None, ALU.is_equal))
            then(V.tensor_tensor(d1[:, :, :], d1[:, :, :], eq[:, :, :], ALU.add))
            then(V.reciprocal(d1[:, :, :], d1[:, :, :]))
            dve.wait_ge(logged, 1)
            then(V.tensor_tensor(d1[:, :, :], d1[:, :, :], lg[:, :, :], ALU.mult))
            then(V.tensor_tensor(d1[:, :, :], d1[:, :, :], eq[:, :, :], ALU.add))
            then(V.tensor_tensor(u[:, :, :], u[:, :, :], d1[:, :, :], ALU.mult))
            then(V.scalar_tensor_tensor(v[:, :, :], v[:, :, :], 0.0, u[:, :, :], ALU.max, ALU.add))
            dve.wait_ge(grown, 1)
            V.scalar_tensor_tensor(decay[:, :, :], v[:, :, :], -1.0, over(ea[:, :]), ALU.mult, ALU.mult)
            then(V.tensor_copy(dt[:, :, :], v[:, :, H_A:]))
            V.tensor_scalar(dt[:, 0, :], dt[:, 0, :], real[:, 0, 0:1], None, ALU.mult)


def unit(nc, dram, name, buf, first, n_tiles, matrix, scale, eps=1e-6, times=None, src0=S1, chunks=C1, width=W1):
    live = chunks * width
    with Part(nc, name, dram) as part:
        mats = part.sb("mats", [P, 1, P])
        square = part.sb("square", [P, 2, live])
        root = part.sb("root", [P, 2, chunks, width])
        total = part.ps("total", [P, 2, 4, 512])
        gains = None if isinstance(scale, float) else part.sb("gains", [P, n_tiles])
        loaded, squared, summed, logged, scaled, out_done, step = (part.sem(n) for n in (
            "loaded", "squared", "summed", "logged", "scaled", "out_done", "step"))
        block = part.stack.enter_context(nc.Block())
        tile = lambda f: buf[:, f + first, src0:src0 + live]
        sums = lambda s: total[:, s, :chunks, :width]

        @block.sync
        def _(sp):
            part.load_matrices(sp, mats, [matrix], loaded)
            if gains is not None:
                sp.dma_start(gains[:, :], scale).then_inc(loaded, 16)

        @block.scalar
        def _(act):
            nc.scalar.preload_act_table_set("natural_log_exp_and_others")
            with act.Fori(0, n_tiles // 2) as i:
                for s in range(2):
                    nc.scalar.activation(square[:, s], tile(i * 2 + s), ACT.Square).then_inc(squared, 1)
                for s in range(2):
                    act.wait_ge(summed, i * 2 + s + 1)
                    act.wait_ge(out_done, i * 2 + s + 1)
                    nc.scalar.activation(root[:, s], sums(s), ACT.Ln, bias=eps).then_inc(logged, 1)
                    act.wait_ge(logged, i * 2 + s + 1)
                    nc.scalar.activation(root[:, s], root[:, s], ACT.Exp, scale=-0.5).then_inc(scaled, 1)

        @block.tensor
        def _(pe):
            pe.wait_ge(loaded, 16 if gains is None else 32)
            with pe.Fori(0, n_tiles // 2) as i:
                for s in range(2):
                    pe.wait_ge(squared, i * 2 + s + 1)
                    for c in range(chunks):
                        mm = nc.tensor.matmul(total[:, s, c, :width], mats[:, 0, :], square[:, s, c * width:(c + 1) * width],
                                              start=True, stop=True)
                    mm.then_inc(summed, 1)

        @block.vector
        def _(dve):
            dve.wait_ge(loaded, 16 if gains is None else 32)
            dve.sem_inc(out_done, 2)
            with dve.Fori(0, n_tiles // 2) as i:
                for s in range(2):
                    f = i * 2 + s
                    dve.wait_ge(scaled, f + 1)
                    r = root[:, s].rearrange("p c n -> p (c n)")
                    if times is not None:
                        nc.vector.tensor_tensor(r, r, times[:, f, :], ALU.mult).then_inc(step, 1)
                        dve.wait_ge(step, f + 1)
                    nc.vector.scalar_tensor_tensor(tile(f), tile(f), scale if gains is None else gains[:, bass.ds(f, 1)],
                                                   r, ALU.mult, ALU.mult).then_inc(out_done, 1)


class Inverse:

    LAST = LEVELS - 1

    def __init__(self, nc, part, half, flip, x, x_t, part_x, mat, region):
        self.nc, self.half = nc, half
        self.flip, self.x, self.x_t, self.part_x, self.mat, self.region = flip, x, x_t, part_x, mat, region
        self.start_t, self.product, self.masked, self.joined, self.x_ready, self.xt_ready = (
            part.sem("inv_" + n) for n in ("start_t", "product", "masked", "joined", "x_ready", "xt_ready"))

    @staticmethod
    def count(t, per_tile, step, c):
        return t * (2 * per_tile) + (2 * step + c + 1)

    def tensor(self, pe, t):
        nc, L, n = self.nc, self.LAST, self.count
        for c in range(2):
            pe.wait_ge(self.start_t, n(t, 1, 0, c))
            for i, h in enumerate(self.half(c)):
                mm = nc.tensor.transpose(self.region(2, c)[:, i, :], self.x_t[:, h, :], self.mat("ident"))
            mm.then_inc(self.joined, 1)
        for l in range(1, LEVELS):
            for c in range(2):
                pe.wait_ge(self.x_ready, n(t, L, l - 1, c))
                for i, h in enumerate(self.half(c)):
                    mm = nc.tensor.matmul(self.region(1, c)[:, i, :], self.flip[:, h, :], self.x[:, h, :], start=True, stop=True)
                mm.then_inc(self.product, 1)
            for c in range(2):
                pe.wait_ge(self.masked, n(t, L, l - 1, c))
                if l > 1:
                    pe.wait_ge(self.xt_ready, n(t, L, l - 2, c))
                for i, h in enumerate(self.half(c)):
                    if l < L:
                        nc.tensor.matmul(self.region(2, c)[:, i, :], self.x_t[:, h, :], self.part_x[:, h, :], start=True, stop=True)
                    mm = nc.tensor.matmul(self.region(3, c)[:, i, :], self.part_x[:, h, :], self.x_t[:, h, :], start=True, stop=True)
                mm.then_inc(self.joined, 1)

    def scalar(self, act, t):
        for l in range(LEVELS - 1):
            for c in range(2):
                act.wait_ge(self.joined, self.count(t, LEVELS, l, c))
                h = self.half(c)
                self.nc.scalar.activation(self.x[:, h[0]:h[-1] + 1, :], self.region(2, c), ACT.Copy).then_inc(self.x_ready, 1)

    def vector(self, dve, t, meanwhile=None):
        V, L = self.nc.vector, self.LAST
        for c in range(2):
            h = slice(self.half(c)[0], self.half(c)[-1] + 1)
            V.tensor_tensor(self.x_t[:, h, :], self.flip[:, h, :], over_heads(self.mat("join0T"), len(self.half(c))), ALU.mult).then_inc(self.start_t, 1)
        if meanwhile:
            meanwhile()
        for l in range(1, LEVELS):
            for c in range(2):
                h = slice(self.half(c)[0], self.half(c)[-1] + 1)
                dve.wait_ge(self.product, self.count(t, L, l - 1, c))
                V.tensor_tensor(self.part_x[:, h, :], self.region(1, c), over_heads(self.mat(f"join{l}"), len(self.half(c))), ALU.mult).then_inc(self.masked, 1)
            for c in range(2):
                h = slice(self.half(c)[0], self.half(c)[-1] + 1)
                dve.wait_ge(self.joined, self.count(t, LEVELS, l, c))
                V.tensor_copy(self.x_t[:, h, :], self.region(3, c)).then_inc(self.xt_ready, 1)


def delta_rule(nc, dram, act_a, decay, beta):
    H, HH = H_A, H_A // 2
    with Part(nc, "delta", dram) as part:
        names = ["ident", "ones", "upto", "after", "neg_before", "join0T"] + [f"join{l}" for l in range(1, LEVELS)]
        mt = part.sb("mats", [P, len(names), P])
        mat = lambda n: mt[:, names.index(n), :]
        over = lambda n: over_heads(mat(n), HH)
        head = lambda n: part.sb(n, [P, H, P])
        stage = part.sb("stage", [P, 3 * H, P])
        q, k, v = (stage[:, i * H:(i + 1) * H, :] for i in range(3))
        state = head("state")
        gm, dec, eg, pt, dn, flip, x, xt, px, kt, vt = (head(n) for n in (
            "gm", "dec", "eg", "pt", "dn", "flip", "x", "xt", "px", "kt", "vt"))
        gs = part.sb("gs", [P, 2, 3, HH])
        vn, qd = gm, eg
        R = [part.ps(f"r{i}", [P, 8, P]) for i in range(4)]
        r = lambda i, c: R[i][:, 4 * c:4 * c + HH, :]
        small = lambda c: R[0][:, 4 * c + HH, 0:3 * HH].rearrange("p (a h) -> p a h", a=3)
        half = lambda c: range(HH * c, HH * c + HH)
        sl = lambda c: slice(HH * c, HH * c + HH)
        S = {n: part.sem(n) for n in (
            "loaded", "staged", "decays_spread", "segments", "exps", "keys", "flip_ready", "turned", "kt_done",
            "vt_done", "ks", "rhs", "fresh", "fresh_read", "outputs", "grown", "state_done", "d")}
        inv = Inverse(nc, part, half, flip, x, xt, px, mat, r)
        block = part.stack.enter_context(nc.Block())

        def nth(t, c):
            return t * 2 + (c + 1)

        @block.sync
        def _(sp):
            part.load_matrices(sp, mt, names, S["loaded"])
            sp.dma_start(stage[:, :, :], act_a[:, 0:3 * H, 0:P]).then_inc(S["staged"], 16)
            with sp.Fori(1, NT1) as t:
                sp.wait_ge(S["ks"], t * 2)
                sp.dma_start(stage[:, :, :], act_a[:, 0:3 * H, bass.ts(t, P)]).then_inc(S["staged"], 16)

        @block.tensor
        def _(pe):
            M = nc.tensor.matmul
            pe.wait_ge(S["loaded"], 16 * len(names))
            with pe.Fori(0, NT1) as t:
                for c in range(2):
                    pe.wait_ge(S["decays_spread"], nth(t, c))
                    for i, m in ((0, "after"), (1, "ones")):
                        M(r(i, c), mat(m), gm[:, sl(c), :], start=True, stop=True)
                    for i, m in enumerate(("upto", "ones", "after")):
                        mm = M(small(c)[:, i, :], mat(m), decay[:, bass.ds(t, 1), sl(c)].rearrange("p a h -> p (a h)"), start=True, stop=True)
                    mm.then_inc(S["segments"], 1)
                pe.wait_ge(S["staged"], t * 16 + 16)
                for c in range(2):
                    for i, h in enumerate(half(c)):
                        M(r(2, c)[:, i, :], k[:, h, :], k[:, h, :], start=True, stop=True)
                        mm = M(r(3, c)[:, i, :], k[:, h, :], q[:, h, :], start=True, stop=True)
                    mm.then_inc(S["keys"], 1)
                for c in range(2):
                    pe.wait_ge(S["exps"], t * 6 + 3 * c + 3)
                    for i, h in enumerate(half(c)):
                        nc.tensor.transpose(r(0, c)[:, i, :], k[:, h, :], mat("ident"))
                        mm = nc.tensor.transpose(r(1, c)[:, i, :], v[:, h, :], mat("ident"))
                    mm.then_inc(S["turned"], 1)
                for c in range(2):
                    pe.wait_ge(S["vt_done"], nth(t, c))
                    pe.wait_ge(S["flip_ready"], nth(t, c))
                inv.tensor(pe, t)
                for c in range(2):
                    pe.wait_ge(S["kt_done"], nth(t, c))
                    for i, h in enumerate(half(c)):
                        mm = M(r(0, c)[:, i, :], k[:, h, :], state[:, h, :], start=True, stop=True)
                    mm.then_inc(S["ks"], 1)
                for c in range(2):
                    pe.wait_ge(S["rhs"], nth(t, c))
                    pe.wait_ge(inv.xt_ready, inv.count(t, 6, 5, c))
                    for i, h in enumerate(half(c)):
                        mm = M(r(1, c)[:, i, :], xt[:, h, :], px[:, h, :], start=True, stop=True)
                    mm.then_inc(S["fresh"], 1)
                for c in range(2):
                    pe.wait_ge(S["fresh_read"], nth(t, c))
                    for i, h in enumerate(half(c)):
                        mm = M(r(2, c)[:, i, :], kt[:, h, :], vn[:, h, :], start=True, stop=True)
                    mm.then_inc(S["grown"], 1)
                    for i, h in enumerate(half(c)):
                        M(r(0, c)[:, i, :], vn[:, h, :], pt[:, h, :], start=True, stop=False)
                        mm = M(r(0, c)[:, i, :], state[:, h, :], qd[:, h, :], start=False, stop=True)
                    mm.then_inc(S["outputs"], 1)

        @block.scalar
        def _(act):
            A = nc.scalar.activation
            nc.scalar.preload_act_table_set("natural_log_exp_and_others")
            with act.Fori(0, NT1) as t:
                for c in range(2):
                    act.wait_ge(S["segments"], nth(t, c))
                    A(dec[:, sl(c), :], r(0, c), ACT.Exp).then_inc(S["exps"], 1)
                    A(gs[:, c, :, :], small(c), ACT.Exp).then_inc(S["exps"], 1)
                    A(eg[:, sl(c), :], r(1, c), ACT.Exp).then_inc(S["exps"], 1)
                for c in range(2):
                    act.wait_ge(S["turned"], nth(t, c))
                    A(vt[:, sl(c), :], r(1, c), ACT.Copy).then_inc(S["vt_done"], 1)
                inv.scalar(act, t)
                for c in range(2):
                    act.wait_ge(S["outputs"], nth(t, c))
                    A(act_a[:, sl(c), bass.ts(t, P)], r(0, c), ACT.Copy).then_inc(S["state_done"], 1)

        @block.vector
        def _(dve):
            V, T = nc.vector, nc.vector.tensor_tensor
            V.memset(state[:, :, :], 0.0).then_inc(S["state_done"], 2)
            dve.wait_ge(S["state_done"], 2)
            dve.wait_ge(S["loaded"], 16 * len(names))
            K = 12
            with dve.Fori(0, NT1) as t:
                n = [0]

                def then(i):
                    n[0] += 1
                    i.then_inc(S["d"], 1)
                    dve.wait_ge(S["d"], t * K + n[0])
                per_head = lambda a: spread(a, P)
                beta_h = lambda c: per_head(beta[:, bass.ds(t, 1), sl(c)].rearrange("p a h -> p (a h)"))
                decay_h = lambda c: per_head(decay[:, bass.ds(t, 1), sl(c)].rearrange("p a h -> p (a h)"))
                for c in range(2):
                    dve.wait_ge(S["state_done"], nth(t, c))
                    T(gm[:, sl(c), :], over("upto"), decay_h(c), ALU.mult).then_inc(S["decays_spread"], 1)
                for c in range(2):
                    a = sl(c)
                    dve.wait_ge(S["exps"], t * 6 + 3 * c + 3)
                    T(dn[:, a, :], dec[:, a, :], over("neg_before"), ALU.mult)
                    then(T(dec[:, a, :], dec[:, a, :], over("upto"), ALU.mult))
                    then(T(dn[:, a, :], dn[:, a, :], beta_h(c), ALU.mult))
                    dve.wait_ge(S["keys"], nth(t, c))
                    T(pt[:, a, :], r(3, c), dec[:, a, :], ALU.mult)
                    then(T(flip[:, a, :], r(2, c), dn[:, a, :], ALU.mult))
                    T(qd[:, a, :], q[:, a, :], eg[:, a, :], ALU.mult)
                    T(flip[:, a, :], flip[:, a, :], over("ident"), ALU.add).then_inc(S["flip_ready"], 1)
                    dve.wait_ge(S["flip_ready"], nth(t, c))
                inv.vector(dve, t, lambda: [
                    (dve.wait_ge(S["turned"], nth(t, c)),
                     T(kt[:, sl(c), :], r(0, c), per_head(gs[:, c, 2, :]), ALU.mult).then_inc(S["kt_done"], 1)) for c in range(2)])
                for c in range(2):
                    dve.wait_ge(S["ks"], nth(t, c))
                    then(T(px[:, sl(c), :], r(0, c), per_head(gs[:, c, 0, :]), ALU.mult))
                    T(px[:, sl(c), :], vt[:, sl(c), :], px[:, sl(c), :], ALU.subtract).then_inc(S["rhs"], 1)
                for c in range(2):
                    dve.wait_ge(S["fresh"], nth(t, c))
                    T(vn[:, sl(c), :], r(1, c), beta_h(c), ALU.mult).then_inc(S["fresh_read"], 1)
                for c in range(2):
                    a = sl(c)
                    dve.wait_ge(S["outputs"], nth(t, c))
                    then(T(state[:, a, :], state[:, a, :], per_head(gs[:, c, 1, :]), ALU.mult))
                    then(T(state[:, a, :], state[:, a, :], r(2, c), ALU.add))
                assert n[0] == K, n[0]


def rwkv_prepare(nc, dram, b, rate, unit_k):
    F = 4
    with Part(nc, "rwprep", dram) as part:
        a2 = part.sb("a2", [P, D_B])
        w2 = part.sb("w2", [64, D_B])
        w0 = part.sb("w0", [1, D_B])
        mt = part.sb("mats", [P, 1, P])
        par = part.sb("par", [P, 4, F])
        mixk = part.sb("mixk", [P, 2, LIVE])
        lw = part.sb("lw", [P, 2, D_B])
        acc = [part.ps(f"acc{s}", [P, C1, 512]) for s in range(2)]
        dec = part.ps("dec", [P, 2, 512])
        loaded, squashed, product, rate_done, dec_done, dec_read, scaled, stored, mixed, used, step = (part.sem(n) for n in (
            "loaded", "squashed", "product", "rate_done", "dec_done", "dec_read", "scaled", "stored", "mixed", "used", "step"))
        stored = [stored, mixed]
        block = part.stack.enter_context(nc.Block())

        @block.sync
        def _(sp):
            sp.dma_start(a2[64:128, :], dram["rw_a2"][:, :]).then_inc(loaded, 16)
            sp.dma_start(w2[:, :], dram["rw_w2"][:, :]).then_inc(loaded, 16)
            sp.dma_start(w0[:, :], dram["rw_w0"][:, :]).then_inc(loaded, 16)
            for i, n in enumerate(("rw_a0", "rw_k_k", "rw_k_a")):
                sp.dma_start(par[:, i, :], dram[n]).then_inc(loaded, 16)
            part.load_matrices(sp, mt, ["ones"], loaded)
            for t in range(NT1):
                sp.wait_ge(scaled, t + 1)
                sp.dma_start(dram["log_w"][t * P:(t + 1) * P, :], lw[:, t % 2, :]).then_inc(stored[t % 2], 16)
            sp.wait_ge(stored[0], 16 * ((NT1 + 1) // 2))
            sp.wait_ge(stored[1], 16 * (NT1 // 2))

        @block.scalar
        def _(act):
            A = nc.scalar.activation
            act.wait_ge(loaded, 112)
            A(b[0:64, 16, :], b[0:64, 16, :], ACT.Tanh).then_inc(squashed, 1)
            for f in range(F):
                act.wait_ge(product, f + 1)
                A(rate[:, f, S1:].rearrange("p (c n) -> p c n", c=C1), acc[f % 2][:, :, :W1], ACT.Sigmoid,
                  bias=par[:, 0, f:f + 1]).then_inc(rate_done, 1)
            for t in range(NT1):
                act.wait_ge(dec_done, t + 1)
                if t >= 2:
                    act.wait_ge(stored[t % 2], 16 * (t // 2))
                A(lw[:, t % 2, :], dec[:, t % 2, :], ACT.Sigmoid).then_inc(dec_read, 1)
                act.wait_ge(dec_read, t + 1)
                A(lw[:, t % 2, :], lw[:, t % 2, :], ACT.Copy, scale=-math.exp(-0.5)).then_inc(scaled, 1)
            A(b[:, 12:16, :], b[:, 12:16, :], ACT.Silu)

        @block.tensor
        def _(pe):
            M = nc.tensor.matmul
            pe.wait_ge(loaded, 112)
            for f in range(F):
                if f >= 2:
                    pe.wait_ge(rate_done, f - 1)
                for c in range(C1):
                    mm = M(acc[f % 2][:, c, :W1], a2[64:128, f * P:(f + 1) * P],
                           b[64:128, 16, S1 + c * W1:S1 + (c + 1) * W1], start=True, stop=True)
                mm.then_inc(product, 1)
            pe.wait_ge(squashed, 1)
            for t in range(NT1):
                if t >= 2:
                    pe.wait_ge(dec_read, t - 1)
                M(dec[:, t % 2, :], b[0:64, 16, t * P:(t + 1) * P], w2[:, :], start=True, stop=False)
                M(dec[:, t % 2, :], mt[0:1, 0, :], w0[:, :], start=False, stop=True).then_inc(dec_done, 1)

        @block.vector
        def _(dve):
            V = nc.vector
            dve.wait_ge(loaded, 112)
            V.tensor_scalar(par[:, 3, :], par[:, 2, :], -1.0, 1.0, ALU.mult, ALU.add).then_inc(step, 1)
            dve.wait_ge(step, 1)
            for f in range(F):
                dve.wait_ge(rate_done, f + 1)
                V.tensor_scalar(unit_k[:, f, S1:], b[:, 4 + f, S1:], par[:, 1, f:f + 1], None, ALU.mult)
                V.tensor_scalar(mixk[:, f % 2, :], rate[:, f, S1:], par[:, 2, f:f + 1], par[:, 3, f:f + 1],
                                ALU.mult, ALU.add).then_inc(step, 1)
                dve.wait_ge(step, 2 * f + 2)
                V.tensor_tensor(b[:, 4 + f, S1:], b[:, 4 + f, S1:], mixk[:, f % 2, :], ALU.mult).then_inc(step, 1)
                dve.wait_ge(step, 2 * f + 3)


def rwkv(nc, dram, b, rate, unit_k):
    H, F = H_B, 4
    BIG = 1e38
    with Part(nc, "rwkv", dram) as part:
        names = ["ident", "upto_mid", "before_mid", "mid", "upto", "before", "join0T"] + \
                [f"join{l}" for l in range(1, LEVELS)]
        mt = part.sb("mats", [P, len(names), P])
        mat = lambda n: mt[:, names.index(n), :]
        over = lambda n: over_heads(mat(n), H // 2)
        lw, vst, bt, kt, e1, e2, e3 = (part.sb(n, [P, F, P]) for n in (
            "lw", "vst", "bt", "kt", "e1", "e2", "e3"))
        rz, az = (part.sb(n, [P, F, 2, P]) for n in ("rz", "az"))
        flip, x, xt, px, ak, pb, pk = (part.sb(n, [P, H, P]) for n in ("flip", "x", "xt", "px", "ak", "pb", "pk"))
        tok = part.sb("tok", [P, 3, F, P])
        em = part.sb("em", [P, F])
        state, hm = (part.sb(n, [P, F, 64]) for n in ("state", "hm"))
        rhs, u = e2, e3
        heads = lambda a: a.rearrange("p f (e c) -> p (f e) c", e=2)
        R = [part.ps(f"r{i}", [P, 8, P]) for i in range(4)]
        r = lambda i, c: R[i][:, 4 * c:4 * c + 4, :]
        half = lambda c: range(4 * c, 4 * c + 4)
        hs = lambda c: slice(4 * c, 4 * c + 4)
        pairs = lambda c: range(2 * c, 2 * c + 2)
        fs = lambda c: slice(2 * c, 2 * c + 2)
        S = {n: part.sem(n) for n in (
            "loaded", "staged", "start", "decays", "exps", "scaled_in", "scores", "scores_read",
            "turned", "tokens", "hm_done", "rhs_done", "rhs_read", "u_done", "u_read", "outputs",
            "grown", "stored", "state_done", "d")}
        inv = Inverse(nc, part, half, flip, x, xt, px, mat, r)
        block = part.stack.enter_context(nc.Block())

        def nth(t, c):
            return t * 2 + (c + 1)

        def stage(sp, t):
            sp.dma_start(lw[:, :, :].rearrange("p f c -> p (f c)"), dram["log_w"][bass.ts(t, P), :]).then_inc(S["staged"], 16)
            sp.dma_start(vst[:, :, :], b[:, 8:12, bass.ts(t, P)]).then_inc(S["staged"], 16)

        @block.sync
        def _(sp):
            part.load_matrices(sp, mt, names, S["loaded"])
            stage(sp, 0)
            with sp.Fori(1, NT1) as t:
                sp.wait_ge(S["turned"], t * 2)
                stage(sp, t)

        @block.tensor
        def _(pe):
            M = nc.tensor.matmul
            pe.wait_ge(S["loaded"], 16 * len(names))
            with pe.Fori(0, NT1) as t:
                pe.wait_ge(S["staged"], t * 32 + 32)
                for c in range(2):
                    pe.wait_ge(S["state_done"], nth(t, c))
                    for i, f in enumerate(pairs(c)):
                        M(r(0, c)[:, i, :], lw[:, f, :], mat("upto_mid"), start=True, stop=True)
                        M(r(0, c)[:, 2 + i, :], lw[:, f, :], mat("before_mid"), start=True, stop=True)
                        mm = M(r(1, c)[:, 0, i:i + 1], lw[:, f, :], mat("mid")[:, 0:1], start=True, stop=True)
                    mm.then_inc(S["decays"], 1)
                for c in range(2):
                    pe.wait_ge(S["scaled_in"], nth(t, c))
                    for p, f in enumerate(pairs(c)):
                        for i, (l, right) in enumerate(((bt, az), (kt, az), (bt, rz), (kt, rz))):
                            mm = M(r(i, c)[:, 2 * p:2 * p + 2, :], l[:, f, :], right[:, f, :, :], start=True, stop=True)
                    mm.then_inc(S["scores"], 1)
                for c in range(2):
                    pe.wait_ge(S["scores_read"], nth(t, c))
                    for i, f in enumerate(pairs(c)):
                        nc.tensor.transpose(r(0, c)[:, i, :], vst[:, f, :], mat("ident"))
                        nc.tensor.transpose(r(0, c)[:, 2 + i, :], bt[:, f, :], mat("ident"))
                        mm = nc.tensor.transpose(r(1, c)[:, i, :], kt[:, f, :], mat("ident"))
                    mm.then_inc(S["turned"], 1)
                for c in range(2):
                    pe.wait_ge(S["tokens"], t * 4 + (2 * c + 2))
                inv.tensor(pe, t)
                for c in range(2):
                    pe.wait_ge(S["hm_done"], nth(t, c))
                    out = heads(r(0, c)[:, 0:2, :])
                    for i, h in enumerate(half(c)):
                        M(out[:, i, :], az[:, h // 2, h % 2, :], hm[:, h // 2, :], start=True, stop=False)
                        mm = M(out[:, i, :], ak[:, h, :], heads(tok[:, 0])[:, h, :], start=False, stop=True)
                    mm.then_inc(S["rhs_done"], 1)
                for c in range(2):
                    pe.wait_ge(S["rhs_read"], nth(t, c))
                    pe.wait_ge(inv.xt_ready, inv.count(t, 6, 5, c))
                    out = heads(r(1, c)[:, 0:2, :])
                    for i, h in enumerate(half(c)):
                        mm = M(out[:, i, :], xt[:, h, :], heads(rhs[:, :, :])[:, h, :], start=True, stop=True)
                    mm.then_inc(S["u_done"], 1)
                for c in range(2):
                    pe.wait_ge(S["u_read"], nth(t, c))
                    for i, f in enumerate(pairs(c)):
                        M(r(3, c)[:, i, :], tok[:, 1, f, :], u[:, f, :], start=True, stop=False)
                        mm = M(r(3, c)[:, i, :], tok[:, 2, f, :], tok[:, 0, f, :], start=False, stop=True)
                    mm.then_inc(S["grown"], 1)
                    for i, h in enumerate(half(c)):
                        o = r(2, c)[(h % 2) * 64:(h % 2) * 64 + 64, i // 2, :]
                        M(o, heads(u[:, :, :])[:, h, :], pb[:, h, :], start=True, stop=False)
                        M(o, heads(tok[:, 0])[:, h, :], pk[:, h, :], start=False, stop=False)
                        mm = M(o, hm[:, h // 2, :], rz[:, h // 2, h % 2, :], start=False, stop=True)
                    mm.then_inc(S["outputs"], 1)

        @block.scalar
        def _(act):
            nc.scalar.preload_act_table_set("natural_log_exp_and_others")
            A = nc.scalar.activation
            with act.Fori(0, NT1) as t:
                for c in range(2):
                    act.wait_ge(S["decays"], nth(t, c))
                    A(e1[:, fs(c), :], r(0, c)[:, 0:2, :], ACT.Exp).then_inc(S["exps"], 1)
                    A(e3[:, fs(c), :], r(0, c)[:, 0:2, :], ACT.Exp, scale=-1.0).then_inc(S["exps"], 1)
                    A(e2[:, fs(c), :], r(0, c)[:, 2:4, :], ACT.Exp).then_inc(S["exps"], 1)
                    A(em[:, fs(c)], r(1, c)[:, 0, 0:2], ACT.Exp).then_inc(S["exps"], 1)
                for c in range(2):
                    act.wait_ge(S["turned"], nth(t, c))
                    A(tok[:, 0:2, fs(c), :], r(0, c).rearrange("p (a f) c -> p a f c", a=2), ACT.Copy).then_inc(S["tokens"], 1)
                    A(tok[:, 2, fs(c), :], r(1, c)[:, 0:2, :], ACT.Copy).then_inc(S["tokens"], 1)
                inv.scalar(act, t)
                for c in range(2):
                    act.wait_ge(S["rhs_done"], nth(t, c))
                    A(rhs[:, fs(c), :], r(0, c)[:, 0:2, :], ACT.Copy).then_inc(S["rhs_read"], 1)
                for c in range(2):
                    act.wait_ge(S["u_done"], nth(t, c))
                    A(u[:, fs(c), :], r(1, c)[:, 0:2, :], ACT.Copy).then_inc(S["u_read"], 1)
                for c in range(2):
                    act.wait_ge(S["outputs"], nth(t, c))
                    act.wait_ge(S["state_done"], nth(t, c) + 2)
                    A(unit_k[:, fs(c), bass.ts(t, P)], r(2, c)[:, 0:2, :], ACT.Copy).then_inc(S["stored"], 1)

        @block.vector
        def _(dve):
            V, T, STT = nc.vector, nc.vector.tensor_tensor, nc.vector.scalar_tensor_tensor
            K = 12
            V.memset(rz[:, :, :, :], 0.0)
            V.memset(az[:, :, :, :], 0.0)
            V.memset(state[:, :, :], 0.0).then_inc(S["state_done"], 2)
            dve.wait_ge(S["state_done"], 2)
            dve.wait_ge(S["loaded"], 16 * len(names))
            with dve.Fori(0, NT1) as t:
                n = [0]

                def then(i):
                    n[0] += 1
                    i.then_inc(S["d"], 1)
                    dve.wait_ge(S["d"], t * K + n[0])
                at = bass.ts(t, P)
                for c in range(2):
                    a, k2 = fs(c), b[:, 4 + 2 * c:6 + 2 * c, at]
                    dve.wait_ge(S["exps"], t * 8 + (4 * c + 4))
                    T(bt[:, a, :], unit_k[:, a, at], e3[:, a, :], ALU.mult).then_inc(S["d"], 1)
                    n[0] += 1
                    for e in range(2):
                        part_e = slice(64 * e, 64 * e + 64)
                        T(rz[part_e, a, e, :], b[part_e, fs(c), at], e1[part_e, a, :], ALU.mult)
                        STT(az[part_e, a, e, :], unit_k[part_e, a, at], -1.0, e2[part_e, a, :], ALU.mult, ALU.mult)
                    dve.wait_ge(S["d"], t * K + n[0])
                    T(kt[:, a, :], k2, e3[:, a, :], ALU.mult)
                    T(bt[:, a, :], bt[:, a, :], rate[:, a, at], ALU.mult).then_inc(S["scaled_in"], 1)
                    T(hm[:, a, :], state[:, a, :], spread(em[:, a], 64), ALU.mult).then_inc(S["hm_done"], 1)
                for c in range(2):
                    a = hs(c)
                    dve.wait_ge(S["scores"], nth(t, c))
                    then(STT(flip[:, a, :], r(0, c), BIG, over("before"), ALU.min, ALU.mult))
                    then(T(flip[:, a, :], flip[:, a, :], over("ident"), ALU.add))
                    STT(ak[:, a, :], r(1, c), BIG, over("before"), ALU.min, ALU.mult)
                    STT(pb[:, a, :], r(2, c), BIG, over("upto"), ALU.min, ALU.mult)
                    STT(pk[:, a, :], r(3, c), BIG, over("upto"), ALU.min, ALU.mult).then_inc(S["scores_read"], 1)
                dve.wait_ge(S["scores_read"], t * 2 + 2)
                inv.vector(dve, t)
                for c in range(2):
                    a = fs(c)
                    dve.wait_ge(S["grown"], nth(t, c))
                    for e in range(2):
                        part_e = slice(64 * e, 64 * e + 64)
                        then(T(state[part_e, a, :], hm[part_e, a, :], r(3, c)[part_e, 0:2, part_e], ALU.add))
                    T(state[:, a, :], state[:, a, :], e1[:, a, P - 1:P].to_broadcast([P, 2, 64]), ALU.mult).then_inc(S["d"], 1)
                    n[0] += 1
                    dve.wait_ge(S["d"], t * K + n[0])
                    dve.sem_inc(S["state_done"], 1)
                assert n[0] == K, n[0]


def rwkv_finish(nc, dram, b, out):
    F = 4
    with Part(nc, "rwend", dram) as part:
        names = ["head_mean", "head_ones"]
        mt = part.sb("mats", [P, 2, P])
        par = part.sb("par", [P, 3, F])
        rk, sq = (part.sb(n, [P, 2, LIVE]) for n in ("rk", "sq"))
        ps = [part.ps(f"ps{s}", [P, C1, 512]) for s in range(2)]
        cut = lambda a: a.rearrange("p (c n) -> p c n", c=C1)
        loaded, products, means, bonuses, bonus_used, centred, squared, sums, logged, roots, d, stored = (part.sem(n) for n in (
            "loaded", "products", "means", "bonuses", "bonus_used", "centred", "squared", "sums", "logged", "roots", "d", "stored"))
        block = part.stack.enter_context(nc.Block())
        tile = lambda a, f: a[:, f, S1:]

        @block.sync
        def _(sp):
            part.load_matrices(sp, mt, names, loaded)
            for i, n in enumerate(("rw_r_k", "rw_ln_w", "rw_ln_b")):
                sp.dma_start(par[:, i, :], dram[n]).then_inc(loaded, 16)

        @block.tensor
        def _(pe):
            def product(m, f, right, sem):
                for c in range(C1):
                    mm = nc.tensor.matmul(ps[f % 2][:, c, :W1], mt[:, m, :], right[:, c * W1:(c + 1) * W1], start=True, stop=True)
                mm.then_inc(sem, 1)
            pe.wait_ge(loaded, 80)
            for f0 in range(0, F, 2):
                for f in (f0, f0 + 1):
                    if f >= 2:
                        pe.wait_ge(logged, f - 1)
                    product(0, f, tile(out, f), means)
                for f in (f0, f0 + 1):
                    pe.wait_ge(products, f + 1)
                    pe.wait_ge(centred, f + 1)
                    product(1, f, rk[:, f % 2, :], bonuses)
                for f in (f0, f0 + 1):
                    pe.wait_ge(squared, f + 1)
                    pe.wait_ge(bonus_used, f + 1)
                    product(0, f, sq[:, f % 2, :], sums)

        @block.scalar
        def _(act):
            nc.scalar.preload_act_table_set("natural_log_exp_and_others")
            A = nc.scalar.activation
            for f0 in range(0, F, 2):
                for f in (f0, f0 + 1):
                    act.wait_ge(centred, f + 1)
                    A(sq[:, f % 2, :], tile(out, f), ACT.Square).then_inc(squared, 1)
                for f in (f0, f0 + 1):
                    act.wait_ge(sums, f + 1)
                    A(cut(sq[:, f % 2, :]), ps[f % 2][:, :, :W1], ACT.Ln, bias=GN_EPS).then_inc(logged, 1)
                    act.wait_ge(logged, f + 1)
                    A(sq[:, f % 2, :], sq[:, f % 2, :], ACT.Exp, scale=-0.5).then_inc(roots, 1)

        @block.vector
        def _(dve):
            T, STT = nc.vector.tensor_tensor, nc.vector.scalar_tensor_tensor
            n = [0]

            def then(i):
                n[0] += 1
                i.then_inc(d, 1)
                dve.wait_ge(d, n[0])
            dve.wait_ge(loaded, 80)
            for f0 in range(0, F, 2):
                for f in (f0, f0 + 1):
                    STT(rk[:, f % 2, :], tile(b, f), par[:, 0, f:f + 1], tile(b, 4 + f), ALU.mult, ALU.mult).then_inc(products, 1)
                for f in (f0, f0 + 1):
                    dve.wait_ge(means, f + 1)
                    T(cut(tile(out, f)), cut(tile(out, f)), ps[f % 2][:, :, :W1], ALU.subtract).then_inc(centred, 1)
                for f in (f0, f0 + 1):
                    dve.wait_ge(bonuses, f + 1)
                    T(cut(rk[:, f % 2, :]), cut(tile(b, 8 + f)), ps[f % 2][:, :, :W1], ALU.mult).then_inc(bonus_used, 1)
                for f in (f0, f0 + 1):
                    o = tile(out, f)
                    dve.wait_ge(roots, f + 1)
                    then(STT(o, o, par[:, 1, f:f + 1], sq[:, f % 2, :], ALU.mult, ALU.mult))
                    dve.wait_ge(bonus_used, f + 1)
                    then(STT(o, o, par[:, 2, f:f + 1], rk[:, f % 2, :], ALU.add, ALU.add))
                    then(T(o, o, tile(b, 12 + f), ALU.mult))


def clear(nc, dram, name, *where):
    with Part(nc, name, dram) as part:
        block = part.stack.enter_context(nc.Block())

        @block.gpsimd
        def _(pool):
            for w in where:
                nc.gpsimd.memset(w, 0.0)


def copy_out(nc, dram, name, to, what):
    with Part(nc, name, dram) as part:
        moved = part.sem("moved")
        block = part.stack.enter_context(nc.Block())

        @block.sync
        def _(sp):
            sp.dma_start(to, what).then_inc(moved, 16)
            sp.wait_ge(moved, 16)


def mamba(nc, dram, c_in, decay, dt):
    H, G, F = H_C, G_C, D_C // P
    with Part(nc, "mamba", dram) as part:
        groups = [f"group{a}{b}" for a in range(3) for b in range(3) if abs(a - b) < 2]
        names = ["ident", "ones", "upto", "after"] + groups
        mt = part.sb("mats", [P, len(names), P])
        mat = lambda n: mt[:, names.index(n), :]
        par = part.sb("par", [P, 2, F])
        stage = part.sb("stage", [P, 14, P])
        xs, bs, cs = stage[:, 0:6, :], stage[:, 6:10, :], stage[:, 10:14, :]
        gm, dec, pt = (part.sb(n, [P, H, P]) for n in ("gm", "dec", "pt"))
        cd = gm
        y, sq, skip, rs = (part.sb(n, [P, F, P]) for n in ("y", "sq", "skip", "rs"))
        xdt, xdd, state = (part.sb(n, [P, H, DH_C]) for n in ("xdt", "xdd", "state"))
        btok = part.sb("btok", [P, G, P])
        gs = part.sb("gs", [P, 2, H])
        bank = [part.ps(f"bank{i}", [P, n, 512]) for i, n in ((0, 3), (3, 2), (5, 2), (7, 1))]
        flat = lambda a: a.rearrange("p b (s c) -> p (b s) c", c=P)
        seg, ys, cb = flat(bank[0]), flat(bank[1]), flat(bank[3])
        small = bank[2][:, 1, 0:2 * H].rearrange("p (a h) -> p a h", a=2)
        grow = bank[2][:, :, :].rearrange("p b (s c) -> p (b s) c", c=256)[:, :, 0:192]
        S = {n: part.sem(n) for n in (
            "loaded", "staged", "stage_used", "turn", "decays_spread", "segments", "exps", "cb_done",
            "dec_read", "turned", "bt_done", "x_done", "ready", "outputs", "grown", "squared", "sums",
            "logs", "roots", "gated", "stored", "d")}
        block = part.stack.enter_context(nc.Block())
        n_loads = 16 * (len(names) + 2)

        @block.sync
        def _(sp):
            part.load_matrices(sp, mt, names, S["loaded"])
            sp.dma_start(par[:, 0, :], dram["mb_D"]).then_inc(S["loaded"], 16)
            sp.dma_start(par[:, 1, :], dram["mb_norm"]).then_inc(S["loaded"], 16)
            with sp.Fori(0, NT1) as t:
                sp.wait_ge(S["stage_used"], t + 1)
                sp.dma_start(stage[:, :, :], c_in[:, 6:20, bass.ts(t, P)]).then_inc(S["staged"], 16)
                sp.wait_ge(S["gated"], t * 2 + 2)
                sp.dma_start(dram["mix"].rearrange("(f p) t -> p f t", p=P)[:, 10:16, bass.ts(t, P)], y[:, :, :]).then_inc(S["stored"], 16)
            sp.wait_ge(S["stored"], 16 * NT1 + 16)

        @block.tensor
        def _(pe):
            M = nc.tensor.matmul
            pe.wait_ge(S["loaded"], n_loads)
            with pe.Fori(0, NT1) as t:
                pe.wait_ge(S["decays_spread"], t + 1)
                for b in range(3):
                    M(seg[:, 4 * b:4 * b + 4, :], mat("after"), gm[:, 4 * b:4 * b + 4, :], start=True, stop=True)
                for b in range(2):
                    M(ys[:, 4 * b:4 * b + 4, :], mat("ones"), gm[:, 4 * b:4 * b + 4, :], start=True, stop=True)
                M(flat(bank[2])[:, 0:4, :], mat("ones"), gm[:, 8:12, :], start=True, stop=True)
                for i, m in enumerate(("ones", "after")):
                    mm = M(small[:, i, :], mat(m), decay[:, bass.ds(t, 1), H_A:].rearrange("p a h -> p (a h)"), start=True, stop=True)
                mm.then_inc(S["segments"], 1)
                pe.wait_ge(S["staged"], t * 16 + 16)
                for g in range(G):
                    mm = M(cb[:, g, :], bs[:, g, :], cs[:, g, :], start=True, stop=True)
                mm.then_inc(S["cb_done"], 1)
                pe.wait_ge(S["exps"], t * 4 + 4)
                for f in range(F):
                    nc.tensor.transpose(seg[:, f, :], xs[:, f, :], mat("ident"))
                for g in range(G):
                    mm = nc.tensor.transpose(seg[:, 8 + g, :], bs[:, g, :], mat("ident"))
                mm.then_inc(S["turned"], 1)
                pe.wait_ge(S["bt_done"], t + 1)
                pe.wait_ge(S["ready"], t + 1)
                for h in range(H):
                    o = ys[(h % 2) * 64:(h % 2) * 64 + 64, h // 2, :]
                    M(o, xdt[:, h, :], pt[:, h, :], start=True, stop=False)
                    mm = M(o, state[:, h, :], cd[:, h, :], start=False, stop=True)
                mm.then_inc(S["outputs"], 1)
                for g in range(G):
                    mm = M(grow[:, g, :], btok[:, g, :], xdd[:, 3 * g:3 * g + 3, :], start=True, stop=True)
                mm.then_inc(S["grown"], 1)
                pe.wait_ge(S["squared"], t + 1)
                for m in range(3):
                    near = [f for f in range(3) if abs(f - m) < 2]
                    for f in near:
                        mm = M(bank[0][:, m, 0:256], mat(f"group{f}{m}"),
                               sq[:, :, :].rearrange("p (a f) c -> p a f c", a=2)[:, :, f, :],
                               start=(f == near[0]), stop=(f == near[-1]))
                mm.then_inc(S["sums"], 1)

        @block.scalar
        def _(act):
            nc.scalar.preload_act_table_set("natural_log_exp_and_others")
            A = nc.scalar.activation
            with act.Fori(0, NT1) as t:
                act.wait_ge(S["segments"], t + 1)
                act.wait_ge(S["turn"], t + 1)
                A(dec[:, :, :], seg, ACT.Exp).then_inc(S["exps"], 1)
                A(cd[:, 0:8, :], ys, ACT.Exp).then_inc(S["exps"], 1)
                A(cd[:, 8:12, :], flat(bank[2])[:, 0:4, :], ACT.Exp).then_inc(S["exps"], 1)
                A(gs[:, :, :], small, ACT.Exp).then_inc(S["exps"], 1)
                act.wait_ge(S["turned"], t + 1)
                A(btok[:, :, :], seg[:, 8:12, :], ACT.Copy).then_inc(S["bt_done"], 1)
                act.wait_ge(S["gated"], t * 2 + 1)
                A(sq[:, :, :], y[:, :, :], ACT.Square).then_inc(S["squared"], 1)
                act.wait_ge(S["sums"], t + 1)
                rs3 = rs[:, :, :].rearrange("p (m a) c -> p m (a c)", m=3)
                A(rs3, bank[0][:, :, 0:256], ACT.Ln, bias=NORM_EPS).then_inc(S["logs"], 1)
                act.wait_ge(S["logs"], t + 1)
                A(rs3, rs3, ACT.Exp, scale=-0.5).then_inc(S["roots"], 1)

        @block.vector
        def _(dve):
            V, T = nc.vector, nc.vector.tensor_tensor
            K = 9
            V.memset(state[:, :, :], 0.0).then_inc(S["turn"], 1)
            dve.sem_inc(S["stage_used"], 1)
            dve.sem_inc(S["stored"], 16)
            dve.wait_ge(S["loaded"], n_loads)
            with dve.Fori(0, NT1) as t:
                n = [0]

                def then(i):
                    n[0] += 1
                    i.then_inc(S["d"], 1)
                    dve.wait_ge(S["d"], t * K + n[0])
                row = lambda a: a.rearrange("p a h -> p (a h)")
                dve.wait_ge(S["turn"], t + 1)
                T(gm[:, :, :], over_heads(mat("upto"), H), spread(row(decay[:, bass.ds(t, 1), H_A:]), P), ALU.mult).then_inc(S["decays_spread"], 1)
                dve.wait_ge(S["staged"], t * 16 + 16)
                T(skip[:, :, :], xs, spread(par[:, 0, :], P), ALU.mult)
                dve.wait_ge(S["exps"], t * 4 + 4)
                then(T(dec[:, :, :], dec[:, :, :], over_heads(mat("upto"), H), ALU.mult))
                grouped = lambda a: a.rearrange("p (g e) c -> p g e c", g=G)
                by_group = lambda a: a.unsqueeze(2).to_broadcast([P, G, H // G, P])
                T(grouped(cd[:, :, :]), grouped(cd[:, :, :]), by_group(cs), ALU.mult)
                dve.wait_ge(S["cb_done"], t + 1)
                T(grouped(pt[:, :, :]), by_group(cb), grouped(dec[:, :, :]), ALU.mult)
                dve.wait_ge(S["turned"], t + 1)
                then(T(xdt[:, :, :], seg[:, 0:6, :].rearrange("p f (e c) -> p (f e) c", e=2), spread(row(dt[:, bass.ds(t, 1), :]), DH_C), ALU.mult))
                then(T(xdd[:, :, :], xdt[:, :, :], spread(gs[:, 1, :], DH_C), ALU.mult))
                dve.sem_inc(S["ready"], 1)
                dve.wait_ge(S["outputs"], t + 1)
                dve.wait_ge(S["stored"], t * 16 + 16)
                then(T(y[:, :, :], ys[:, 0:6, :], skip[:, :, :], ALU.add))
                then(T(y[:, :, :], y[:, :, :], c_in[:, 0:6, bass.ts(t, P)], ALU.mult))
                dve.sem_inc(S["gated"], 1)
                dve.wait_ge(S["grown"], t + 1)
                then(T(state[:, :, :], state[:, :, :], spread(gs[:, 0, :], DH_C), ALU.mult))
                then(T(state[:, :, :].rearrange("p (g e) c -> p g (e c)", g=G), state[:, :, :].rearrange("p (g e) c -> p g (e c)", g=G), grow, ALU.add))
                dve.wait_ge(S["roots"], t + 1)
                turned = y[:, :, :].rearrange("p (a m) c -> p m a c", a=2)
                then(T(turned, turned, rs[:, :, :].rearrange("p (m a) c -> p m a c", m=3), ALU.mult))
                then(T(y[:, :, :], y[:, :, :], spread(par[:, 1, :], P), ALU.mult))
                dve.sem_inc(S["gated"], 1)
                dve.sem_inc(S["stage_used"], 1)
                dve.sem_inc(S["turn"], 1)
                assert n[0] == K, n[0]


W_CONV = 512
HEADS2 = 8
DFF = 4096
EPS = 1e-6


def by_tokens(nc, dram, name, src, weights, col0, n, dst, func):
    with Part(nc, name, dram) as part:
        w = part.sb("w", [P, KD, n])
        acc = part.ps("acc", [P, 4, 512])
        loaded, product, read = (part.sem(x) for x in ("loaded", "product", "read"))
        block = part.stack.enter_context(nc.Block())

        @block.sync
        def _(sp):
            sp.dma_start(w[:, :, :], weights.rearrange("(k p) c -> p k c", p=P)[:, :, col0:col0 + n]).then_inc(loaded, 16)

        @block.tensor
        def _(pe):
            pe.wait_ge(loaded, 16)
            for t in range(NT):
                if t >= 4:
                    pe.wait_ge(read, t - 3)
                for k in range(KD):
                    mm = nc.tensor.matmul(acc[:, t % 4, :n], src[:, k, t * P:(t + 1) * P], w[:, k, :],
                                          start=(k == 0), stop=(k == KD - 1))
                mm.then_inc(product, 1)

        @block.scalar
        def _(act):
            for t in range(NT):
                act.wait_ge(product, t + 1)
                nc.scalar.activation(dst[:, t, :], acc[:, t % 4, :n], func).then_inc(read, 1)


def gated_conv(nc, dram, b, c, u, dst):
    F, N = 4, SEQ
    with Part(nc, "gconv", dram) as part:
        taps = part.sb("taps", [P, 3, F])
        v = part.sb("v", [P, 2, 2 + N])
        loaded, step = part.sem("loaded"), part.sem("step")
        block = part.stack.enter_context(nc.Block())

        @block.sync
        def _(sp):
            sp.dma_start(taps[:, :, :], dram["conv_w_2"]).then_inc(loaded, 16)

        @block.vector
        def _(dve):
            V, n = nc.vector, [0]

            def then(i):
                n[0] += 1
                i.then_inc(step, 1)
                dve.wait_ge(step, n[0])
            dve.wait_ge(loaded, 16)
            then(V.memset(v[:, :, 0:2], 0.0))
            for f in range(F):
                s, out = f % 2, dst[:, f, :]
                then(V.tensor_tensor(v[:, s, 2:], c[:, f, :], u[:, f, :], ALU.mult))
                then(V.tensor_scalar(out, v[:, s, 2:], taps[:, 2, f:f + 1], None, ALU.mult))
                then(V.scalar_tensor_tensor(out, v[:, s, 1:1 + N], taps[:, 1, f:f + 1], out, ALU.mult, ALU.add))
                then(V.scalar_tensor_tensor(out, v[:, s, 0:N], taps[:, 0, f:f + 1], out, ALU.mult, ALU.add))
                then(V.tensor_tensor(out, out, b[:, f, :], ALU.mult))


def stick_breaking(nc, dram, qk, v, dst):
    PAIRS, QC = HEADS2 // 2, SEQ // 512
    units = [(qc, kt, e) for qc in range(QC) for kt in range(4 * qc + 3, -1, -1) for e in range(2)]
    U, SL = len(units), 4

    def span(u):
        qc, kt, _ = units[u]
        return max(kt * P - qc * 512, 0), kt >= 4 * qc
    first = lambda u: units[u][1] == 4 * units[u][0] + 3
    last = lambda u: units[u][1] == 0
    runs = lambda u: sum(not last(w) for w in range(u + 1))
    RU = runs(U - 1)
    with Part(nc, "stick", dram) as part:
        names = ["neg_from", "neg_ones", "before", "zeros"]
        mt = part.sb("mats", [P, len(names), P])
        mat = lambda n: mt[:, names.index(n), :]
        k = part.sb("k", [P, SEQ])
        vs = part.sb("vs", [P, NT, P])
        qz = part.sb("qz", [P, 2, SEQ])
        ex, soft, att = (part.sb(n, [P, SL, 512]) for n in ("ex", "soft", "att"))
        run = part.sb("run", [P, 2, 512])
        score = part.ps("score", [P, SL, 512])
        out = part.ps("out", [P, 4, 512])
        S = {n: part.sem(n) for n in (
            "loaded", "staged", "stage_used", "zeroed", "q_ready", "z_done", "absd", "expd", "logd", "soft_done",
            "summed", "weighed", "masked", "run_done", "applied", "out_read", "d")}
        block = part.stack.enter_context(nc.Block())
        n_diag = sum(span(u)[1] for u in range(U))

        @block.sync
        def _(sp):
            part.load_matrices(sp, mt, names, S["loaded"])
            with sp.Fori(0, PAIRS) as i:
                sp.wait_ge(S["stage_used"], i + 1)
                sp.dma_start(k[:, :], qk[:, bass.ds(i + 4, 1), :].rearrange("p a n -> p (a n)")).then_inc(S["staged"], 16)
                sp.dma_start(vs[:, :, :], v[:, :, bass.ts(i, P)]).then_inc(S["staged"], 16)

        @block.tensor
        def _(pe):
            M = nc.tensor.matmul
            pe.wait_ge(S["loaded"], 16 * len(names))
            with pe.Fori(0, PAIRS) as i:
                def scores(u):
                    qc, kt, e = units[u]
                    o, _ = span(u)
                    if u >= SL:
                        pe.wait_ge(S["weighed"], i * U + u - SL + 1)
                    M(score[:, u % SL, o:], k[:, kt * P:(kt + 1) * P], qz[:, e, qc * 512 + o:(qc + 1) * 512],
                      start=True, stop=True).then_inc(S["z_done"], 1)
                pe.wait_ge(S["staged"], i * 32 + 32)
                pe.wait_ge(S["q_ready"], i + 1)
                pe.wait_ge(S["out_read"], i + 1)
                for e in range(2):
                    for qc in range(QC):
                        M(out[64 * e:64 * e + 64, 2 * e + qc, :], mat("zeros")[:, 0:64], qz[:, e, qc * 512:(qc + 1) * 512],
                          start=True, stop=True)
                scores(0)
                scores(1)

                def apply(u):
                    qc, kt, e = units[u]
                    o, _ = span(u)
                    if span(u)[1]:
                        pe.wait_ge(S["masked"], i * n_diag + sum(span(w)[1] for w in range(u + 1)))
                    else:
                        pe.wait_ge(S["weighed"], i * U + u + 1)
                    M(out[64 * e:64 * e + 64, 2 * e + qc, o:], vs[:, kt, 64 * e:64 * e + 64], att[:, u % SL, o:],
                      start=False, stop=True, skip_group_check=True).then_inc(S["applied"], 1)
                for u in range(U):
                    if u + 2 < U:
                        scores(u + 2)
                    o, _ = span(u)
                    pe.wait_ge(S["soft_done"], i * U + u + 1)
                    mm = M(score[:, u % SL, o:], mat("neg_from"), soft[:, u % SL, o:], start=False, stop=True,
                           skip_group_check=True)
                    if not first(u):
                        pe.wait_ge(S["run_done"], i * RU + runs(u - 2))
                        mm = M(score[:, u % SL, o:], mat("neg_ones"), run[:, units[u][2], o:], start=False, stop=True,
                               skip_group_check=True)
                    mm.then_inc(S["summed"], 1)
                    if u >= 1:
                        apply(u - 1)
                apply(U - 1)

        @block.scalar
        def _(act):
            nc.scalar.preload_act_table_set("natural_log_exp_and_others")
            A = nc.scalar.activation
            with act.Fori(0, PAIRS) as i:
                def softplus(u):
                    o, _ = span(u)
                    act.wait_ge(S["z_done"], i * U + u + 1)
                    if u >= SL:
                        act.wait_ge(S["run_done"], i * RU + runs(u - SL))
                        act.wait_ge(S["summed"], i * U + u - SL + 1)
                    A(ex[:, u % SL, o:], score[:, u % SL, o:], ACT.Abs).then_inc(S["absd"], 1)
                    act.wait_ge(S["absd"], i * U + u + 1)
                    A(ex[:, u % SL, o:], ex[:, u % SL, o:], ACT.Exp, scale=-1.0).then_inc(S["expd"], 1)
                    act.wait_ge(S["expd"], i * U + u + 1)
                    A(soft[:, u % SL, o:], ex[:, u % SL, o:], ACT.Ln, bias=1.0).then_inc(S["logd"], 1)

                def weigh(u):
                    o, _ = span(u)
                    act.wait_ge(S["summed"], i * U + u + 1)
                    if u >= SL:
                        act.wait_ge(S["applied"], i * U + u - SL + 1)
                    A(att[:, u % SL, o:], score[:, u % SL, o:], ACT.Exp).then_inc(S["weighed"], 1)
                softplus(0)
                for u in range(U):
                    if u + 1 < U:
                        softplus(u + 1)
                    weigh(u)

        @block.gpsimd
        def _(pool):
            pool.wait_ge(S["loaded"], 16 * len(names))
            with pool.Fori(0, PAIRS) as i:
                for u in range(U):
                    e, (o, _) = units[u][2], span(u)
                    if last(u):
                        continue
                    pool.wait_ge(S["soft_done"], i * U + u + 1)
                    pool.wait_ge(S["summed"], i * U + u + 1)
                    r = run[:, e, :]
                    if first(u):
                        nc.gpsimd.tensor_tensor(r[:, o:], soft[:, u % SL, o:], mat("zeros"), ALU.add)
                        nc.gpsimd.memset(r[:, 0:o], 0.0).then_inc(S["run_done"], 1)
                    else:
                        nc.gpsimd.tensor_tensor(r[:, o:], r[:, o:], soft[:, u % SL, o:], ALU.add).then_inc(S["run_done"], 1)
                    pool.wait_ge(S["run_done"], i * RU + runs(u))

        @block.vector
        def _(dve):
            V, T = nc.vector, nc.vector.tensor_tensor
            V.memset(qz[:, :, :], 0.0).then_inc(S["zeroed"], 1)
            dve.wait_ge(S["zeroed"], 1)
            dve.wait_ge(S["loaded"], 16 * len(names))
            dve.sem_inc(S["stage_used"], 1)
            dve.sem_inc(S["out_read"], 1)
            with dve.Fori(0, PAIRS) as i:
                for e in range(2):
                    half = slice(64 * e, 64 * e + 64)
                    q = V.tensor_scalar(qz[half, e, :], qk[half, bass.ds(i, 1), :].rearrange("p a n -> p (a n)"), 0.125, None, ALU.mult)
                q.then_inc(S["q_ready"], 1)

                def soft_of(u):
                    o, diag = span(u)
                    s = soft[:, u % SL, :]
                    dve.wait_ge(S["logd"], i * U + u + 1)
                    a = V.scalar_tensor_tensor(s[:, o:], score[:, u % SL, o:], 0.0, s[:, o:], ALU.max, ALU.add)
                    if diag:
                        a.then_inc(S["d"], 1)
                        dve.wait_ge(S["d"], i * n_diag + sum(span(w)[1] for w in range(u + 1)))
                        a = T(s[:, o:o + P], s[:, o:o + P], mat("before"), ALU.mult)
                    a.then_inc(S["soft_done"], 1)

                def mask_of(u):
                    o, diag = span(u)
                    if diag:
                        dve.wait_ge(S["weighed"], i * U + u + 1)
                        a = att[:, u % SL, o:o + P]
                        T(a, a, mat("before"), ALU.mult).then_inc(S["masked"], 1)
                soft_of(0)
                for u in range(U):
                    if u + 1 < U:
                        soft_of(u + 1)
                    mask_of(u)
                dve.wait_ge(S["applied"], i * U + U)
                for e in range(2):
                    half = slice(64 * e, 64 * e + 64)
                    c = V.tensor_copy(dst[half, bass.ds(i + 4, 1), :].rearrange("p a (q n) -> p (a q) n", n=512),
                                      out[half, 2 * e:2 * e + 2, :])
                c.then_inc(S["out_read"], 1)
                dve.sem_inc(S["stage_used"], 1)


def turn_rows(nc, dram, name, rows_in, n, dst):
    with Part(nc, name, dram) as part:
        ident = part.sb("ident", [P, 1, P])
        rows = part.sb("rows", [P, NT, n])
        cross = part.ps("cross", [P, 4, n // P, P])
        loaded, turned, moved = (part.sem(x) for x in ("loaded", "turned", "moved"))
        block = part.stack.enter_context(nc.Block())

        @block.sync
        def _(sp):
            part.load_matrices(sp, ident, ["ident"], loaded)
            sp.dma_start(rows[:, :, :], rows_in.rearrange("(t p) d -> p t d", p=P)).then_inc(loaded, 16)

        @block.tensor
        def _(pe):
            pe.wait_ge(loaded, 32)
            for t in range(0, NT):
                if t >= 2:
                    pe.wait_ge(moved, t - 1)
                for k in range(n // P):
                    mm = nc.tensor.transpose(cross[:, 2 * (t % 2), k, :], rows[:, t, k * P:(k + 1) * P], ident[:, 0, :])
                mm.then_inc(turned, 1)

        @block.vector
        def _(dve):
            for t in range(NT):
                dve.wait_ge(turned, t + 1)
                nc.vector.tensor_copy(dst[:, :, t * P:(t + 1) * P], cross[:, 2 * (t % 2)]).then_inc(moved, 1)


def second_block(nc, dram, hid):
    full = dict(src0=0, chunks=C2, width=W2)
    with Part(nc, "s2", dram) as p:
        mix = p.sb("mix", [P, KD, SEQ])
        with Part(nc, "s2a", dram) as a:
            conv = a.sb("conv", [P, KD, SEQ])
            v = a.sb("v", [P, NT, 512])
            with Part(nc, "s2b", dram) as b:
                m = b.sb("m", [P, KD, SEQ])
                normalise(nc, dram, "n2", hid, 0, dram["g_mix_2"], C2, W2, m, scratch=[conv[:, 0:KD, 0:W2], conv[:, 0:KD, W2:SEQ]])
                by_tokens(nc, dram, "p2v", m, dram["w_in_2"], 2560, 512, v, ACT.Copy)
                m_hi = b.sb("m_hi", [P, KD, SEQ])
                project(nc, dram, "p2c", m, 0, dram["w_in_2"], 0, KD, 8, C2, W2, conv, 0, 0, "copy", hi=m_hi)
                project(nc, dram, "p2d", m, 0, dram["w_in_2"], 1024, KD, 4, C2, W2, mix, 0, 4, "copy", hi=m_hi, split_already=True)
                gated_conv(nc, dram, conv[:, 0:4], conv[:, 4:8], mix[:, 4:8], mix)
                unit(nc, dram, "u2c", mix, 0, 4, "head_mean", dram["g_conv_out_2"], **full)
                project(nc, dram, "p2q", m, 0, dram["w_in_2"], 1536, KD, 8, C2, W2, conv, 0, 0, "copy", hi=m_hi, split_already=True)
            stick_breaking(nc, dram, conv, v, mix)
            unit(nc, dram, "u2a", mix, 4, 4, "head_mean", dram["g_attn_out_2"], **full)
        mix_hi = p.sb("mix_hi", [P, KD, SEQ])
        project(nc, dram, "p2o", mix, 0, dram["w_out_2"], 0, KD, 8, C2, W2, hid, 0, 0, "add", hi=mix_hi)
    feed_forward(nc, dram, "2", hid, dram["g_mlp_2"], dram["w_up_2"], dram["w_down_2"])
    with Part(nc, "s2g", dram) as p:
        gate = p.sb("gate", [P, KD, SEQ])
        m, m_hi = (p.sb(n, [P, KD, SEQ]) for n in ("m", "m_hi"))
        pt = p.sb("pt", [P, 2, SEQ])
        normalise(nc, dram, "n2g", hid, 0, dram["g_ple_2"], C2, W2, m)
        project(nc, dram, "p2g", m, 0, dram["w_ple_gate_2"], 0, KD, 8, C2, W2, gate, 0, 0, "sigmoid", hi=m_hi)
        turn_rows(nc, dram, "t2", dram["p_2"], 256, pt)
        project(nc, dram, "p2p", pt, 0, dram["w_ple_proj_2"], 0, 2, 8, C2, W2, hid, 0, 0, "gate_add", {"gate": gate}, hi=m_hi)
    normalise(nc, dram, "n2f", hid, 0, dram["g_final_2"], C2, W2, hid)


def feed_forward(nc, dram, n, hid, gain, up, down):
    G = KD
    GROUPS = DFF // P // G
    STEPS = 2 * G
    with Part(nc, "ff" + n, dram) as p:
        m, m_hi, inner, inner_hi = (p.sb(x, [P, KD, SEQ]) for x in ("m", "m_hi", "inner", "inner_hi"))
        normalise(nc, dram, "nf" + n, hid, 0, gain, C2, W2, m,
                  scratch=[inner[:, :, 0:W2], inner[:, :, W2:SEQ]])
        with Part(nc, "ffp" + n, dram) as part:
            w, w_hi = (part.sb(x, [P, 2, KD, P]) for x in ("w", "w_hi"))
            acc = [part.ps(f"acc{s}", [P, C2, W2]) for s in range(2)]
            w_loaded = [part.sem(f"w_loaded{s}") for s in range(2)]
            w_rounded, w_split, m_rounded, m_split, product_done, acc_free, rectified, inner_rounded, inner_split = (
                part.sem(x) for x in ("w_rounded", "w_split", "m_rounded", "m_split", "product_done", "acc_free",
                                      "rectified", "inner_rounded", "inner_split"))
            block = part.stack.enter_context(nc.Block())
            up_view, down_view = (x.rearrange("(k p) c -> p k c", p=P) for x in (up, down))
            cut = lambda a: a.rearrange("p (c n) -> p c n", c=C2)

            def steps(eng, up_step, down_step):
                for g in range(GROUPS):
                    for body, base in ((up_step, g * STEPS), (down_step, g * STEPS + G)):
                        final = 2 if base + G == GROUPS * STEPS else 0
                        with eng.Fori(0, (G - final) // 2) as i:
                            for s in range(2):
                                body(g, i * 2 + s, i * 2 + (base + s), s, True)
                        for f in range(G - final, G):
                            body(g, f, base + f, f % 2, f < G - 1)

            @block.sync
            def _(sp):
                def load(view, n, s):
                    sp.wait_ge(product_done, n + 1)
                    sp.dma_start(w[:, s], view).then_inc(w_loaded[s], 16)
                steps(sp, lambda g, f, n, s, more: load(up_view[:, :, bass.ds(f * P + g * G * P, P)], n, s),
                      lambda g, f, n, s, more: load(down_view[:, g * G:(g + 1) * G, bass.ds(f * P, P)], n, s))

            @block.tensor
            def _(pe):
                pe.sem_inc(product_done, 2)

                def multiply(n, s, src, src_hi, wait):
                    pe.wait_ge(w_split, n + 1)
                    pe.wait_ge(acc_free, n + 1)
                    for c in range(C2):
                        at = slice(c * W2, (c + 1) * W2)
                        for k in range(KD):
                            if c == 0:
                                wait(k)
                            for i, (a, b) in enumerate(((w_hi, src_hi), (w, src_hi), (w_hi, src))):
                                mm = nc.tensor.matmul(acc[s][:, c, :], rounded(a[:, s, k, :]), rounded(b[:, k, at]),
                                                      start=(k == 0 and i == 0), stop=(k == KD - 1 and i == 2))
                    mm.then_inc(product_done, 1)
                steps(pe, lambda g, f, n, s, more: multiply(n, s, m, m_hi, lambda k: pe.wait_ge(m_split, k + 1)),
                      lambda g, f, n, s, more: multiply(n, s, inner, inner_hi, lambda k: pe.wait_ge(inner_split, g * G + k + 1)))

            def round_weights(act, n, s):
                act.wait_ge(w_loaded[s], n * 8 + (16 - 8 * s))
                act.wait_ge(product_done, n + 1)
                nc.scalar.activation(rounded(w_hi[:, s]), w[:, s], ACT.Copy).then_inc(w_rounded, 1)

            @block.scalar
            def _(act):
                A = nc.scalar.activation
                for k in range(KD):
                    A(rounded(m_hi[:, k, :]), m[:, k, :], ACT.Copy).then_inc(m_rounded, 1)
                    if k == 1:
                        round_weights(act, 0, 0)

                def ahead(n, s, more):
                    if more:
                        round_weights(act, n + 1, 1 - s)

                def up_step(g, f, n, s, more):
                    ahead(n, s, more)
                    act.wait_ge(product_done, n + 3)
                    A(cut(inner[:, f, :]), acc[s][:, :, :], ACT.Relu).then_inc(rectified, 1)
                    act.wait_ge(acc_free, n + 3)
                    A(rounded(inner_hi[:, f, :]), inner[:, f, :], ACT.Copy).then_inc(inner_rounded, 1)
                steps(act, up_step, lambda g, f, n, s, more: ahead(n, s, more))

            @block.vector
            def _(dve):
                V, T = nc.vector, nc.vector.tensor_tensor

                def split_weights(n, s):
                    dve.wait_ge(w_rounded, n + 1)
                    T(rounded(w[:, s]), w[:, s], rounded(w_hi[:, s]), ALU.subtract).then_inc(w_split, 1)
                dve.sem_inc(acc_free, 2)
                for k in range(KD):
                    dve.wait_ge(m_rounded, k + 1)
                    T(rounded(m[:, k, :]), m[:, k, :], rounded(m_hi[:, k, :]), ALU.subtract).then_inc(m_split, 1)
                    if k == 1:
                        split_weights(0, 0)

                def up_step(g, f, n, s, more):
                    split_weights(n + 1, 1 - s)
                    done = f + (g * G + 1)
                    dve.wait_ge(rectified, done)
                    T(cut(inner[:, f, :]), cut(inner[:, f, :]), acc[s][:, :, :], ALU.mult).then_inc(acc_free, 1)
                    dve.wait_ge(inner_rounded, done)
                    T(rounded(inner[:, f, :]), inner[:, f, :], rounded(inner_hi[:, f, :]), ALU.subtract).then_inc(inner_split, 1)

                def down_step(g, f, n, s, more):
                    if more:
                        split_weights(n + 1, 1 - s)
                    dve.wait_ge(product_done, n + 3)
                    T(cut(hid[:, f, :]), cut(hid[:, f, :]), acc[s][:, :, :], ALU.add).then_inc(acc_free, 1)
                steps(dve, up_step, down_step)


def spatial_gate(nc, dram, sv, su, dst):
    G = 4
    with Part(nc, "sgu", dram) as part:
        ident = part.sb("ident", [P, 1, P])
        ws = part.sb("ws", [P, G, P])
        wt = part.sb("wt", [P, G, P])
        bs = part.sb("bs", [P, G, P])
        gain = part.sb("gain", [P, G])
        sq = part.sb("sq", [P, 32, P])
        ss = part.sb("ss", [P, 32])
        acc = part.ps("acc", [P, 4, NT, P])
        loaded, turned, moved, squared, summed, rooted, ready, mixed, read, step = (part.sem(x) for x in (
            "loaded", "turned", "moved", "squared", "summed", "rooted", "ready", "mixed", "read", "step"))
        block = part.stack.enter_context(nc.Block())
        svg = sv[:, :, :].rearrange("p t (g c) -> p (t g) c", g=G)

        @block.sync
        def _(sp):
            part.load_matrices(sp, ident, ["ident"], loaded)
            sp.dma_start(ws[:, :, :], dram["w_s_3"].rearrange("g p q -> p g q")).then_inc(loaded, 16)
            sp.dma_start(bs[:, :, :].rearrange("p g q -> p (g q)"), dram["b_s_3"].to_broadcast([P, 512])).then_inc(loaded, 16)
            sp.dma_start(gain[:, :], dram["sgu_norm_g_3"]).then_inc(loaded, 16)

        @block.tensor
        def _(pe):
            pe.wait_ge(loaded, 64)
            for g in range(G):
                mm = nc.tensor.transpose(acc[:, 0, g, :], ws[:, g, :], ident[:, 0, :])
            mm.then_inc(turned, 1)
            pe.wait_ge(moved, 1)
            pe.wait_ge(ready, 1)
            for g in range(G):
                for t in range(NT):
                    mm = nc.tensor.matmul(acc[:, g, t, :], sv[:, t, g * P:(g + 1) * P], wt[:, g, :], start=True, stop=True)
                mm.then_inc(mixed, 1)

        @block.scalar
        def _(act):
            nc.scalar.preload_act_table_set("natural_log_exp_and_others")
            nc.scalar.activation(sq[:, :, :], svg, ACT.Square).then_inc(squared, 1)
            act.wait_ge(turned, 1)
            nc.scalar.activation(wt[:, :, :], acc[:, 0, 0:4, :], ACT.Copy).then_inc(moved, 1)
            act.wait_ge(summed, 1)
            nc.scalar.activation(ss[:, :], ss[:, :], ACT.Ln, scale=1.0 / P, bias=EPS).then_inc(step, 1)
            act.wait_ge(step, 1)
            nc.scalar.activation(ss[:, :], ss[:, :], ACT.Exp, scale=-0.5).then_inc(rooted, 1)

        @block.vector
        def _(dve):
            V = nc.vector
            dve.wait_ge(squared, 1)
            V.tensor_reduce(ss[:, :], sq[:, :, :], mybir.AxisListType.X, ALU.add).then_inc(summed, 1)
            dve.wait_ge(rooted, 1)
            V.tensor_tensor(svg, svg, spread(ss[:, :], P), ALU.mult).then_inc(ready, 1)
            dve.wait_ge(loaded, 64)
            for g in range(G):
                dve.wait_ge(mixed, g + 1)
                o = dst[:, 4 + g, :].rearrange("p (t c) -> p t c", c=P)
                V.scalar_tensor_tensor(o, acc[:, g], gain[:, g:g + 1], over_heads(bs[:, g, :], NT), ALU.mult, ALU.add).then_inc(read, 1)
                dve.wait_ge(read, g + 1)
                V.tensor_tensor(dst[:, 4 + g, :], dst[:, 4 + g, :], su[:, g, :], ALU.mult)


def gla_decays(nc, dram, low, la):
    C, NCH = 64, SEQ // 64
    with Part(nc, "gdec", dram) as part:
        ones = part.sb("ones", [P, 1, P])
        w2 = part.sb("w2", [32, 512])
        bias = part.sb("bias", [1, 512])
        t = part.sb("t", [C, 2, 512])
        acc = part.ps("acc", [C, 2, 512])
        loaded, zeroed, product, absd, expd, logd, read, done = (part.sem(x) for x in (
            "loaded", "zeroed", "product", "absd", "expd", "logd", "read", "done"))
        block = part.stack.enter_context(nc.Block())

        @block.sync
        def _(sp):
            part.load_matrices(sp, ones, ["ones"], loaded)
            sp.wait_ge(zeroed, 1)
            sp.dma_start(w2[0:16, 0:256], dram["w_a2_fwd_3"]).then_inc(loaded, 16)
            sp.dma_start(w2[16:32, 256:512], dram["w_a2_bwd_3"]).then_inc(loaded, 16)
            sp.dma_start(bias[:, :], dram["b_a_3"]).then_inc(loaded, 16)

        @block.tensor
        def _(pe):
            pe.wait_ge(loaded, 64)
            for c in range(NCH):
                if c >= 2:
                    pe.wait_ge(read, c - 1)
                nc.tensor.matmul(acc[:, c % 2, :], low[0:32, 0, c * C:(c + 1) * C], w2[:, :], start=True, stop=False)
                nc.tensor.matmul(acc[:, c % 2, :], ones[0:1, 0, 0:C], bias[:, :], start=False, stop=True).then_inc(product, 1)

        @block.scalar
        def _(act):
            nc.scalar.preload_act_table_set("natural_log_exp_and_others")
            A = nc.scalar.activation
            for c in range(NCH):
                act.wait_ge(product, c + 1)
                if c >= 2:
                    act.wait_ge(read, c - 1)
                A(t[:, c % 2, :], acc[:, c % 2, :], ACT.Abs).then_inc(absd, 1)
                act.wait_ge(absd, c + 1)
                A(t[:, c % 2, :], t[:, c % 2, :], ACT.Exp, scale=-1.0).then_inc(expd, 1)
                act.wait_ge(expd, c + 1)
                A(t[:, c % 2, :], t[:, c % 2, :], ACT.Ln, bias=1.0).then_inc(logd, 1)

        @block.vector
        def _(dve):
            V = nc.vector
            V.memset(w2[:, :], 0.0).then_inc(zeroed, 1)
            for c in range(NCH):
                dve.wait_ge(logd, c + 1)
                V.scalar_tensor_tensor(la[:, c, :], acc[:, c % 2, :], 0.0, t[:, c % 2, :], ALU.min, ALU.subtract).then_inc(read, 1)
                dve.wait_ge(read, c + 1)
                V.tensor_scalar(la[:, c, :], la[:, c, :], 1.0 / 16.0, None, ALU.mult)


def gla(nc, dram, qk, v, la, osum, scratch):
    C, H, F = 64, 4, 2
    ends = (C - 1, 0)
    with Part(nc, "gla", dram) as part:
        names = ["ident", "mid64", "upto_mid64", "upto", "from_mid64", "after"]
        mt = part.sb("mats", [P, len(names), P])
        shift = [mt[0:C, 2 + 2 * d, 0:C] for d in range(2)]
        mid = [mt[0:C, 1, d:d + 1] for d in range(2)]
        keep = [mt[0:C, 3 + 2 * d, 0:C] for d in range(2)]
        both = lambda n, shape: [part.sb(f"{n}{d}", shape) for d in range(2)]
        las = both("las", [C, 2, 256])
        vs = [scratch[0:C, 2 * d:2 * d + 2, 0:512] for d in range(2)]
        e1, e3, kt = (both(n, [P, F, C]) for n in ("e1", "e3", "kt"))
        em = both("em", [P, F])
        qz = both("qz", [P, F, 2, C])
        state, sm = (both(n, [P, F, P]) for n in ("state", "sm"))
        at = both("at", [C, H, C])
        ktok = both("ktok", [C, F, P])
        bank = [part.ps(f"bank{i}", [P, 512]) for i in range(8)]
        E = [bank[4 * d][:, 0:F * C].rearrange("p (f c) -> p f c", f=F) for d in range(2)]
        mids = [bank[4 * d][:, F * C:F * C + F] for d in range(2)]
        kx = [bank[4 * d][0:C, F * P:2 * F * P].rearrange("p (f c) -> p f c", f=F) for d in range(2)]
        sc = [bank[4 * d + 1][0:C, 0:H * C].rearrange("p (h c) -> p h c", h=H) for d in range(2)]
        out = [bank[4 * d + 2][:, 0:H * C].rearrange("p (h c) -> p h c", h=H) for d in range(2)]
        grow = [bank[4 * d + 3][:, :].rearrange("p (f c) -> p f c", f=F) for d in range(2)]
        loaded = part.sem("loaded")
        S = [{n: part.sem(f"{n}{d}") for n in (
            "staged0", "staged1", "stage_used", "turn", "decays", "exps", "scaled_in", "turned", "at_done",
            "ktok_done", "outputs", "d")} for d in range(2)]
        block = part.stack.enter_context(nc.Block())

        def turns(eng, *steps):
            with eng.Fori(0, NT) as i:
                for j in range(2):
                    for step in steps:
                        step(0, i, j, j, i * 2 + j)
                        step(1, (i - (NT - 1)) * (-1), 1 - j, j, i * 2 + j)

        @block.sync
        def _(sp):
            part.load_matrices(sp, mt, names, loaded)

            def load(d, t, s, slot, n):
                sp.wait_ge(S[d]["stage_used"], n + 1)
                sp.dma_start(las[d][:, slot, :], la[:, bass.ds(t * 2 + s, 1), 256 * d:256 * d + 256].rearrange("p a c -> p (a c)")).then_inc(S[d][f"staged{slot}"], 16)
                sp.dma_start(vs[d][:, slot, :], v[64 * s:64 * s + 64, bass.ds(t, 1), :].rearrange("p a c -> p (a c)")).then_inc(S[d][f"staged{slot}"], 16)
            turns(sp, load)

        @block.tensor
        def _(pe):
            M = nc.tensor.matmul
            pe.wait_ge(loaded, 16 * len(names))

            def decays(d, t, s, slot, n):
                pe.wait_ge(S[d][f"staged{slot}"], n * 16 + (32 - 16 * slot))
                for f in range(F):
                    M(E[d][:, f, :], las[d][:, slot, f * P:(f + 1) * P], shift[d], start=True, stop=True)
                    mm = M(mids[d][:, f:f + 1], las[d][:, slot, f * P:(f + 1) * P], mid[d], start=True, stop=True)
                mm.then_inc(S[d]["decays"], 1)

            def scores(d, t, s, slot, n):
                pe.wait_ge(S[d]["scaled_in"], n + 1)
                for f in range(F):
                    M(sc[d][:, 2 * f:2 * f + 2, :], kt[d][:, f, :], qz[d][:, f, :, :], start=True, stop=True)
                for f in range(F):
                    mm = nc.tensor.transpose(kx[d][:, f, :], kt[d][:, f, :], mt[:, 0, :])
                mm.then_inc(S[d]["turned"], 1)

            def outputs(d, t, s, slot, n):
                vc = vs[d][:, slot, :]
                pe.wait_ge(S[d]["at_done"], n + 1)
                for h in range(H):
                    M(out[d][:, h, :], vc[:, h * P:(h + 1) * P], at[d][:, h, :], start=True, stop=False)
                    M(out[d][:, h, :], sm[d][:, h // 2, :], qz[d][:, h // 2, h % 2, :], start=False, stop=True)
                pe.wait_ge(S[d]["ktok_done"], n + 1)
                for f in range(F):
                    mm = M(grow[d][:, f, :], ktok[d][:, f, :], vc[:, f * 256:(f + 1) * 256], start=True, stop=True)
                mm.then_inc(S[d]["outputs"], 1)
            turns(pe, decays, scores, outputs)

        @block.scalar
        def _(act):
            A = nc.scalar.activation
            nc.scalar.preload_act_table_set("natural_log_exp_and_others")

            def exps(d, t, s, slot, n):
                act.wait_ge(S[d]["decays"], n + 1)
                act.wait_ge(S[d]["turn"], n + 1)
                A(e1[d][:, :, :], E[d], ACT.Exp).then_inc(S[d]["exps"], 1)
                A(e3[d][:, :, :], E[d], ACT.Exp, scale=-1.0).then_inc(S[d]["exps"], 1)
                A(em[d][:, :], mids[d], ACT.Exp).then_inc(S[d]["exps"], 1)

            def keys(d, t, s, slot, n):
                act.wait_ge(S[d]["turned"], n + 1)
                A(ktok[d][:, :, :], kx[d], ACT.Copy).then_inc(S[d]["ktok_done"], 1)
            turns(act, exps, keys)

        @block.vector
        def _(dve):
            V, T = nc.vector, nc.vector.tensor_tensor
            for d in range(2):
                V.memset(qz[d][:, :, :, :], 0.0)
                V.memset(state[d][:, :, :], 0.0)
                V.memset(osum[:, 2 * d:2 * d + 2, :], 0.0).then_inc(S[d]["turn"], 1)
                dve.wait_ge(S[d]["turn"], 1)
                dve.sem_inc(S[d]["stage_used"], 2)
            dve.wait_ge(loaded, 16 * len(names))

            def scaled(d, t, s, slot, n):
                tok = bass.ds(t * P + s * C, C)
                dve.wait_ge(S[d]["exps"], n * 3 + 3)
                for e in range(2):
                    half = slice(64 * e, 64 * e + 64)
                    V.scalar_tensor_tensor(qz[d][half, :, e, :], qk[half, 0:2, tok], 0.125, e1[d][half, :, :], ALU.mult, ALU.mult)
                T(kt[d][:, :, :], qk[:, 2:4, tok], e3[d][:, :, :], ALU.mult).then_inc(S[d]["scaled_in"], 1)
                T(sm[d][:, :, :], state[d][:, :, :], spread(em[d][:, :], P), ALU.mult).then_inc(S[d]["d"], 1)

            def masked(d, t, s, slot, n):
                dve.wait_ge(S[d]["turned"], n + 1)
                dve.wait_ge(S[d]["d"], n * 4 + 1)
                T(at[d][:, :, :], sc[d], over_heads(keep[d], H), ALU.mult).then_inc(S[d]["at_done"], 1)

            def grown(d, t, s, slot, n):
                tok = bass.ds(t * P + s * C, C)
                dve.wait_ge(S[d]["outputs"], n + 1)
                dve.sem_inc(S[d]["stage_used"], 1)
                for e in range(2):
                    half = slice(64 * e, 64 * e + 64)
                    i = T(state[d][half, :, :], sm[d][half, :, :], grow[d][half, :, e * P:(e + 1) * P], ALU.add)
                i.then_inc(S[d]["d"], 1)
                T(osum[:, :, tok], osum[:, :, tok], out[d], ALU.add).then_inc(S[d]["d"], 1)
                dve.wait_ge(S[d]["d"], n * 4 + 3)
                end = e1[d][:, :, ends[d]:ends[d] + 1].to_broadcast([P, F, P])
                T(state[d][:, :, :], state[d][:, :, :], end, ALU.mult).then_inc(S[d]["d"], 1)
                dve.wait_ge(S[d]["d"], n * 4 + 4)
                dve.sem_inc(S[d]["turn"], 1)
            turns(dve, scaled, masked, grown)


def third_block(nc, dram, hid):
    full = dict(src0=0, chunks=C2, width=W2)
    w = dram["w_in_3"]
    with Part(nc, "s3", dram) as p:
        mix = p.sb("mix", [P, KD, SEQ])
        su = p.sb("su", [P, 4, SEQ])
        sv = p.sb("sv", [P, NT, 512])
        v = p.sb("v", [P, NT, 512])
        qk = p.sb("qk", [P, 4, SEQ])
        g = p.sb("g", [P, 4, SEQ])
        low = p.sb("low", [P, 1, SEQ])
        with Part(nc, "s3m", dram) as q:
            m = q.sb("m", [P, KD, SEQ])
            normalise(nc, dram, "n3", hid, 0, dram["norm_mix_g_3"], 4, 256, m)
            by_tokens(nc, dram, "p3v", m, w, 512, 512, v, ACT.Copy)
            by_tokens(nc, dram, "p3s", m, w, 2080, 512, sv, ACT.Gelu)
            project(nc, dram, "p3q", m, 0, w, 0, KD, 4, C2, W2, qk, 0, 0, "copy", hi=mix)
            project(nc, dram, "p3g", m, 0, w, 1024, KD, 4, C2, W2, g, 0, 0, "silu", hi=mix, split_already=True)
            project(nc, dram, "p3a", m, 0, w, 1536, KD, 1, C2, W2, low, 0, 0, "copy", hi=mix, split_already=True)
            project(nc, dram, "p3u", m, 0, w, 1568, KD, 4, C2, W2, su, 0, 0, "gelu", hi=mix, split_already=True)
        spatial_gate(nc, dram, sv, su, mix)
        with Part(nc, "s3l", dram) as q:
            la = q.sb("la", [64, SEQ // 64, 512])
            gla_decays(nc, dram, low, la)
            gla(nc, dram, qk, v, la, mix[:, 0:4, :], su)
        unit(nc, dram, "u3", mix, 0, 4, "mean", dram["gla_norm_g_3"], times=g, **full)
        mix_hi = p.sb("mix_hi", [P, KD, SEQ])
        project(nc, dram, "p3o", mix, 0, dram["w_out_3"], 0, KD, 8, C2, W2, hid, 0, 0, "add", hi=mix_hi)
    feed_forward(nc, dram, "3", hid, dram["norm_mlp_g_3"], dram["w_mlp1_3"], dram["w_mlp2_3"])
    normalise(nc, dram, "n3f", hid, 0, dram["final_norm_g_3"], C2, W2, hid)


def rows_of(a):
    return a.rearrange("(f p) t -> p f t", p=P)


def first_block(nc, dram):
    w = dram["w_in"]
    with Part(nc, "b1", dram) as p:
        decay = p.sb("decay", [P, NT1, H_A + H_C])
        beta = p.sb("beta", [P, NT1, H_A])
        dt = p.sb("dt", [P, NT1, H_C])
        pool = p.sb("pool", [P, 25, T1])
        with Part(nc, "b1h", dram) as q:
            hn = q.sb("hn", [P, KD, T1])
            rows = pool[:, KD:2 * KD].rearrange("p a t -> p (a t)").rearrange("p (t d) -> p t d", d=D)
            entry(nc, dram, pool[:, 0:KD], rows)
            copy_out(nc, dram, "keep", dram["hidden"].rearrange("(k p) t -> p k t", p=P), pool[:, 0:KD, T1 - SEQ:])
            normalise(nc, dram, "n1", pool[:, 0:KD], S1, dram["norm_pre"], C1, W1, hn)
            clear(nc, dram, "c1", pool[:, :, :S1], hn[:, :, :S1])
            gates(nc, dram, hn, decay, beta, dt)
            project(nc, dram, "pa", hn, S1, w, 0, KD, 18, C1, W1, pool, S1, 0, "conv", {"taps": dram["dn_conv"]})
            project(nc, dram, "pz", hn, S1, w, 18 * P, KD, 6, C1, W1, pool, S1, 18, "silu_gain", {"gain": dram["dn_norm"]})
            unit(nc, dram, "uq", pool, 0, 6, "ones", DH_A ** -0.5)
            unit(nc, dram, "uk", pool, 6, 6, "ones", 1.0)
            delta_rule(nc, dram, pool[:, 0:18], decay, beta)
            unit(nc, dram, "uo", pool, 0, 6, "mean", 1.0, times=pool[:, 18:24, S1:])
            copy_out(nc, dram, "oa", rows_of(dram["mix"])[:, 0:6, S1:], pool[:, 0:6, S1:])
            project(nc, dram, "pc", hn, S1, w, P_A + P_B, KD, 6, C1, W1, pool, S1, 0, "silu")
            project(nc, dram, "pd", hn, S1, w, P_A + P_B + D_C, KD, 14, C1, W1, pool, S1, 6, "conv",
                    {"taps": dram["mb_conv"], "bias": dram["mb_conv_b"]})
            mamba(nc, dram, pool, decay, dt)
            clear(nc, dram, "c3", pool[:, :, :S1])
            project(nc, dram, "pb", hn, S1, w, P_A, KD, 17, C1, W1, pool, S1, 0, "shift", {"mu": dram["rw_mu"]})
        b, rate, unit_k = pool[:, 0:17], pool[:, 17:21], pool[:, 21:25]
        rwkv_prepare(nc, dram, b, rate, unit_k)
        unit(nc, dram, "uu", unit_k, 0, 4, "head_ones", 1.0)
        rwkv(nc, dram, b, rate, unit_k)
        rwkv_finish(nc, dram, b, unit_k)
        copy_out(nc, dram, "ob", rows_of(dram["mix"])[:, 6:10, S1:], unit_k[:, :, S1:])


def first_out(nc, dram, hid):
    with Part(nc, "b1o", dram) as p:
        mix, mix_hi, o = (p.sb(n, [P, KD, SEQ]) for n in ("mix", "mix_hi", "o"))
        copy_out(nc, dram, "ldh", hid[:, :, :], dram["hidden"].rearrange("(k p) t -> p k t", p=P))
        for half in range(2):
            copy_out(nc, dram, f"ldm{half}", mix[:, :, :], rows_of(dram["mix"])[:, half * KD:(half + 1) * KD, T1 - SEQ:])
            project(nc, dram, f"p1o{half}", mix, 0, dram["w_out"][half * D:(half + 1) * D, :], 0, KD, 8, C2, W2, o, 0, 0,
                    "add" if half else "copy", hi=mix_hi)
        normalise(nc, dram, "n1o", o, 0, dram["norm_post"], 4, 256, hid, add=True)


def program(nc, dram, out):
    dram["hidden"] = nc.dram_tensor("hidden", (D, SEQ), F32, kind="Internal").ap()
    dram["mix"] = nc.dram_tensor("mix", (2 * D, T1), F32, kind="Internal").ap()
    dram["log_w"] = nc.dram_tensor("log_w", (T1, D_B), F32, kind="Internal").ap()
    first_block(nc, dram)
    with Part(nc, "all", dram) as p:
        hid = p.sb("hid", [P, KD, SEQ])
        first_out(nc, dram, hid)
        second_block(nc, dram, hid)
        third_block(nc, dram, hid)
        leave(nc, dram, hid, out)


def pack(inputs):
    f = {k: np.asarray(v) for k, v in inputs.items()}
    cols = lambda v: np.ascontiguousarray(v.reshape(-1, P).T)
    taps = lambda v: np.ascontiguousarray(v.reshape(v.shape[0], -1, P).transpose(2, 0, 1))
    m = constant_matrices()
    d = {"matrices": np.concatenate([m[n] for n in NAMES]), "x": f["x"], "meta_tokens": f["meta_tokens"],
         "w_in": f["w_in"][0], "w_out": f["w_out"][0],
         "dn_conv": taps(f["dn_conv"][0]), "mb_conv": taps(f["mb_conv"][0]), "conv_w_2": taps(f["conv_w_2"][0]),
         "gate_bias": np.concatenate([f["dn_dt_bias"], f["mb_dt_bias"]], 1),
         "gate_log": np.concatenate([f["dn_A_log"], f["mb_A_log"]], 1),
         "g_final_2": cols(f["g_final_2"]), "final_norm_g_3": cols(f["final_norm_g_3"]),
         "mb_D": cols(np.repeat(f["mb_D"][0], DH_C)), "rw_w0": f["rw_w0"],
         "p_2": f["p_2"][0, 0], "b_s_3": f["b_s_3"].reshape(1, -1),
         "b_a_3": np.concatenate([f["b_a_fwd_3"], f["b_a_bwd_3"]], 1)}
    d["dn_norm"] = cols(np.tile(f["dn_norm"][0], H_A))
    for n in ("norm_pre", "norm_post", "mb_conv_b", "rw_mu", "rw_a0", "rw_k_k", "rw_k_a", "rw_r_k",
              "rw_ln_w", "rw_ln_b", "mb_norm", "g_mix_2", "g_conv_out_2", "g_attn_out_2", "g_mlp_2", "g_ple_2",
              "norm_mix_g_3", "gla_norm_g_3", "sgu_norm_g_3", "norm_mlp_g_3"):
        d[n] = cols(f[n][0])
    for n in ("rw_w2", "rw_a2", "w_in_2", "w_out_2", "w_up_2", "w_down_2", "w_ple_gate_2", "w_ple_proj_2",
              "w_in_3", "w_a2_fwd_3", "w_a2_bwd_3", "w_s_3", "w_out_3", "w_mlp1_3", "w_mlp2_3"):
        d[n] = f[n][0]
    return d



def kernel(**inputs):
    import concourse.bacc as _bacc
    from concourse.bass_utils import run_bass_kernel_spmd as _run

    nc = _bacc.Bacc("TRN2", target_bir_lowering=False, num_devices=1)
    arrays = pack(inputs)
    dram = {n: nc.dram_tensor(n + "_dram", a.shape, mybir.dt.from_np(a.dtype), kind="ExternalInput").ap()
            for n, a in arrays.items()}
    out = nc.dram_tensor("out_dram", (SEQ, D), F32, kind="ExternalOutput").ap()
    program(nc, dram, out)
    r = _run(nc, [{n + "_dram": a for n, a in arrays.items()}], core_ids=[0])
    return r.results[0]["out_dram"].reshape(1, SEQ, D)
```
